# Optimizing a Trainium2 kernel written in Bass

```python
import math
import jax, jax.numpy as jnp
from jax import lax
import numpy as np

D_MODEL = 1024
BATCH = 1
SEQ = 1024
DEPTH = 1

HEAD_DIM = 64
SWA_HEADS = 8
SWA_KV_HEADS = 2
SWA_WINDOW = 128
DSA_HEADS = 8
DSA_KV_RANK = 128
IDX_HEADS = 8
IDX_DIM = 64
IDX_TOPK_MAX = 256
DSA_QBLOCK = 128
REL_BUCKETS = 32
REL_MAX_DIST = 128
N_SELF_HEADS = SWA_HEADS + DSA_HEADS
MEM_LEN = 256
MEM_HEADS = 4
MEM_HEAD_DIM = D_MODEL // MEM_HEADS
D_FF = 4 * D_MODEL
DN_ALPHA = (2.0 * DEPTH) ** 0.25
DN_BETA = (8.0 * DEPTH) ** -0.25
LN_EPS = 1e-5
NEG_INF = -1e30
IN_SPLITS = (SWA_HEADS * HEAD_DIM,
             SWA_KV_HEADS * HEAD_DIM,
             SWA_KV_HEADS * HEAD_DIM,
             DSA_HEADS * HEAD_DIM,
             DSA_KV_RANK,
             IDX_HEADS * IDX_DIM,
             IDX_DIM,
             IDX_HEADS)
D_IN = sum(IN_SPLITS)
MIX_WIDTH = (SWA_HEADS + DSA_HEADS) * HEAD_DIM


def layer_norm(x, g, b):
    xf = x.astype(jnp.float32)
    mu = jnp.mean(xf, axis=-1, keepdims=True)
    var = jnp.mean(jnp.square(xf - mu), axis=-1, keepdims=True)
    return ((xf - mu) * lax.rsqrt(var + LN_EPS) * g.astype(jnp.float32) + b.astype(jnp.float32)).astype(x.dtype)

def rms_norm(x, g):
    xf = x.astype(jnp.float32)
    ms = jnp.mean(jnp.square(xf), axis=-1, keepdims=True)
    return (xf * lax.rsqrt(ms + LN_EPS) * g.astype(jnp.float32)).astype(x.dtype)

def rel_bucket(dist):
    n = jnp.maximum(dist, 0)
    max_exact = REL_BUCKETS // 2
    nf = jnp.maximum(n, 1).astype(jnp.float32)
    large = max_exact + (jnp.log(nf / max_exact) / math.log(REL_MAX_DIST / max_exact)
                         * (REL_BUCKETS - max_exact)).astype(jnp.int32)
    large = jnp.minimum(large, REL_BUCKETS - 1)
    return jnp.where(n < max_exact, n, large)

def swa_sink_attention(q, k, v, sinks, rel_table):
    B, T, Hq, dh = q.shape
    W = SWA_WINDOW
    nb = T // W
    Hkv = SWA_KV_HEADS
    G = Hq // Hkv
    qb = q.reshape(B, nb, W, Hkv, G, dh)

    def band_blocks(z):
        zp = jnp.pad(z, ((0, 0), (W, 0), (0, 0), (0, 0)))
        prev = zp[:, :T].reshape(B, nb, W, Hkv, dh)
        cur = z.reshape(B, nb, W, Hkv, dh)
        return jnp.concatenate([prev, cur], axis=2)

    kb = band_blocks(k)
    vb = band_blocks(v)
    s = jnp.einsum('bnqkgd,bnskd->bnkgqs', qb, kb,
                   preferred_element_type=jnp.float32) * (dh ** -0.5)
    qi = jnp.arange(W)[:, None]
    si = jnp.arange(2 * W)[None, :]
    rel = qi + W - si
    band = (rel >= 0) & (rel < W)
    has_prev = (jnp.arange(nb) > 0)[:, None, None] | (si >= W)[None]
    valid = band[None] & has_prev
    bias = rel_table[rel_bucket(rel)].astype(jnp.float32)
    bias = jnp.transpose(bias, (2, 0, 1)).reshape(Hkv, G, W, 2 * W)
    logits = jnp.where(valid[None, :, None, None, :, :], s + bias, NEG_INF)
    sink = sinks.astype(jnp.float32).reshape(Hkv, G)[:, :, None, None]
    m = jnp.maximum(jnp.max(logits, axis=-1, keepdims=True), sink)
    p = jnp.exp(logits - m)
    denom = jnp.sum(p, axis=-1, keepdims=True) + jnp.exp(sink - m)
    o = jnp.einsum('bnkgqs,bnskd->bnqkgd', (p / denom).astype(v.dtype), vb)
    return o.reshape(B, T, Hq * dh)

def dsa_attention(q, c_kv, iq, ik, iw, w_uk, w_uv, rel_table):
    B, T, H, dh = q.shape
    topk = min(IDX_TOPK_MAX, T // 4)
    QB = DSA_QBLOCK
    nb = T // QB
    q_lat = jnp.einsum('bthd,hcd->bthc', q, w_uk) * (dh ** -0.5)
    key_pos = jnp.arange(T)

    def to_blocks(z):
        return jnp.moveaxis(z.reshape(B, nb, QB, *z.shape[2:]), 1, 0)

    def block(args):
        ql, iqb, iwb, n = args
        t = n * QB + jnp.arange(QB)
        dots = jnp.einsum('bqhd,bsd->bqhs', iqb, ik,
                          preferred_element_type=jnp.float32) * (IDX_DIM ** -0.5)
        score = jnp.einsum('bqh,bqhs->bqs', iwb.astype(jnp.float32), jax.nn.relu(dots))
        causal = key_pos[None, :] <= t[:, None]
        score = jnp.where(causal[None], score, NEG_INF)
        _, idx = lax.top_k(score, topk)
        ok = idx <= t[None, :, None]
        sel = jax.vmap(lambda c, i: c[i])(c_kv, idx)
        logits = jnp.einsum('bqhc,bqkc->bhqk', ql, sel, preferred_element_type=jnp.float32)
        bias = rel_table[rel_bucket(t[None, :, None] - idx)].astype(jnp.float32)
        logits = jnp.where(ok[:, None], logits + jnp.moveaxis(bias, 3, 1), NEG_INF)
        p = jax.nn.softmax(logits, axis=-1).astype(sel.dtype)
        o_lat = jnp.einsum('bhqk,bqkc->bqhc', p, sel)
        return jnp.einsum('bqhc,hcd->bqhd', o_lat, w_uv)

    out = lax.map(block, (to_blocks(q_lat), to_blocks(iq), to_blocks(iw), jnp.arange(nb)))
    return jnp.moveaxis(out, 0, 1).reshape(B, T, H * dh)

def memory_cross_attention(x, mem, wq, bq, wkv, bkv, wo, bo):
    B, T, _ = x.shape
    M = mem.shape[1]
    q = (x @ wq + bq).reshape(B, T, MEM_HEADS, MEM_HEAD_DIM)
    kv = mem @ wkv + bkv
    k, v = jnp.split(kv, 2, axis=-1)
    k = k.reshape(B, M, MEM_HEADS, MEM_HEAD_DIM)
    v = v.reshape(B, M, MEM_HEADS, MEM_HEAD_DIM)
    s = jnp.einsum('bthd,bmhd->bhtm', q, k, preferred_element_type=jnp.float32) * (MEM_HEAD_DIM ** -0.5)
    p = jax.nn.softmax(s, axis=-1).astype(v.dtype)
    o = jnp.einsum('bhtm,bmhd->bthd', p, v).reshape(B, T, D_MODEL)
    return o @ wo + bo

def first_inputs(seed: int = 0) -> dict:
    key = jax.random.key(seed)
    ks = jax.random.split(key, 40)
    f32 = jnp.float32

    def w(k, shape, fan_in, scale=1.0):
        return jax.random.normal(k, shape, f32) * (fan_in ** -0.5) * scale

    def gain(k, shape):
        return 1.0 + 0.05 * jax.random.normal(k, shape, f32)

    def small(k, shape):
        return 0.01 * jax.random.normal(k, shape, f32)

    L = DEPTH
    return {
        "x": jax.random.normal(ks[0], (BATCH, SEQ, D_MODEL), f32),
        "mem": jax.random.normal(ks[1], (BATCH, MEM_LEN, D_MODEL), f32),
        "ln_emb_g": gain(ks[2], (D_MODEL,)),
        "ln_emb_b": small(ks[3], (D_MODEL,)),
        "w_in": w(ks[4], (L, D_MODEL, D_IN), D_MODEL),
        "b_in": small(ks[5], (L, D_IN)),
        "swa_sinks": 0.5 * jax.random.normal(ks[6], (L, SWA_HEADS), f32),
        "dsa_kv_norm_g": gain(ks[7], (L, DSA_KV_RANK)),
        "dsa_w_uk": w(ks[8], (L, DSA_HEADS, DSA_KV_RANK, HEAD_DIM), DSA_KV_RANK),
        "dsa_w_uv": w(ks[9], (L, DSA_HEADS, DSA_KV_RANK, HEAD_DIM), DSA_KV_RANK),
        "idx_k_ln_g": gain(ks[10], (L, IDX_DIM)),
        "idx_k_ln_b": small(ks[11], (L, IDX_DIM)),
        "rel_bias": 0.5 * jax.random.normal(ks[12], (REL_BUCKETS, N_SELF_HEADS), f32),
        "w_o": w(ks[13], (L, MIX_WIDTH, D_MODEL), MIX_WIDTH, DN_BETA),
        "b_o": small(ks[14], (L, D_MODEL)),
        "ln1_g": gain(ks[15], (L, D_MODEL)),
        "ln1_b": small(ks[16], (L, D_MODEL)),
        "xa_wq": w(ks[17], (L, D_MODEL, D_MODEL), D_MODEL),
        "xa_bq": small(ks[18], (L, D_MODEL)),
        "xa_wkv": w(ks[19], (L, D_MODEL, 2 * D_MODEL), D_MODEL),
        "xa_bkv": small(ks[20], (L, 2 * D_MODEL)),
        "xa_wo": w(ks[21], (L, D_MODEL, D_MODEL), D_MODEL, DN_BETA),
        "xa_bo": small(ks[22], (L, D_MODEL)),
        "ln2_g": gain(ks[23], (L, D_MODEL)),
        "ln2_b": small(ks[24], (L, D_MODEL)),
        "w_up": w(ks[25], (L, D_MODEL, D_FF), D_MODEL),
        "b_up": small(ks[26], (L, D_FF)),
        "w_down": w(ks[27], (L, D_FF, D_MODEL), D_FF, DN_BETA),
        "b_down": small(ks[28], (L, D_MODEL)),
        "ln3_g": gain(ks[29], (L, D_MODEL)),
        "ln3_b": small(ks[30], (L, D_MODEL)),
    }

def first_block(x, mem, ln_emb_g, ln_emb_b, w_in, b_in, swa_sinks, dsa_kv_norm_g, dsa_w_uk, dsa_w_uv,
              idx_k_ln_g, idx_k_ln_b, rel_bias, w_o, b_o, ln1_g, ln1_b, xa_wq, xa_bq, xa_wkv, xa_bkv,
              xa_wo, xa_bo, ln2_g, ln2_b, w_up, b_up, w_down, b_down, ln3_g, ln3_b):
    B, T, _ = x.shape
    offsets = [int(o) for o in np.cumsum(IN_SPLITS)[:-1]]
    rel_a = rel_bias[:, :SWA_HEADS]
    rel_b = rel_bias[:, SWA_HEADS:]
    x = layer_norm(x, ln_emb_g, ln_emb_b)
    for l in range(DEPTH):
        h = x @ w_in[l] + b_in[l]
        qa, ka, va, qb, cb, iq, ik, iw = jnp.split(h, offsets, axis=-1)
        qa = qa.reshape(B, T, SWA_HEADS, HEAD_DIM)
        ka = ka.reshape(B, T, SWA_KV_HEADS, HEAD_DIM)
        va = va.reshape(B, T, SWA_KV_HEADS, HEAD_DIM)
        out_a = swa_sink_attention(qa, ka, va, swa_sinks[l], rel_a)
        qb = qb.reshape(B, T, DSA_HEADS, HEAD_DIM)
        cb = rms_norm(cb, dsa_kv_norm_g[l])
        iq = iq.reshape(B, T, IDX_HEADS, IDX_DIM)
        ik = layer_norm(ik, idx_k_ln_g[l], idx_k_ln_b[l])
        iw = iw * (IDX_HEADS ** -0.5)
        out_b = dsa_attention(qb, cb, iq, ik, iw, dsa_w_uk[l], dsa_w_uv[l], rel_b)
        mix = jnp.concatenate([out_a, out_b], axis=-1) @ w_o[l] + b_o[l]
        x = layer_norm(DN_ALPHA * x + mix, ln1_g[l], ln1_b[l])
        ca = memory_cross_attention(x, mem, xa_wq[l], xa_bq[l], xa_wkv[l], xa_bkv[l], xa_wo[l], xa_bo[l])
        x = layer_norm(DN_ALPHA * x + ca, ln2_g[l], ln2_b[l])
        f = jnp.square(jax.nn.relu(x @ w_up[l] + b_up[l])) @ w_down[l] + b_down[l]
        x = layer_norm(DN_ALPHA * x + f, ln3_g[l], ln3_b[l])
    return x


GRID_W = 64
CTX_LEN = 256
N_MIXERS = 2
M_HEADS = 4
M_DV = D_MODEL // M_HEADS
M_DK = M_DV // 2
M_CHUNK = 128
M_PROJ = 2 * M_HEADS * M_DK + 2 * M_HEADS * M_DV + 4 * M_HEADS
F_GROUPS = 8
F_GROUP_DIM = D_MODEL // F_GROUPS
FFN_DIM = 2816
CONV_W = 3
EPS = 1e-6


def rmsnorm(x, g):
    x32 = x.astype(jnp.float32)
    y = x32 * lax.rsqrt(jnp.mean(x32 * x32, axis=-1, keepdims=True) + EPS)
    return (y * g.astype(jnp.float32)).astype(x.dtype)

def modulate(h, shift, scale):
    return h * (1 + scale[..., None, :]) + shift[..., None, :]

def _ctx_stream_needed(layer):
    return any(j % N_MIXERS == 0 for j in range(layer + 1, DEPTH))

def mlstm_project(h, w_in, b_in):
    B, T, _ = h.shape
    hk, hv = M_HEADS * M_DK, M_HEADS * M_DV
    p = h @ w_in + b_in
    q, k, v, o, gates = jnp.split(p, [hk, 2 * hk, 2 * hk + hv, 2 * hk + 2 * hv], axis=-1)

    def heads(t, d):
        return t.reshape(B, T, M_HEADS, d).transpose(0, 2, 1, 3).astype(jnp.float32)

    q = heads(q, M_DK)
    k = heads(k, M_DK) * (M_DK ** -0.5)
    v = heads(v, M_DV)
    g = gates.astype(jnp.float32).reshape(B, T, 4, M_HEADS).transpose(2, 0, 3, 1)
    fwd = (g[0], jax.nn.log_sigmoid(g[1]))
    bwd = (g[2], jax.nn.log_sigmoid(g[3]))
    return q, k, v, o, fwd, bwd

def mlstm_zero_state(B):
    return (jnp.zeros((B, M_HEADS, M_DK, M_DV), jnp.float32),
            jnp.zeros((B, M_HEADS, M_DK), jnp.float32),
            jnp.zeros((B, M_HEADS), jnp.float32))

def mlstm_chunk_scan(q, k, v, logi, logf, state0, with_outputs):
    B, H, T, _ = q.shape
    L = M_CHUNK
    nc = T // L

    def chunks(t):
        return jnp.moveaxis(t.reshape((B, H, nc, L) + t.shape[3:]), 2, 0)

    tri = jnp.tril(jnp.ones((L, L), dtype=bool))

    def step(carry, inp):
        C, n, m = carry
        qc, kc, vc, li, lf = inp
        b = jnp.cumsum(lf, axis=-1)
        bL = b[..., -1]
        g_s = bL[..., None] - b + li
        m_new = jnp.maximum(bL + m, jnp.max(g_s, axis=-1))
        a = jnp.exp(bL + m - m_new)
        ws = jnp.exp(g_s - m_new[..., None])
        C_new = a[..., None, None] * C + jnp.einsum('bhs,bhsd,bhse->bhde', ws, kc, vc)
        n_new = a[..., None] * n + jnp.einsum('bhs,bhsd->bhd', ws, kc)
        if not with_outputs:
            return (C_new, n_new, m_new), None
        dmat = jnp.where(tri, b[..., :, None] - b[..., None, :] + li[..., None, :], -jnp.inf)
        inter = b + m[..., None]
        m_t = jnp.maximum(inter, jnp.max(dmat, axis=-1))
        w_inter = jnp.exp(inter - m_t)
        s = jnp.einsum('bhtd,bhsd->bhts', qc, kc) * jnp.exp(dmat - m_t[..., None])
        num = w_inter[..., None] * jnp.einsum('bhtd,bhde->bhte', qc, C) + jnp.einsum('bhts,bhse->bhte', s, vc)
        den = w_inter * jnp.einsum('bhtd,bhd->bht', qc, n) + jnp.sum(s, axis=-1)
        h = num / jnp.maximum(jnp.abs(den), jnp.exp(-m_t))[..., None]
        return (C_new, n_new, m_new), h

    state, hs = lax.scan(step, state0, (chunks(q), chunks(k), chunks(v), chunks(logi), chunks(logf)))
    if with_outputs:
        hs = jnp.moveaxis(hs, 0, 2).reshape(B, H, T, M_DV)
    return hs, state

def mlstm_direction(q, k, v, gates, state0, reverse, with_outputs):
    logi, logf = gates
    if reverse:
        q, k, v = q[:, :, ::-1], k[:, :, ::-1], v[:, :, ::-1]
        logi, logf = logi[..., ::-1], logf[..., ::-1]
    h, state = mlstm_chunk_scan(q, k, v, logi, logf, state0, with_outputs)
    if reverse and with_outputs:
        h = h[:, :, ::-1]
    return h, state

def mlstm_readout(h, o, norm_g, w_out):
    B, H, T, _ = h.shape
    hn = h * lax.rsqrt(jnp.mean(h * h, axis=-1, keepdims=True) + EPS)
    hn = hn * norm_g.astype(jnp.float32).reshape(H, 1, M_DV)
    hn = hn.transpose(0, 2, 1, 3).reshape(B, T, H * M_DV)
    y = (hn * jax.nn.sigmoid(o.astype(jnp.float32))).astype(o.dtype)
    return y @ w_out

def mlstm_mixer(hx, hc, w_in, b_in, norm_g, w_out, ctx_outputs):
    B = hx.shape[0]
    s0 = mlstm_zero_state(B)
    qc, kc, vc, oc, gfc, gbc = mlstm_project(hc, w_in, b_in)
    hcf, st_f = mlstm_direction(qc, kc, vc, gfc, s0, False, ctx_outputs)
    hcb, st_b = mlstm_direction(qc, kc, vc, gbc, s0, True, ctx_outputs)
    qx, kx, vx, ox, gfx, gbx = mlstm_project(hx, w_in, b_in)
    hxf, _ = mlstm_direction(qx, kx, vx, gfx, st_f, False, True)
    hxb, _ = mlstm_direction(qx, kx, vx, gbx, st_b, True, True)
    yx = mlstm_readout(hxf + hxb, ox, norm_g, w_out)
    yc = mlstm_readout(hcf + hcb, oc, norm_g, w_out) if ctx_outputs else None
    return yx, yc

def fourier_mixer(h, w_out, b_out):
    B, T, D = h.shape
    hg = h.astype(jnp.float32).reshape(B, T, F_GROUPS, F_GROUP_DIM)
    y = jnp.real(jnp.fft.fft2(hg, axes=(1, 3), norm="ortho")).reshape(B, T, D).astype(h.dtype)
    return y @ w_out + b_out

def dwconv3(g, w, b, axis):
    n = g.shape[axis]
    pad = [(0, 0)] * g.ndim
    pad[axis] = (1, 1)
    gp = jnp.pad(g, pad)
    return (lax.slice_in_dim(gp, 0, n, axis=axis) * w[0]
            + lax.slice_in_dim(gp, 1, n + 1, axis=axis) * w[1]
            + lax.slice_in_dim(gp, 2, n + 2, axis=axis) * w[2] + b)

def conv_ffn(h, up_w, conv_w, conv_b, down_w, on_grid):
    u, g = jnp.split(h @ up_w, 2, axis=-1)
    if on_grid:
        B, T, F = g.shape
        rows = T // GRID_W
        g = dwconv3(g.reshape(B, rows, GRID_W, F), conv_w, conv_b, axis=2).reshape(B, T, F)
    else:
        g = dwconv3(g, conv_w, conv_b, axis=1)
    return (jax.nn.silu(g) * u) @ down_w

def second_inputs(seed: int = 0) -> dict:
    key = jax.random.key(seed)
    ks = jax.random.split(key, 24)
    D, F = D_MODEL, FFN_DIM
    NA = (DEPTH + N_MIXERS - 1) // N_MIXERS
    NB = DEPTH // N_MIXERS
    nrm = jax.random.normal
    x = nrm(ks[0], (BATCH, SEQ, D), jnp.float32)
    c = nrm(ks[1], (BATCH, D), jnp.float32)
    ctx = nrm(ks[2], (BATCH, CTX_LEN, D), jnp.float32)
    c_ctx = nrm(ks[3], (D,), jnp.float32)
    ada_w = nrm(ks[4], (DEPTH, D, 6 * D), jnp.float32) * D ** -0.5
    ada_b = 0.02 * nrm(ks[5], (DEPTH, 6 * D), jnp.float32)
    pre_mix_g = 1.0 + 0.05 * nrm(ks[6], (DEPTH, D), jnp.float32)
    post_mix_g = 1.0 + 0.05 * nrm(ks[7], (DEPTH, D), jnp.float32)
    pre_ffn_g = 1.0 + 0.05 * nrm(ks[8], (DEPTH, D), jnp.float32)
    post_ffn_g = 1.0 + 0.05 * nrm(ks[9], (DEPTH, D), jnp.float32)
    ffn_up_w = nrm(ks[10], (DEPTH, D, 2 * F), jnp.float32) * D ** -0.5
    ffn_conv_w = nrm(ks[11], (DEPTH, CONV_W, F), jnp.float32) * CONV_W ** -0.5
    ffn_conv_b = 0.02 * nrm(ks[12], (DEPTH, F), jnp.float32)
    ffn_down_w = nrm(ks[13], (DEPTH, F, D), jnp.float32) * F ** -0.5
    m_in_w = nrm(ks[14], (NA, D, M_PROJ), jnp.float32) * D ** -0.5
    lin_b = 0.02 * nrm(ks[15], (NA, M_PROJ - 4 * M_HEADS), jnp.float32)
    f_base = jnp.linspace(3.0, 6.0, M_HEADS, dtype=jnp.float32)
    gn = 0.1 * nrm(ks[16], (NA, 4, M_HEADS), jnp.float32)
    gate_b = gn + jnp.stack([jnp.zeros_like(f_base), f_base, jnp.zeros_like(f_base), f_base])[None]
    m_in_b = jnp.concatenate([lin_b, gate_b.reshape(NA, 4 * M_HEADS)], axis=-1)
    m_norm_g = 1.0 + 0.05 * nrm(ks[17], (NA, M_HEADS * M_DV), jnp.float32)
    m_out_w = nrm(ks[18], (NA, M_HEADS * M_DV, D), jnp.float32) * (M_HEADS * M_DV) ** -0.5
    f_out_w = nrm(ks[19], (NB, D, D), jnp.float32) * D ** -0.5
    f_out_b = 0.02 * nrm(ks[20], (NB, D), jnp.float32)
    return {"x": x, "c": c, "ctx": ctx, "c_ctx": c_ctx,
            "ada_w": ada_w, "ada_b": ada_b,
            "pre_mix_g": pre_mix_g, "post_mix_g": post_mix_g,
            "pre_ffn_g": pre_ffn_g, "post_ffn_g": post_ffn_g,
            "ffn_up_w": ffn_up_w, "ffn_conv_w": ffn_conv_w, "ffn_conv_b": ffn_conv_b,
            "ffn_down_w": ffn_down_w,
            "m_in_w": m_in_w, "m_in_b": m_in_b, "m_norm_g": m_norm_g, "m_out_w": m_out_w,
            "f_out_w": f_out_w, "f_out_b": f_out_b}

def second_block(x, c, ctx, c_ctx, ada_w, ada_b, pre_mix_g, post_mix_g, pre_ffn_g, post_ffn_g,
              ffn_up_w, ffn_conv_w, ffn_conv_b, ffn_down_w,
              m_in_w, m_in_b, m_norm_g, m_out_w, f_out_w, f_out_b):
    cx = jax.nn.silu(c)
    cc = jax.nn.silu(c_ctx)
    h_ctx = ctx
    for i in range(DEPTH):
        is_mlstm = (i % N_MIXERS) == 0
        j = i // N_MIXERS
        ctx_out = _ctx_stream_needed(i)
        sh1, sc1, g1, sh2, sc2, g2 = jnp.split(cx @ ada_w[i] + ada_b[i], 6, axis=-1)
        if is_mlstm or ctx_out:
            csh1, csc1, cg1, csh2, csc2, cg2 = jnp.split(cc @ ada_w[i] + ada_b[i], 6, axis=-1)
        hx = modulate(rmsnorm(x, pre_mix_g[i]), sh1, sc1)
        if is_mlstm:
            hc = modulate(rmsnorm(h_ctx, pre_mix_g[i]), csh1, csc1)
            yx, yc = mlstm_mixer(hx, hc, m_in_w[j], m_in_b[j], m_norm_g[j], m_out_w[j], ctx_out)
        else:
            yx = fourier_mixer(hx, f_out_w[j], f_out_b[j])
            if ctx_out:
                hc = modulate(rmsnorm(h_ctx, pre_mix_g[i]), csh1, csc1)
                yc = fourier_mixer(hc, f_out_w[j], f_out_b[j])
        x = x + g1[..., None, :] * rmsnorm(yx, post_mix_g[i])
        if ctx_out:
            h_ctx = h_ctx + cg1[..., None, :] * rmsnorm(yc, post_mix_g[i])
        hx = modulate(rmsnorm(x, pre_ffn_g[i]), sh2, sc2)
        yx = conv_ffn(hx, ffn_up_w[i], ffn_conv_w[i], ffn_conv_b[i], ffn_down_w[i], True)
        x = x + g2[..., None, :] * rmsnorm(yx, post_ffn_g[i])
        if ctx_out:
            hc = modulate(rmsnorm(h_ctx, pre_ffn_g[i]), csh2, csc2)
            yc = conv_ffn(hc, ffn_up_w[i], ffn_conv_w[i], ffn_conv_b[i], ffn_down_w[i], False)
            h_ctx = h_ctx + cg2[..., None, :] * rmsnorm(yc, post_ffn_g[i])
    return x


def setup_inputs(seed=0):
    out = dict(first_inputs(seed))
    for name, value in second_inputs(seed + 1).items():
        if name != "x":
            out[name + "_2"] = value
    return out


def reference(
    x, mem, ln_emb_g, ln_emb_b, w_in, b_in, swa_sinks, dsa_kv_norm_g, dsa_w_uk, dsa_w_uv,
    idx_k_ln_g, idx_k_ln_b, rel_bias, w_o, b_o, ln1_g, ln1_b, xa_wq, xa_bq, xa_wkv, xa_bkv,
    xa_wo, xa_bo, ln2_g, ln2_b, w_up, b_up, w_down, b_down, ln3_g, ln3_b, c_2, ctx_2, c_ctx_2,
    ada_w_2, ada_b_2, pre_mix_g_2, post_mix_g_2, pre_ffn_g_2, post_ffn_g_2, ffn_up_w_2,
    ffn_conv_w_2, ffn_conv_b_2, ffn_down_w_2, m_in_w_2, m_in_b_2, m_norm_g_2, m_out_w_2,
    f_out_w_2, f_out_b_2,
):
    x = first_block(
        x, mem, ln_emb_g, ln_emb_b, w_in, b_in, swa_sinks, dsa_kv_norm_g, dsa_w_uk, dsa_w_uv,
        idx_k_ln_g, idx_k_ln_b, rel_bias, w_o, b_o, ln1_g, ln1_b, xa_wq, xa_bq, xa_wkv, xa_bkv,
        xa_wo, xa_bo, ln2_g, ln2_b, w_up, b_up, w_down, b_down, ln3_g, ln3_b,
    )
    return second_block(
        x, c_2, ctx_2, c_ctx_2, ada_w_2, ada_b_2, pre_mix_g_2, post_mix_g_2, pre_ffn_g_2,
        post_ffn_g_2, ffn_up_w_2, ffn_conv_w_2, ffn_conv_b_2, ffn_down_w_2, m_in_w_2, m_in_b_2,
        m_norm_g_2, m_out_w_2, f_out_w_2, f_out_b_2,
    )


_drawn_inputs = setup_inputs


def setup_inputs(seed=0):
    import zlib

    import numpy as np

    out = dict(_drawn_inputs(seed))
    spreads = {}
    factors = {'b_in': 4.199,
     'swa_sinks': 22.079,
     'dsa_kv_norm_g': 6.282,
     'idx_k_ln_g': 5.163,
     'idx_k_ln_b': 8.0,
     'b_o': 2.748,
     'xa_bq': 52.223,
     'xa_bkv': 4.273,
     'xa_bo': 2.711,
     'b_up': 3.939,
     'b_down': 2.961,
     'ffn_conv_b_2': 7.803}
    for name, (base, spread) in spreads.items():
        noise = np.random.default_rng([zlib.crc32(name.encode()), seed]).standard_normal(out[name].shape)
        drawn = base * np.exp(spread * noise) if base else spread * noise
        out[name] = __import__('jax').numpy.asarray(drawn.astype(out[name].dtype))
    for name, factor in factors.items():
        out[name] = (out[name] * factor).astype(out[name].dtype)
    return out
```

```python
from contextlib import ExitStack

import numpy as np

import concourse.bass as bass
from concourse import mybir

F32 = mybir.dt.float32
ALU = mybir.AluOpType
ACT = mybir.ActivationFunctionType
AX = mybir.AxisListType

P = 128
D = 1024
T = 1024
NT = T // P
KC = D // P
MEM = 256
DH = 64
NH = 8
RANK = 128
TOPK = 256
XH, XD = 4, 256
FF = 4096
FF2 = 2816
GRID = 64
MH, DK, DV = 4, 128, 256
NB = 32
MAXD = 128
NEG = -1.0e30
TAKEN = -3.0e38
ALPHA = 2.0 ** 0.25
LN_EPS, RMS_EPS = 1e-5, 1e-6
BW = 512
N_BIAS = 3 * P
MISC = 2 * P + DH + NH

COLS = {}
_at = 0
for _name, _n in (("qa", 4), ("qb", 4), ("iq", 4), ("ka", 1), ("xq", 8), ("xk", 8), ("mq", 4),
                  ("pre_mix", 8), ("pre_ffn", 8), ("sh1", 8), ("sc1", 8), ("sh2", 8), ("sc2", 8),
                  ("c", 16)):
    COLS[_name] = (_at, _at + _n)
    _at += _n
N_COLS = _at


def bases(*stages):
    at, out = 0, {}
    for name, n in stages:
        out[name] = at
        at += n
    out["end"] = at
    return out


FT = bases(("xt0", 16), ("qa", 8), ("qb", 8), ("iq", 8), ("ka", 2), ("vb", 2), ("ukT", 1),
           ("ckT", 4), ("ada", 12), ("memT", 4), ("xk", 8), ("xt1", 16), ("xq", 16), ("xt2", 16),
           ("up", 64), ("ctxT", 4), ("cg", 2), ("xtm", 16), ("mg", 4), ("mq", 8), ("kT", 8),
           ("yT", 16), ("xtf", 16), ("up2", 88))
TT = bases(("misc", 8), ("wo", 16), ("xv", 4), ("xo", 16), ("down", 64), ("ck", 2), ("cv", 4),
           ("mk", 8), ("mv", 16), ("mo", 16), ("mout", 16), ("down2", 96))


def build_program(nc, I, out):
    with ExitStack() as ctx:
        def sb(name, shape, dt=F32):
            return ctx.enter_context(nc.sbuf_tensor(name, shape, dt))

        def sem(name):
            return ctx.enter_context(nc.semaphore(name))

        mods_d = nc.dram_tensor("mods_scratch", (2, 6 * D), F32, kind="Internal").ap()
        bias_d = nc.dram_tensor("bias_scratch", (2 * NH, P, N_BIAS), F32, kind="Internal").ap()
        x_d = nc.dram_tensor("x_scratch", (P, NT * D), F32, kind="Internal").ap()

        XR = sb("x_rows", [P, NT, D])
        XT = sb("x_cols", [P, KC, T])
        WB = [sb(f"weights{i}", [P, KC, BW]) for i in range(2)]
        Q = sb("wide", [P, 8, T])
        ROW = sb("rows", [P, 3, D])
        R = sb("region", [P, 15936])
        ident = sb("ident", [P, P])
        cols = sb("cols", [P, N_COLS])
        modc = sb("modc", [P, 6, KC])
        st = sb("stats", [P, 32, 6])
        mv = sb("mean_var", [P, 32, 2])
        ve = sb("var_eps", [P, 32])
        sdv = sb("std", [P, 32])
        rs = sb("rstd", [P, 32])
        PS = ctx.enter_context(nc.psum_tensor("psum", [P, 8, BW], F32))
        PSf = PS[:, :, :].rearrange("p a b -> p (a b)")

        def view(base, at, shape):
            n = int(np.prod(shape))
            v = base[:, at:at + n]
            if len(shape) == 1:
                return v
            if len(shape) == 2:
                return v.rearrange("p (a b) -> p a b", a=shape[0])
            return v.rearrange("p (a b c) -> p a b c", a=shape[0], b=shape[1])

        def over_last(v, n):
            return v.unsqueeze(2).to_broadcast([v.shape[0], v.shape[1], n])

        def over_mid(v, n):
            return v.unsqueeze(1).to_broadcast([v.shape[0], n, v.shape[1]])

        XTf = XT[:, :, :].rearrange("p a b -> p (a b)")
        XRf = XR[:, :, :].rearrange("p a b -> p (a b)")
        Qf = Q[:, :, :].rearrange("p a b -> p (a b)")
        ROWf = ROW[:, :, :].rearrange("p a b -> p (a b)")
        stf = st[:, :, :].rearrange("p a b -> p (a b)")

        iqT = view(R, 0, (4, T))
        kaT = view(R, 4096, (2, T))
        ikT = view(R, 6144, (T,))
        cT = view(R, 7168, (T,))
        cR = view(R, 8192, (NT, RANK))
        misc = view(R, 9216, (NT, MISC))
        SB = view(R, 11840, (NH, 2 * P))
        LG = view(R, 11840, (2, T))
        PT = view(R, 13888, (16, P))
        RL = view(R, 13888, (2, T))
        bias = view(XTf, 0, (16, 2 * P))
        msk = view(XTf, 4096, (T,))
        score = view(XTf, 5120, (T,))
        OL = view(XTf, 5120, (NH, P))
        work = view(XTf, 6144, (T,))
        QL = view(XTf, 7168, (NH, P))
        wuk = view(ROWf, 0, (NH, DH))
        wukT = view(ROWf, 512, (4, P))
        wuv = view(ROWf, 1024, (NH, DH))
        mrow = view(ROWf, 1536, (MISC,))
        kvg = view(ROWf, 1864, (RANK,))
        ikg = view(ROWf, 1992, (2, DH))
        far = view(ROWf, 2120, (NH,))
        sink = view(ROWf, 2128, (NH,))
        mx = view(ROWf, 2136, (NH,))
        nm = view(ROWf, 2144, (NH,))
        den = view(ROWf, 2152, (NH,))
        sd = view(ROWf, 2160, (NH,))
        es = view(ROWf, 2168, (NH,))
        top = view(ROWf, 2176, (8,))
        iwt = view(ROWf, 2184, (NT, NH))
        hot = view(ROWf, 2248, (2, N_BIAS))
        modr = view(R, 13888, (4, BW))
        cx = sb("cond", [P, KC, 2])
        relb = view(R, 11840, (2 * NH,))
        vb = view(R, 11904, (2, N_BIAS))
        ikn = view(R, 12700, (NT, 2 * DH))
        kaS = view(R, 14000, (2, BW))

        memR = view(R, 0, (2, D))
        memT = view(R, 2048, (KC, MEM))
        xkT = view(R, 4096, (KC, MEM))
        xv = view(R, 6144, (2, D))
        XP = view(R, 8192, (2, XH * MEM))
        XPT = view(R, 10240, (2, 8 * P))
        RU = view(R, 12288, (2, BW))
        vrow = view(R, 13312, (D,))
        upb = view(R, 14336, (2, 4))
        xm = view(R, 14344, (2, XH))
        xn = view(R, 14352, (2, XH))
        xd = view(R, 14360, (2, XH))

        NC = NT
        V1 = DV + 1
        GR = 36
        ctxR = view(R, 0, (2, D))
        hcT = view(R, 2048, (KC, MEM))
        KX = view(R, 4096, (2, MH * DK))
        VX = view(R, 5120, (2, MH, V1))
        GW = view(R, 7232, (KC, 2, GR))
        VV = view(R, 0, (NC, MH, V1))
        KK = view(R, 8224, (NC, MH * DK))
        CC = view(R, 12320, (2 * MH, V1))
        COL = view(R, 14376, (NC, 3, GR))
        MPB = view(R, 15240, (2 * MH, NC))
        MASK = view(R, 15304, (2, P))
        gb = view(R, 15560, (2,))
        ms = view(R, 15562, (1,))
        mpc = view(R, 15563, (NC,))
        dn = view(R, 15571, (2, MH))
        li, lf, bb, uu, tmp, enm, wsr = [view(Qf, i * T, (T,)) for i in range(7)]
        ones = view(Qf, 7 * T, (P,))
        krow = view(Qf, 7 * T + BW, (BW,))
        MM = ROW[:, 0, :]
        SEL = view(ROWf, T, (2 * MH, P))
        KS = view(ROWf, 2 * T, (2, BW))
        WB0f = WB[0][:, :, :].rearrange("p a b -> p (a b)")
        DD = view(WB0f, 0, (2, BW))
        PP = view(WB0f, 1024, (2, BW))
        WI = view(WB0f, 2048, (2, BW))
        QS = view(WB0f, 3072, (2, BW))
        qT = view(XRf, 0, (MH, T))
        kT = view(XRf, 4 * T, (MH, T))
        OG = view(ROWf, T, (2, BW))

        XN = view(R, 0, (NT, D))
        HH = view(R, 0, (4, T))
        UU = view(R, 8192, (2, T))
        GG = view(R, 10240, (2, T))
        TC = view(R, 12288, (2, T))
        cw = view(R, 14336, (2, 8))

        S = {}

        def s(name):
            if name not in S:
                S[name] = sem(name)
            return S[name]

        f_ready, f_free, t_ready, t_free = s("f_ready"), s("f_free"), s("t_ready"), s("t_free")
        w_in = [s("w_in0"), s("w_in1")]
        rows_in, x_in, cols_in, own_dve, own_act = s("rows_in"), s("x_in"), s("cols_in"), s("own_dve"), s("own_act")

        def cols_of(w, a, b):
            return w[:, a:b].rearrange("(k p) n -> p k n", p=P)

        w_in_w = I["w_in"][0]
        blocks = []

        def block_of(pieces, done_sem, done_at):
            blocks.append((pieces, done_sem, done_at))

        for name, a in (("qa", 0), ("qb", 768), ("iq", 1408)):
            block_of([(0, BW, cols_of(w_in_w, a, a + BW))], f_ready, FT[name] + 8)
        block_of([(0, 256, cols_of(w_in_w, 512, 768)), (256, 384, cols_of(w_in_w, 1280, 1408)),
                  (384, 456, cols_of(w_in_w, 1920, 1992))], t_ready, TT["misc"] + 8)
        ADA0 = len(blocks)
        for j in range(12):
            block_of([(0, BW, cols_of(I["ada_w_2"][0], BW * j, BW * j + BW))], f_ready, FT["ada"] + j + 1)
        WO0 = len(blocks)
        for j in range(2):
            block_of([(0, BW, cols_of(I["w_o"][0], BW * j, BW * j + BW))], t_ready, TT["wo"] + 8 * j + 8)

        for name, w, a0, n, ds_, tiles in (("xk", "xa_wkv", 0, 2, f_ready, 4), ("xv", "xa_wkv", D, 2, t_ready, 2),
                                           ("xq", "xa_wq", 0, 2, f_ready, 8), ("xo", "xa_wo", 0, 2, t_ready, 8)):
            for j in range(n):
                block_of([(0, BW, cols_of(I[w][0], a0 + BW * j, a0 + BW * j + BW))], ds_,
                         (FT if ds_ is f_ready else TT)[name] + tiles * (j + 1))
        UP0 = len(blocks)
        N_UP = FF // D
        for g in range(N_UP):
            for j in range(2):
                block_of([None, None], f_ready, FT["up"] + 16 * g + 8 * j + 8)
            for j in range(2):
                block_of([None], t_ready, TT["down"] + 16 * g + 8 * j + 8)
        assert UP0 % 2 == 0
        M0 = len(blocks)
        m_w = I["m_in_w_2"][0]
        for name, a0, n, ds_, tiles in (("ck", 512, 1, t_ready, 2), ("cv", 1024, 2, t_ready, 2), ("mq", 0, 1, f_ready, 8),
                                        ("mk", 512, 1, t_ready, 8), ("mv", 1024, 2, t_ready, 8), ("mo", 2048, 2, t_ready, 8)):
            for j in range(n):
                block_of([(0, BW, cols_of(m_w, a0 + BW * j, a0 + BW * j + BW))], ds_,
                         (FT if ds_ is f_ready else TT)[name] + tiles * (j + 1))
        for j in range(2):
            block_of([(0, BW, cols_of(I["m_out_w_2"][0], BW * j, BW * j + BW))], t_ready, TT["mout"] + 8 * j + 8)
        G0 = len(blocks)
        assert G0 % 2 == 1
        N_G = FF2 // BW
        for g in range(N_G):
            block_of([None] * 3, f_ready, 0)
            block_of([None] * 3, f_ready, 0)
            block_of([None], t_ready, 0)
            block_of([None], t_ready, 0)
        for n in (3, 1, 1):
            block_of([None] * n, f_ready, 0)

        def loaded(b):
            return 16 * sum(len(p) for i, (p, _, _) in enumerate(blocks[:b + 1]) if i % 2 == b % 2)

        CTX_STEPS = [(c if d == 0 else 1 - c, d) for c in range(2) for d in range(2)]
        X_STEPS = [(c if d == 0 else NC - 1 - c, d) for c in range(NC) for d in range(2)]

        block = ctx.enter_context(nc.Block())

        @block.sync
        def _(sp):
            for h in range(2):
                sp.dma_start(XR[:, 4 * h:4 * h + 4, :],
                             I["x"][0, 512 * h:512 * h + 512, :].rearrange("(t p) d -> p t d", p=P)).then_inc(x_in, 16)

            def load(b):
                if b >= 2:
                    sp.wait_ge(blocks[b - 2][1], blocks[b - 2][2])
                for a, z, src in blocks[b][0]:
                    sp.dma_start(WB[b % 2][:, :, a:z], src).then_inc(w_in[b % 2], 16)

            for b in range(WO0):
                load(b)
            for j in range(4):
                sp.wait_ge(s(f"mods_out{j}"), 48)
            for i, (row, part) in enumerate(((0, 0), (0, 1), (0, 3), (0, 4), (1, 0), (1, 1))):
                sp.dma_start(modc[:, i, :], mods_d[row, D * part:D * part + D].rearrange("(k p) -> p k", p=P),
                             allow_slow_non_contiguous=True).then_inc(s("modc_in"), 16)
            for b in range(WO0, WO0 + 2):
                load(b)
            sp.wait_ge(s("d_fe"), NT)
            sp.dma_start(memR, I["mem"][0].rearrange("(t p) d -> p t d", p=P)).then_inc(s("mem_in"), 16)
            sp.dma_start(vrow, I["xa_bkv"][0, D:2 * D].partition_broadcast(P)).then_inc(s("mem_in"), 16)
            for b in range(WO0 + 2, UP0):
                load(b)
            with sp.Fori(0, N_UP) as g:
                for j in range(2):
                    sp.wait_ge(t_ready, g * 16 + (TT["down"] - 8 + 8 * j))
                    sp.dma_start(WB[j][:, :, :], I["w_up"][0][:, bass.ds(g * D + BW * j, BW)]
                                 .rearrange("(k p) n -> p k n", p=P)).then_inc(w_in[j], 16)
                    sp.dma_start(upb[:, j, :], I["bup_h"][bass.ds(g * 2 + j, 1)]
                                 .rearrange("a p c -> p (a c)")).then_inc(w_in[j], 16)
                for j in range(2):
                    sp.wait_ge(f_ready, g * 16 + (FT["up"] + 8 + 8 * j))
                    sp.dma_start(WB[j][:, :, :], I["w_down"][0][bass.ds(g * D, D), BW * j:BW * j + BW]
                                 .rearrange("(k p) n -> p k n", p=P)).then_inc(w_in[j], 16)
            sp.wait_ge(s("ln_done"), 4 * NT)
            for h in range(2):
                sp.dma_start(x_d[:, 4 * D * h:4 * D * h + 4 * D], XRf[:, 4 * D * h:4 * D * h + 4 * D]).then_inc(s("x_out"), 16)
            sp.dma_start(ctxR, I["ctx_2"][0].rearrange("(t p) d -> p t d", p=P)).then_inc(s("ctx_in"), 16)
            sp.wait_ge(s("gw_zero"), 2)
            for gi in range(2):
                for d in range(2):
                    a = 3072 + 8 * d + 4 * gi
                    sp.dma_start(GW[:, :, gi, 32 * d:32 * d + 4], cols_of(m_w, a, a + 4)).then_inc(s("gw_in"), 16)
                    sp.dma_start(gb[32 * d:32 * d + 4, gi:gi + 1], I["m_in_b_2"][0, a:a + 4].rearrange("(p c) -> p c", c=1)).then_inc(s("gw_in"), 16)
            for b in range(M0, M0 + 4):
                load(b)
            sp.wait_ge(s("m_cu"), 8)
            for b in range(M0 + 4, M0 + 8):
                load(b)
            sp.wait_ge(s("m_cu"), 40)
            sp.wait_ge(s("m_h"), 16)
            load(M0 + 8)
            for h in range(2):
                sp.dma_start(XRf[:, 4 * D * h:4 * D * h + 4 * D], x_d[:, 4 * D * h:4 * D * h + 4 * D]).then_inc(s("x_back"), 16)
            load(M0 + 9)
            load(M0 + 10)
            w_u, w_d = I["ffn_up_w_2"][0], I["ffn_down_w_2"][0]

            def load_up(buf, g, j):
                for half in range(2):
                    sp.dma_start(WB[buf][:, :, 256 * half:256 * half + 256],
                                 w_u[:, bass.ds(g * BW + (256 * j + FF2 * half), 256)].rearrange("(k p) n -> p k n", p=P)).then_inc(w_in[buf], 16)
                sp.dma_start(cw[:, j, :], I["conv_h"][bass.ds(g * 2 + j, 1)].rearrange("a p c -> p (a c)")).then_inc(w_in[buf], 16)

            with sp.Fori(0, N_G) as g:
                for j in range(2):
                    sp.wait_ge(t_ready, g * 16 + (TT["down2"] - 8 + 8 * j))
                    load_up(1 - j, g, j)
                for j in range(2):
                    sp.wait_ge(f_ready, g * 16 + (FT["up2"] + 8 + 8 * j))
                    sp.dma_start(WB[1 - j][:, 0:4, :], w_d[bass.ds(g * BW, BW), BW * j:BW * j + BW]
                                 .rearrange("(k p) n -> p k n", p=P)).then_inc(w_in[1 - j], 16)
            sp.wait_ge(t_ready, TT["down2"] + 16 * N_G - 8)
            load_up(1, N_G, 0)
            for j in range(2):
                if j == 0:
                    sp.wait_ge(t_ready, TT["down2"] + 16 * N_G)
                else:
                    sp.wait_ge(f_ready, FT["up2"] + 16 * N_G + 8)
                sp.dma_start(WB[j][:, 0:2, :], w_d[N_G * BW:FF2, BW * j:BW * j + BW]
                             .rearrange("(k p) n -> p k n", p=P)).then_inc(w_in[j], 16)
            for t in range(NT):
                sp.wait_ge(s("x_new"), NT + t + 1)
                sp.dma_start(out[0, t * P:t * P + P, :], XR[:, t, :]).then_inc(s("out_done"), 16)
            sp.wait_ge(s("out_done"), 16 * NT)

        @block.tensor
        def _(pe):
            def bank(n):
                if n >= 4:
                    pe.wait_ge(f_free, n - 3)
                return PS[:, n % 4, :]

            def bank_t(n):
                if n >= 4:
                    pe.wait_ge(t_free, n - 3)
                return PS[:, 4 + n % 4, :]

            def transposes(name, src, ready, ready_at):
                for h in range(2):
                    pe.wait_ge(ready, ready_at(h))
                    for k in range(KC):
                        n = FT[name] + 8 * h + k
                        o = bank(n)
                        for j in range(4):
                            m = pe.transpose(o[:, j * P:j * P + P], src[:, 4 * h + j, k * P:k * P + P], ident[:, :])
                        m.then_inc(f_ready, 1)

            def gemm_f(name, n0, w, chunks, x=XT, halves=2, width=BW):
                n = n0
                for f in chunks:
                    for h in range(halves):
                        o = bank(n)
                        for k in range(KC):
                            m = pe.matmul(o[:, 0:width], lhsT=w[:, k, f * P:f * P + P], rhs=x[:, k, h * width:h * width + width],
                                          start=(k == 0), stop=(k == KC - 1))
                        m.then_inc(f_ready, 1)
                        n += 1

            def gemm_t(n0, w, x=XT, tiles=NT, a=0, z=BW, kc=KC):
                for t in range(tiles):
                    o = bank_t(n0 + t)
                    for k in range(kc):
                        m = pe.matmul(o[:, 0:z - a], lhsT=x[:, k, t * P:t * P + P], rhs=w[:, k, a:z],
                                      start=(k == 0), stop=(k == kc - 1))
                    m.then_inc(t_ready, 1)

            def weights(b):
                pe.wait_ge(w_in[b % 2], loaded(b))
                return WB[b % 2]

            pe.wait_ge(s("ident_ok"), 1)
            transposes("xt0", XR, s("ln_done"), lambda h: 4 * h + 4)
            pe.wait_ge(f_free, FT["qa"])
            for b, name in enumerate(("qa", "qb", "iq")):
                gemm_f(name, FT[name], weights(b), range(4))
            gemm_f("ka", FT["ka"], weights(3), range(1))
            gemm_t(TT["misc"], weights(3), a=P, z=P + MISC)
            pe.wait_ge(s("relb_in"), 48)
            for g in range(2):
                o = bank(FT["vb"] + g)
                pe.matmul(o[0:NH, 0:N_BIAS], lhsT=relb[0:NB + 1, g * NH:g * NH + NH], rhs=hot[0:NB + 1, g, :],
                          start=True, stop=True).then_inc(f_ready, 1)
            o = bank(FT["ukT"])
            for c in range(4):
                m = pe.transpose(o[:, c * P:c * P + P], wuk[:, 2 * c:2 * c + 2, :].rearrange("p a b -> p (a b)"), ident[:, :])
            m.then_inc(f_ready, 1)
            pe.wait_ge(s("ck_ready"), 2)
            for i, src in ((0, cR), (2, ikn)):
                for h in range(2):
                    o = bank(FT["ckT"] + i + h)
                    for j in range(4):
                        m = pe.transpose(o[:, j * P:j * P + P], src[:, 4 * h + j, :], ident[:, :])
                    m.then_inc(f_ready, 1)
            pe.wait_ge(s("cx_ready"), 1)
            for j in range(12):
                w = weights(ADA0 + j)
                o = bank(FT["ada"] + j)
                for k in range(KC):
                    m = pe.matmul(o[0:2, :], lhsT=cx[:, k, :], rhs=w[:, k, :], start=(k == 0), stop=(k == KC - 1))
                m.then_inc(f_ready, 1)

            pe.wait_ge(f_free, FT["memT"])
            pe.wait_ge(t_free, TT["wo"])
            pe.wait_ge(s("attn_in"), 16 * 7)
            for n in range(NT):
                lo = 0 if n == 0 else n - 1
                q = slice(n * P, n * P + P)
                keys = slice(lo * P, n * P + P)
                width = (n + 1 - lo) * P
                if n > 0:
                    pe.wait_ge(s("d_fe"), n)
                for c in range(4):
                    for r in range(2):
                        hp = slice(DH * r, DH * r + DH)
                        m = pe.matmul(PS[:, 2 * r + c // 2, (c % 2) * 256 + 256 - width:(c % 2) * 256 + 256], lhsT=Q[hp, c, q],
                                      rhs=kaT[hp, c // 2, keys], start=True, stop=True)
                        if c % 2 == 1:
                            m.then_inc(s("a_s"), 1)
                pe.wait_ge(s("a_r"), n + 1)
                for b in range(4):
                    pe.wait_ge(s("a_sb"), 4 * n + 4)
                    for j in range(4):
                        h, kt = (4 * b + j) // 2, (4 * b + j) % 2
                        if n == 0 and kt == 0:
                            continue
                        m = pe.transpose(PS[:, b, j * P:j * P + P], SB[:, h, kt * P:kt * P + P], ident[:, :])
                    m.then_inc(s("a_t"), 1)
                pe.wait_ge(s("a_te"), 4 * n + 4)
                for h in range(NH):
                    kts = (1,) if n == 0 else (0, 1)
                    for kt in kts:
                        m = pe.matmul(PS[DH * (h % 2):DH * (h % 2) + DH, 4, (h // 2) * P:(h // 2) * P + P],
                                      lhsT=misc[:, lo + kt - (n == 0), DH * (h // 4):DH * (h // 4) + DH],
                                      rhs=PT[:, 2 * h + kt, :], start=(kt == kts[0]), stop=(kt == 1))
                m.then_inc(s("a_o"), 1)
                L = (n + 1) * P
                if n >= 2:
                    pe.wait_ge(s("a_oe"), n + 1)
                    for h in range(NH):
                        i = NH * (n - 2) + h
                        if h >= 4:
                            pe.wait_ge(s("ix_r"), i - 3)
                        hp = slice(DH * (h % 2), DH * (h % 2) + DH)
                        for a in range(0, L, BW):
                            z = min(L, a + BW)
                            m = pe.matmul(PS[:, 2 * (h % 4) + a // BW, 0:z - a], lhsT=iqT[hp, h // 2, q], rhs=ikT[hp, a:z],
                                          start=True, stop=True)
                        m.then_inc(s("ix_d"), 1)
                    pe.wait_ge(s("ix_r"), NH * (n - 1))
                for h in range(NH):
                    hp = slice(DH * (h % 2), DH * (h % 2) + DH)
                    m = pe.matmul(PS[:, h % 2, (h // 2) * P:(h // 2) * P + P], lhsT=wukT[hp, h // 2, :], rhs=Q[hp, 4 + h // 2, q],
                                  start=True, stop=True)
                    if h >= NH - 2:
                        m.then_inc(s("d_q"), 1)
                pe.wait_ge(s("d_qe"), 2 * n + 2)
                pe.wait_ge(s("a_oe"), n + 1)
                for i in range(NH + 2):
                    if i < NH:
                        if i >= 2:
                            pe.wait_ge(s("d_lb"), NH * n + i - 1)
                        for a in range(0, L, BW):
                            z = min(L, a + BW)
                            m = pe.matmul(PS[:, 4 + 2 * (i % 2) + a // BW, 0:z - a], lhsT=QL[:, i, :], rhs=cT[:, a:z],
                                          start=True, stop=True)
                        m.then_inc(s("d_l"), 1)
                    if 1 <= i <= NH:
                        h = i - 1
                        pe.wait_ge(s("d_n"), NH * n + h + 1)
                        if h >= 2:
                            pe.wait_ge(s("d_oe"), NH * n + h - 1)
                        for kt in range(n + 1):
                            m = pe.transpose(PS[:, 2 * (h % 2) + kt // 4, (kt % 4) * P:(kt % 4) * P + P],
                                             LG[:, h % 2, kt * P:kt * P + P], ident[:, :])
                        m.then_inc(s("d_t"), 1)
                    if i >= 2:
                        h = i - 2
                        pe.wait_ge(s("d_te"), NH * n + h + 1)
                        for kt in range(n + 1):
                            m = pe.matmul(PS[:, 2 * (h % 2), 0:P], lhsT=cR[:, kt, :], rhs=PT[:, 8 * (h % 2) + kt, :],
                                          start=(kt == 0), stop=(kt == n))
                        m.then_inc(s("d_o"), 1)
                pe.wait_ge(s("d_oe"), NH * n + NH)
                for h in range(NH):
                    m = pe.matmul(PS[DH * (h % 2):DH * (h % 2) + DH, 0, (h // 2) * P:(h // 2) * P + P],
                                  lhsT=wuv[:, h, :], rhs=OL[:, h, :], start=True, stop=True)
                m.then_inc(s("d_f"), 1)
            pe.wait_ge(s("d_fe"), NT)
            for j in range(2):
                gemm_t(TT["wo"] + 8 * j, weights(WO0 + j), x=Q)
            pe.wait_ge(s("mem_in"), 32)
            for k in range(0, KC, 2):
                o = bank(FT["memT"] + k // 2)
                for i in range(2):
                    for t in range(2):
                        m = pe.transpose(o[:, (2 * i + t) * P:(2 * i + t) * P + P], memR[:, t, (k + i) * P:(k + i) * P + P], ident[:, :])
                m.then_inc(f_ready, 1)
            pe.wait_ge(f_free, FT["xk"])
            for j in range(2):
                gemm_f("xk", FT["xk"] + 4 * j, weights(WO0 + 2 + j), range(4), x=memT, halves=1, width=MEM)
            for j in range(2):
                gemm_t(TT["xv"] + 2 * j, weights(WO0 + 4 + j), x=memT, tiles=2)
            transposes("xt1", XR, s("ln_done"), lambda h: NT + 4 * h + 4)
            pe.wait_ge(f_free, FT["xq"])
            for j in range(2):
                gemm_f("xq", FT["xq"] + 8 * j, weights(WO0 + 6 + j), range(4))
            pe.wait_ge(f_free, FT["xq"] + 16)
            pe.wait_ge(t_free, TT["xo"])
            for i in range(NT + 1):
                if i < NT:
                    if i >= 2:
                        pe.wait_ge(s("x_p"), i - 1)
                    for h in range(XH):
                        for kk in range(2):
                            m = pe.matmul(PS[:, 2 * (i % 2) + h // 2, (h % 2) * MEM:(h % 2) * MEM + MEM],
                                          lhsT=Q[:, 2 * h + kk, i * P:i * P + P], rhs=xkT[:, 2 * h + kk, :],
                                          start=(kk == 0), stop=(kk == 1))
                    m.then_inc(s("x_s"), 1)
                if i >= 1:
                    t, b0 = i - 1, 4 + 2 * ((i - 1) % 2)
                    pe.wait_ge(s("x_n"), t + 1)
                    if t >= 2:
                        pe.wait_ge(s("x_oe"), t - 1)
                    for j in range(8):
                        m = pe.transpose(PS[:, b0 + j // 4, (j % 4) * P:(j % 4) * P + P], XP[:, t % 2, j * P:j * P + P], ident[:, :])
                    m.then_inc(s("x_t"), 1)
                    pe.wait_ge(s("x_te"), t + 1)
                    for h in range(XH):
                        for dd in range(2):
                            for mt in range(2):
                                m = pe.matmul(PS[:, b0 + h // 2, ((h % 2) * 2 + dd) * P:((h % 2) * 2 + dd) * P + P],
                                              lhsT=xv[:, mt, (2 * h + dd) * P:(2 * h + dd) * P + P],
                                              rhs=XPT[:, t % 2, (2 * h + mt) * P:(2 * h + mt) * P + P],
                                              start=(mt == 0), stop=(mt == 1))
                    m.then_inc(s("x_o"), 1)
            pe.wait_ge(s("x_oe"), NT)
            for j in range(2):
                gemm_t(TT["xo"] + 8 * j, weights(WO0 + 8 + j), x=Q)
            transposes("xt2", XR, s("ln_done"), lambda h: 2 * NT + 4 * h + 4)
            pe.wait_ge(f_free, FT["up"])
            with pe.Fori(0, N_UP) as g:
                for j in range(2):
                    pe.wait_ge(w_in[j], g * 48 + (loaded(UP0 + j)))
                    for f in range(4):
                        for h in range(2):
                            n = FT["up"] + 8 * j + 2 * f + h
                            pe.wait_ge(f_free, g * 16 + (n - 3))
                            for k in range(KC):
                                m = pe.matmul(PS[:, n % 4, :], lhsT=WB[j][:, k, f * P:f * P + P], rhs=XT[:, k, h * BW:h * BW + BW],
                                              start=(k == 0), stop=(k == KC - 1))
                            m.then_inc(f_ready, 1)
                pe.wait_ge(s("squared"), g * 16 + 18)
                for j in range(2):
                    pe.wait_ge(w_in[j], g * 48 + (loaded(UP0 + 2 + j)))
                    for t in range(NT):
                        n = TT["down"] + 8 * j + t
                        pe.wait_ge(t_free, g * 16 + (n - 3))
                        for k in range(KC):
                            m = pe.matmul(PS[:, 4 + n % 4, :], lhsT=Q[:, k, t * P:t * P + P], rhs=WB[j][:, k, :],
                                          start=(k == 0), stop=(k == KC - 1))
                        m.then_inc(t_ready, 1)

            pe.wait_ge(s("ctx_rows"), 1)
            for k in range(0, KC, 2):
                o = bank(FT["ctxT"] + k // 2)
                for i in range(2):
                    for t in range(2):
                        m = pe.transpose(o[:, (2 * i + t) * P:(2 * i + t) * P + P], ctxR[:, t, (k + i) * P:(k + i) * P + P], ident[:, :])
                m.then_inc(f_ready, 1)
            pe.wait_ge(f_free, FT["cg"])
            pe.wait_ge(s("gw_in"), 128)

            def gates(name, x, halves, width):
                n = FT[name]
                for h in range(halves):
                    for gi in range(2):
                        o = bank(n)
                        for k in range(KC):
                            m = pe.matmul(o[0:GR, 0:width], lhsT=GW[:, k, gi, :], rhs=x[:, k, h * width:h * width + width],
                                          start=(k == 0), stop=(k == KC - 1))
                        m.then_inc(f_ready, 1)
                        n += 1

            def gate_columns(nc_, free, i):
                pe.wait_ge(f_free, free)
                pe.wait_ge(s("g_e"), i + 1)
                for c in range(nc_):
                    for j, row in enumerate((uu, enm, wsr)):
                        m = pe.transpose(PS[:, c // 4, ((c % 4) * 3 + j) * GR:((c % 4) * 3 + j) * GR + GR],
                                         row[0:GR, c * P:c * P + P], ident[0:GR, 0:GR])
                for dh in range(2 * MH):
                    m = pe.matmul(PS[:, 2, dh * NC:dh * NC + nc_], lhsT=SEL[0:GR, dh, :], rhs=mpc[0:GR, 0:nc_],
                                  start=True, stop=True)
                m.then_inc(s("g_t"), 1)
                pe.wait_ge(s("g_c"), i + 1)

            def scan(steps, i0, j0, V):
                for idx, (c, d) in enumerate(steps):
                    i = i0 + idx
                    outs = j0 is not None
                    j = idx
                    if i >= 1:
                        pe.wait_ge(s("m_w"), i)
                    if outs and j >= 1:
                        pe.wait_ge(s("m_arg"), j)
                    for h in range(MH):
                        m = pe.matmul(PS[:, 0, h * P:h * P + P], lhsT=SEL[0:GR, d * MH + h, :], rhs=MM[0:GR, c * P:c * P + P],
                                      start=True, stop=True)
                    m.then_inc(s("m_b"), 1)
                    if outs:
                        if j >= 1:
                            pe.wait_ge(s("m_pt"), j)
                        for h in range(MH):
                            m = pe.matmul(PS[:, 1, h * P:h * P + P], lhsT=kT[:, h, c * P:c * P + P], rhs=qT[:, h, c * P:c * P + P],
                                          start=True, stop=True)
                        m.then_inc(s("m_st"), 1)
                        pe.wait_ge(s("m_qs"), j + 1)
                        pe.wait_ge(s("m_cu"), 2 * i - 2)
                        pe.wait_ge(s("m_pt"), j + 1)
                        if j >= 1:
                            pe.wait_ge(s("m_h"), j)
                        for h in range(MH):
                            pe.matmul(PS[:, 2 + h, 0:V1], lhsT=QS[:, j % 2, h * P:h * P + P], rhs=CC[:, d * MH + h, :],
                                      start=True, stop=False)
                            m = pe.matmul(PS[:, 2 + h, 0:V1], lhsT=PP[:, j % 2, h * P:h * P + P], rhs=V[:, c, h, :],
                                          start=False, stop=True)
                        m.then_inc(s("m_n"), 1)
                    pe.wait_ge(s("m_ks"), i + 1)
                    for pair in range(2):
                        if 2 * i + pair >= 1:
                            pe.wait_ge(s("m_cu"), 2 * i + pair)
                        for h in (2 * pair, 2 * pair + 1):
                            m = pe.matmul(PS[:, 6 + h % 2, 0:V1], lhsT=KS[:, i % 2, h * P:h * P + P], rhs=V[:, c, h, :],
                                          start=True, stop=True)
                        m.then_inc(s("m_d"), 1)

            gates("cg", hcT, 1, MEM)
            gemm_t(TT["ck"], weights(M0), x=hcT, tiles=2)
            for j in range(2):
                gemm_t(TT["cv"] + 2 * j, weights(M0 + 1 + j), x=hcT, tiles=2)
            pe.wait_ge(s("v_one"), 1)
            gate_columns(2, FT["xtm"], 0)
            pe.wait_ge(t_free, TT["mk"])
            scan(CTX_STEPS, 0, None, VX)
            pe.wait_ge(s("m_w"), 4)
            pe.wait_ge(s("m_cu"), 8)
            transposes("xtm", XR, s("xr_norm"), lambda h: 4 * h + 4)
            pe.wait_ge(f_free, FT["mg"])
            gates("mg", XT, 2, BW)
            gemm_f("mq", FT["mq"], weights(M0 + 3), range(4))
            gemm_t(TT["mk"], weights(M0 + 4))
            for h in range(MH):
                for half in range(2):
                    pe.wait_ge(t_free, TT["mk"] + 4 * half + 4)
                    o = bank(FT["kT"] + 2 * h + half)
                    for j in range(4):
                        m = pe.transpose(o[:, j * P:j * P + P], KK[:, 4 * half + j, h * P:h * P + P], ident[:, :])
                    m.then_inc(f_ready, 1)
            for j in range(2):
                gemm_t(TT["mv"] + 8 * j, weights(M0 + 5 + j))
            gate_columns(NC, FT["yT"], 1)
            pe.wait_ge(t_free, TT["mo"])
            pe.wait_ge(s("v_one"), 2)
            scan(X_STEPS, 4, 0, VV)
            pe.wait_ge(s("m_h"), 16)
            pe.wait_ge(s("m_cu"), 40)
            for j in range(2):
                gemm_t(TT["mo"] + 8 * j, weights(M0 + 7 + j))
            transposes("yT", Q, s("o_y"), lambda h: NT + 4 * h + 4)
            pe.wait_ge(f_free, FT["xtf"])
            for j in range(2):
                gemm_t(TT["mout"] + 8 * j, weights(M0 + 9 + j))
            transposes("xtf", XN, s("xn_norm"), lambda h: 4 * h + 4)
            pe.wait_ge(f_free, FT["up2"])

            def up2(g, j, buf):
                pe.wait_ge(w_in[buf], g * 64 + loaded(G0 + j))
                for m_ in range(8):
                    n = FT["up2"] + 8 * j + m_
                    part = m_ // 2
                    a = (part % 2) * 256 + (part // 2) * P
                    h = m_ % 2
                    pe.wait_ge(f_free, g * 16 + (n - 3))
                    for k in range(KC):
                        m = pe.matmul(PS[:, n % 4, :], lhsT=WB[buf][:, k, a:a + P], rhs=XT[:, k, h * BW:h * BW + BW],
                                      start=(k == 0), stop=(k == KC - 1))
                    m.then_inc(f_ready, 1)

            def down2(g, j, buf, kc, at):
                pe.wait_ge(w_in[buf], at)
                for t in range(NT):
                    n = TT["down2"] + 8 * j + t
                    pe.wait_ge(t_free, g * 16 + (n - 3))
                    for k in range(kc):
                        m = pe.matmul(PS[:, 4 + n % 4, :], lhsT=HH[:, k, t * P:t * P + P], rhs=WB[buf][:, k, :],
                                      start=(k == 0), stop=(k == kc - 1))
                    m.then_inc(t_ready, 1)

            with pe.Fori(0, N_G) as g:
                for j in range(2):
                    up2(g, j, 1 - j)
                pe.wait_ge(s("hidden"), g * 4 + 6)
                for j in range(2):
                    down2(g, j, 1 - j, 4, g * 64 + loaded(G0 + 2 + j))
            up2(N_G, 0, 1)
            pe.wait_ge(s("hidden"), 4 * N_G + 4)
            down2(N_G, 0, 0, 2, loaded(G0 + 4 * N_G + 1))
            down2(N_G, 1, 1, 2, loaded(G0 + 4 * N_G + 2))

        @block.scalar
        def _(act):
            own = [0]

            def mark(ins):
                ins.then_inc(own_act, 1)
                own[0] += 1

            def settled():
                act.wait_ge(own_act, own[0])

            def load_rows(*rows):
                for i, v in rows:
                    act.dma_start(ROW[:, i, :], v.partition_broadcast(P)).then_inc(rows_in, 16)

            act.dma_start(cols[:, :], I["cols_h"]).then_inc(cols_in, 16)
            load_rows((0, I["ln_emb_g"]), (1, I["ln_emb_b"]))

            def root(r, n=NT):
                act.wait_ge(s("ln_stat"), r)
                act.activation(sdv[:, 0:n], ve[:, 0:n], ACT.Sqrt).then_inc(s("ln_sd"), 1)

            def empty(n, out_ap, bias=0.0, scale=1.0, width=BW, rows=P, func=ACT.Identity):
                act.wait_ge(f_ready, n + 1)
                act.activation(out_ap, PS[0:rows, n % 4, 0:width], func, bias=bias, scale=scale).then_inc(f_free, 1)

            def empty_xt(name, scale=None, bias=None):
                for h in range(2):
                    for k in range(KC):
                        o = XT[:, k, BW * h:BW * h + BW]
                        if scale is None:
                            empty(FT[name] + 8 * h + k, o)
                        else:
                            empty(FT[name] + 8 * h + k, o, bias=bias(k), scale=scale(k))

            root(1)
            act.wait_ge(cols_in, 16)
            act.activation(cx[:, :, :].rearrange("p k c -> p (k c)"), cols[:, COLS["c"][0]:COLS["c"][1]],
                           ACT.Silu).then_inc(s("cx_ready"), 1)
            empty_xt("xt0")
            act.wait_ge(s("ln_done"), NT)
            attn_in = s("attn_in")
            act.dma_start(mrow[:, 0:P], I["b_in"][0, 640:768].partition_broadcast(P)).then_inc(s("misc_in"), 16)
            act.dma_start(mrow[:, P:2 * P], I["b_in"][0, 1280:1408].partition_broadcast(P)).then_inc(s("misc_in"), 16)
            act.dma_start(mrow[:, 2 * P:MISC], I["b_in"][0, 1920:1992].partition_broadcast(P)).then_inc(s("misc_in"), 16)
            act.dma_start(kvg, I["dsa_kv_norm_g"][0].partition_broadcast(P)).then_inc(s("misc_in"), 16)
            act.dma_start(ikg[:, 0, :], I["idx_k_ln_g"][0].partition_broadcast(P)).then_inc(s("misc_in"), 16)
            act.dma_start(ikg[:, 1, :], I["idx_k_ln_b"][0].partition_broadcast(P)).then_inc(s("misc_in"), 16)
            act.dma_start(hot[0:NB + 1, :, :], I["hot_h"]).then_inc(s("relb_in"), 16)
            act.wait_ge(s("relb_one"), 1)
            act.dma_start(relb[0:NB, :], I["rel_bias"]).then_inc(s("relb_in"), 16)
            act.dma_start(wuk, I["dsa_w_uk"][0].rearrange("h c d -> c h d")).then_inc(s("relb_in"), 16)
            act.dma_start(wuv, I["dsa_w_uv"][0].rearrange("h c d -> c h d")).then_inc(attn_in, 16)
            act.dma_start(sink, I["swa_sinks"][0].partition_broadcast(P)).then_inc(attn_in, 16)
            for name, dst in (("qa", Q[:, 0:4, :]), ("qb", Q[:, 4:8, :]), ("iq", iqT)):
                for f in range(4):
                    for h in range(2):
                        empty(FT[name] + 2 * f + h, dst[:, f, BW * h:BW * h + BW],
                              bias=cols[:, COLS[name][0] + f:COLS[name][0] + f + 1])
            for h in range(2):
                a, z = BW * h, BW * h + BW
                empty(FT["ka"] + h, kaS[:, h, :], bias=cols[:, COLS["ka"][0]:COLS["ka"][1]])
                act.wait_ge(f_free, FT["ka"] + h + 1)
                for kv in range(2):
                    for r in range(2):
                        mark(act.activation(kaT[DH * r:DH * r + DH, kv, a:z], kaS[DH * kv:DH * kv + DH, h, :], ACT.Copy))
            for g in range(2):
                empty(FT["vb"] + g, vb[0:NH, g, :], width=N_BIAS, rows=NH)
            act.wait_ge(f_free, FT["vb"] + 2)
            for g in range(2):
                act.dma_start(bias_d[g * NH:g * NH + NH], vb[0:NH, g, :].unsqueeze(1).to_broadcast([NH, P, N_BIAS])
                              ).then_inc(s("vb_out"), 16)
            empty(FT["ukT"], wukT.rearrange("p a b -> p (a b)"))
            root(2, 16)
            for i, dst in ((0, cT), (2, ikT)):
                for h in range(2):
                    empty(FT["ckT"] + i + h, dst[:, BW * h:BW * h + BW])
            act.wait_ge(s("vb_out"), 32)
            bt = bias_d.tensor
            act.wait_ge(f_ready, FT["ka"] + 1)
            act.wait_ge(t_ready, TT["misc"] + 8)
            for g in range(2):
                for h4 in range(2):
                    act.dma_start(bias[:, g * NH + 4 * h4:g * NH + 4 * h4 + 4, :],
                                  bass.AP(bt, (g * NH + 4 * h4) * P * N_BIAS + P - 1,
                                          [[N_BIAS - 1, P], [P * N_BIAS, 4], [1, 2 * P]])).then_inc(attn_in, 16)
            act.dma_start(far, bass.AP(bt, NH * P * N_BIAS, [[0, P], [P * N_BIAS, NH]]), allow_slow_non_contiguous=True).then_inc(attn_in, 16)
            for j in range(12):
                if j >= 4:
                    act.wait_ge(s(f"mods_out{j % 4}"), 16 * (j // 4))
                empty(FT["ada"] + j, modr[0:2, j % 4, :], rows=2)
                act.wait_ge(f_free, FT["ada"] + j + 1)
                act.dma_start(mods_d[:, BW * j:BW * j + BW], modr[0:2, j % 4, :]).then_inc(s(f"mods_out{j % 4}"), 16)
            for j in range(4):
                act.wait_ge(s(f"mods_out{j}"), 16 * 3)
            for n in range(NT):
                w0 = P if n == 0 else 0
                act.wait_ge(s("a_m"), n + 1)
                for h in range(NH):
                    mark(act.activation(SB[:, h, w0:], SB[:, h, w0:], ACT.Exp, bias=nm[:, h:h + 1],
                                        accum_out=den[:, h:h + 1]))
                act.activation(es, sd, ACT.Exp).then_inc(s("a_p"), 1)
                for b in range(4):
                    act.wait_ge(s("a_t"), 4 * n + b + 1)
                    if n == 0:
                        v = PS[:, b, :].rearrange("p (a b c) -> p a b c", a=2, b=2)
                        act.activation(PT[:, 4 * b + 1:4 * b + 4:2, :], v[:, :, 1, :], ACT.Copy).then_inc(s("a_te"), 1)
                    else:
                        act.activation(PT[:, 4 * b:4 * b + 4, :].rearrange("p a b -> p (a b)"), PS[:, b, :],
                                       ACT.Copy).then_inc(s("a_te"), 1)
                L = (n + 1) * P
                if n >= 2:
                    act.wait_ge(s("a_o"), n + 1)
                    for h in range(NH):
                        i = NH * (n - 2) + h
                        act.wait_ge(s("ix_d"), i + 1)
                        if h >= 2:
                            act.wait_ge(s("ix_s"), i - 1)
                        act.activation(RL[:, h % 2, 0:L], PSf[:, 1024 * (h % 4):1024 * (h % 4) + L], ACT.Relu,
                                       scale=DH ** -0.5).then_inc(s("ix_r"), 1)
                for b in range(2):
                    act.wait_ge(s("d_q"), 2 * n + b + 1)
                    act.activation(QL[:, b:NH:2, :], PS[:, b, :].rearrange("p (a b) -> p a b", a=4), ACT.Copy,
                                   scale=DH ** -0.5).then_inc(s("d_qe"), 1)
                for i in range(NH + 2):
                    if i < NH:
                        act.wait_ge(s("d_m"), NH * n + i + 1)
                        act.activation(LG[:, i % 2, 0:L], LG[:, i % 2, 0:L], ACT.Exp, bias=nm[:, i:i + 1],
                                       accum_out=den[:, i:i + 1]).then_inc(s("d_e"), 1)
                    if 1 <= i <= NH:
                        h = i - 1
                        act.wait_ge(s("d_t"), NH * n + h + 1)
                        if n >= 2 and h < 2:
                            act.wait_ge(s("ix_s"), NH * (n - 1))
                        act.activation(PT[:, 8 * (h % 2):8 * (h % 2) + n + 1, :].rearrange("p a b -> p (a b)"),
                                       PSf[:, 1024 * (h % 2):1024 * (h % 2) + L], ACT.Copy).then_inc(s("d_te"), 1)
                    if i >= 2:
                        h = i - 2
                        act.wait_ge(s("d_o"), NH * n + h + 1)
                        if h == 0 and n >= 2:
                            act.wait_ge(s("tk_done"), n - 1)
                        act.activation(OL[:, h, :], PS[:, 2 * (h % 2), 0:P], ACT.Copy).then_inc(s("d_oe"), 1)
            act.wait_ge(s("d_fe"), NT)
            act.wait_ge(s("d_oe"), NH * NT)
            load_rows((0, I["ln1_g"][0]), (1, I["ln1_b"][0]), (2, I["b_o"][0]))
            for k in range(0, KC, 2):
                empty(FT["memT"] + k // 2, memT[:, k:k + 2, :].rearrange("p a b -> p (a b)"))
            for f in range(KC):
                empty(FT["xk"] + f, xkT[:, f, :], bias=cols[:, COLS["xk"][0] + f:COLS["xk"][0] + f + 1], width=MEM)
            root(3)
            empty_xt("xt1")
            load_rows((0, I["ln2_g"][0]), (1, I["ln2_b"][0]), (2, I["xa_bo"][0]))
            for f in range(KC):
                for h in range(2):
                    empty(FT["xq"] + 2 * f + h, Q[:, f, BW * h:BW * h + BW], bias=cols[:, COLS["xq"][0] + f:COLS["xq"][0] + f + 1])
            for i in range(NT + 1):
                if i < NT:
                    act.wait_ge(s("x_m"), i + 1)
                    if i >= 2:
                        act.wait_ge(s("x_t"), i - 1)
                    for h in range(XH):
                        ins = act.activation(XP[:, i % 2, h * MEM:h * MEM + MEM],
                                             PSf[:, 1024 * (i % 2) + h * MEM:1024 * (i % 2) + h * MEM + MEM], ACT.Exp,
                                             bias=xn[:, i % 2, h:h + 1], scale=XD ** -0.5, accum_out=xd[:, i % 2, h:h + 1])
                    ins.then_inc(s("x_p"), 1)
                if i >= 1:
                    t = i - 1
                    act.wait_ge(s("x_t"), t + 1)
                    act.activation(XPT[:, t % 2, :], PSf[:, 2048 + 1024 * (t % 2):3072 + 1024 * (t % 2)], ACT.Copy).then_inc(s("x_te"), 1)
            root(4)
            empty_xt("xt2")
            load_rows((0, I["ln3_g"][0]), (1, I["ln3_b"][0]), (2, I["b_down"][0]))
            with act.Fori(0, N_UP) as g:
                for m in range(16):
                    act.wait_ge(s("squared"), g * 16 + (m + 1))
                    act.wait_ge(f_ready, g * 16 + (FT["up"] + m + 1))
                    act.activation(RU[:, m % 2, :], PS[:, (FT["up"] + m) % 4, :], ACT.Relu,
                                   bias=upb[:, m // 8, (m % 8) // 2:(m % 8) // 2 + 1]).then_inc(f_free, 1)
            root(5)
            rows2_in = s("rows2_in")

            def load_rows2(*rows):
                for dst, v in rows:
                    act.dma_start(dst, v.partition_broadcast(P)).then_inc(rows2_in, 16)

            mb = I["m_in_b_2"][0]
            act.wait_ge(s("ln_done"), 4 * NT)
            load_rows2((krow, mb[512:1024]), (ROW[:, 2, :], mb[1024:2048]))
            root(6, 2)
            act.wait_ge(s("mod_ready"), 1)
            for k in range(KC):
                act.wait_ge(f_ready, FT["ctxT"] + k // 2 + 1)
                n = FT["ctxT"] + k // 2
                ins = act.activation(hcT[:, k, :], PS[:, n % 4, MEM * (k % 2):MEM * (k % 2) + MEM], ACT.Identity,
                                     bias=modc[:, 4, k:k + 1], scale=modc[:, 5, k:k + 1])
                if k % 2 == 1:
                    ins.then_inc(f_free, 1)

            def gates(name, i, halves, width):
                n = FT[name]
                act.wait_ge(s("gw_in"), 128)
                for h in range(halves):
                    for row in (li, lf):
                        empty(n, row[0:GR, h * width:h * width + width], bias=gb[0:GR, (n - FT[name]) % 2:(n - FT[name]) % 2 + 1],
                              width=width, rows=GR)
                        n += 1
                w = halves * width
                act.wait_ge(s("g_a"), i + 1)
                mark(act.activation(enm[0:GR, 0:w], bb[0:GR, 0:w], ACT.Exp))
                settled()
                act.activation(enm[0:GR, 0:w], enm[0:GR, 0:w], ACT.Ln, bias=1.0).then_inc(s("g_l"), 1)

            def gates_exp(i, w):
                act.wait_ge(s("g_b"), i + 1)
                mark(act.activation(enm[0:GR, 0:w], tmp[0:GR, 0:w], ACT.Exp, scale=-1.0))
                act.activation(wsr[0:GR, 0:w], lf[0:GR, 0:w], ACT.Exp).then_inc(s("g_e"), 1)

            def scan(steps, i0, outs):
                for idx, (c, d) in enumerate(steps):
                    i, j = i0 + idx, idx
                    act.wait_ge(s("m_b"), i + 1)
                    if i >= 2:
                        act.wait_ge(s("m_cu"), 2 * i - 2)
                    if outs and j >= 2:
                        act.wait_ge(s("m_qs"), j - 1)
                    for h in range(MH):
                        ins = act.activation(WI[:, i % 2, h * P:h * P + P], PS[:, 0, h * P:h * P + P], ACT.Exp,
                                             bias=MPB[:, d * MH + h, c:c + 1], scale=-1.0)
                    ins.then_inc(s("m_w"), 1)
                    if outs:
                        act.wait_ge(s("m_arg"), j + 1)
                        for h in range(MH):
                            ins = act.activation(DD[:, j % 2, h * P:h * P + P], DD[:, j % 2, h * P:h * P + P], ACT.Exp,
                                                 bias=COL[:, c, 0, 32 * d + h:32 * d + h + 1])
                        ins.then_inc(s("m_e"), 1)

            gates("cg", 0, 1, MEM)
            gates_exp(0, MEM)
            act.wait_ge(s("g_c"), 1)
            scan(CTX_STEPS, 0, False)
            act.wait_ge(s("m_d"), 8)
            load_rows2((ROW[:, 2, :], mb[1024:2048]))
            root(7)
            empty_xt("xtm", scale=lambda k: modc[:, 1, k:k + 1], bias=lambda k: modc[:, 0, k:k + 1])
            n = FT["mg"]
            gates("mg", 1, 2, BW)
            for f in range(MH):
                for h in range(2):
                    empty(FT["mq"] + 2 * f + h, qT[:, f, BW * h:BW * h + BW], bias=cols[:, COLS["mq"][0] + f:COLS["mq"][0] + f + 1])
            gates_exp(1, T)
            for h in range(MH):
                for half in range(2):
                    empty(FT["kT"] + 2 * h + half, kT[:, h, BW * half:BW * half + BW])
            act.wait_ge(s("g_c"), 2)
            scan(X_STEPS, 4, True)
            act.wait_ge(s("m_h"), 16)
            act.wait_ge(s("m_d"), 40)
            load_rows2((ROW[:, 0, :], mb[2048:3072]), (ROW[:, 2, :], I["m_norm_g_2"][0]))
            root(8, 32)
            for m in range(16):
                act.wait_ge(t_free, TT["mo"] + m + 1)
                act.activation(OG[:, m % 2, :], OG[:, m % 2, :], ACT.Sigmoid).then_inc(s("o_s"), 1)
            act.wait_ge(s("o_y"), 16)
            load_rows2((ROW[:, 0, :], mods_d[0, 2 * D:3 * D]), (ROW[:, 1, :], I["ada_b_2"][0, 2 * D:3 * D]),
                       (ROW[:, 2, :], I["post_mix_g_2"][0]))
            empty_xt("yT")
            root(9)
            act.wait_ge(s("x_new"), NT)
            load_rows2((ROW[:, 0, :], mods_d[0, 5 * D:6 * D]), (ROW[:, 1, :], I["ada_b_2"][0, 5 * D:6 * D]),
                       (ROW[:, 2, :], I["post_ffn_g_2"][0]))
            root(10)
            empty_xt("xtf", scale=lambda k: modc[:, 3, k:k + 1], bias=lambda k: modc[:, 2, k:k + 1])

            def chunks2(g, n_chunks):
                for c in range(n_chunks):
                    act.wait_ge(s("hidden"), g * 4 + (c + 1))
                    for m in range(4):
                        n = FT["up2"] + 4 * c + m
                        dst = (UU, GG)[m // 2]
                        act.wait_ge(f_ready, g * 16 + (n + 1))
                        act.activation(dst[:, c % 2, BW * (m % 2):BW * (m % 2) + BW], PS[:, n % 4, :], ACT.Copy).then_inc(f_free, 1)
                    act.wait_ge(s("conv"), g * 4 + (c + 1))
                    act.activation(TC[:, c % 2, :], TC[:, c % 2, :], ACT.Silu).then_inc(s("silu"), 1)

            with act.Fori(0, N_G) as g:
                chunks2(g, 4)
            chunks2(N_G, 2)
            root(11)

        @block.vector
        def _(dve):
            own = [0]

            def mark(ins):
                ins.then_inc(own_dve, 1)
                own[0] += 1

            def settled():
                dve.wait_ge(own_dve, own[0])

            def stats(t0, rows, parts):
                w = rows.shape[1] // parts
                for j in range(parts):
                    mark(dve.bn_stats(st[:, 2 * t0 + j if parts == 2 else t0, :], rows[:, j * w:j * w + w]))
                settled()
                if parts == 2:
                    mark(dve.bn_aggr(mv[:, t0, :], stf[:, 12 * t0:12 * t0 + 12]))
                else:
                    mark(dve.bn_aggr(mv[:, t0, :], stf[:, 6 * t0:6 * t0 + 6]))

            def rstd(n, r):
                dve.wait_ge(s("ln_sd"), r)
                mark(dve.reciprocal(rs[:, 0:n], sdv[:, 0:n]))
                settled()

            def layer_norm(i, r, ready):
                for t in range(NT):
                    ready(t)
                    stats(t, XR[:, t, :], 2)
                settled()
                dve.tensor_scalar(ve[:, 0:NT], mv[:, 0:NT, 1], LN_EPS, None, ALU.add).then_inc(s("ln_stat"), 1)
                rstd(NT, r)
                for t in range(NT):
                    mark(dve.tensor_scalar(XR[:, t, :], XR[:, t, :], mv[:, t, 0:1], rs[:, t:t + 1], ALU.subtract, ALU.mult))
                    settled()
                    dve.tensor_tensor(XR[:, t, :], XR[:, t, :], ROW[:, 0, :], ALU.mult).then_inc(s("ln_half"), 1)

            def ready0(t):
                if t % 4 == 0:
                    dve.wait_ge(x_in, 32)
            ready0(0)
            rows2_v = s("rows2_in")
            dve.wait_ge(rows_in, 32)
            layer_norm(0, 1, ready0)

            dve.wait_ge(s("misc_in"), 96)
            for t in range(NT):
                n = TT["misc"] + t
                dve.wait_ge(t_ready, n + 1)
                dve.tensor_tensor(misc[:, t, :], PS[:, 4 + n % 4, 0:MISC], mrow, ALU.add).then_inc(t_free, 1)
            for t in range(NT):
                dve.wait_ge(t_free, TT["misc"] + t + 1)
                stats(t, misc[:, t, P:2 * P], 1)
                stats(NT + t, misc[:, t, 2 * P:2 * P + DH], 1)
            settled()
            mark(dve.tensor_tensor(ve[:, 0:NT], mv[:, 0:NT, 0], mv[:, 0:NT, 0], ALU.mult))
            settled()
            mark(dve.scalar_tensor_tensor(ve[:, 0:NT], ve[:, 0:NT], LN_EPS, mv[:, 0:NT, 1], ALU.add, ALU.add))
            dve.tensor_scalar(ve[:, NT:2 * NT], mv[:, NT:2 * NT, 1], LN_EPS, None, ALU.add).then_inc(s("ln_stat"), 1)
            rstd(2 * NT, 2)
            for t in range(NT):
                mark(dve.tensor_scalar(cR[:, t, :], misc[:, t, P:2 * P], rs[:, t:t + 1], None, ALU.mult))
                mark(dve.tensor_scalar(ikn[:, t, 0:DH], misc[:, t, 2 * P:2 * P + DH], mv[:, NT + t, 0:1],
                                       rs[:, NT + t:NT + t + 1], ALU.subtract, ALU.mult))
            mark(dve.tensor_scalar(iwt, misc[:, :, 2 * P + DH:MISC], NH ** -0.5, None, ALU.mult))
            settled()
            mark(dve.tensor_tensor(ikn[:, :, 0:DH], ikn[:, :, 0:DH], over_mid(ikg[:, 0, :], NT), ALU.mult))
            dve.tensor_tensor(cR, cR, over_mid(kvg, NT), ALU.mult).then_inc(s("ck_ready"), 1)
            settled()
            mark(dve.tensor_tensor(ikn[:, :, 0:DH], ikn[:, :, 0:DH], over_mid(ikg[:, 1, :], NT), ALU.add))
            settled()
            dve.tensor_copy(ikn[:, :, DH:2 * DH], ikn[:, :, 0:DH]).then_inc(s("ck_ready"), 1)

            dve.wait_ge(s("attn_in"), 16 * 7)
            dve.wait_ge(s("ck_ready"), 2)
            for n in range(NT):
                w0 = P if n == 0 else 0
                L = (n + 1) * P
                for e in range(4):
                    dve.wait_ge(s("a_s"), 4 * n + e + 1)
                    if n > 0 and e == 0:
                        dve.wait_ge(s("d_t"), NH * n)
                    r, h0 = e % 2, 4 * (e // 2) + e % 2
                    v = PS[:, 2 * r + e // 2, :].rearrange("p (a b) -> p a b", a=2)
                    dve.scalar_tensor_tensor(SB[:, h0:h0 + 3:2, w0:], v[:, :, w0:], DH ** -0.5,
                                             bias[:, h0:h0 + 3:2, w0:], ALU.mult, ALU.add).then_inc(s("a_sb"), 1)
                dve.wait_ge(s("a_sb"), 4 * n + 4)
                mark(dve.tensor_reduce(mx, SB[:, :, w0:], AX.X, ALU.max))
                settled()
                mark(dve.tensor_tensor(mx, mx, sink, ALU.max))
                settled()
                mark(dve.tensor_scalar(nm, mx, -1.0, None, ALU.mult))
                dve.tensor_tensor(sd, sink, mx, ALU.subtract).then_inc(s("a_m"), 1)
                dve.wait_ge(s("a_p"), n + 1)
                mark(dve.tensor_tensor(den, den, es, ALU.add))
                settled()
                mark(dve.reciprocal(den, den))
                settled()
                dve.tensor_tensor(SB[:, :, w0:], SB[:, :, w0:], over_last(den, 2 * P - w0), ALU.mult).then_inc(s("a_r"), 1)
                dve.wait_ge(s("a_o"), n + 1)
                dve.tensor_copy(Q[:, 0:4, n * P:n * P + P], PS[:, 4, :].rearrange("p (a b) -> p a b", a=4)).then_inc(s("a_oe"), 1)
                if n >= 2:
                    for h in range(NH):
                        i = NH * (n - 2) + h
                        dve.wait_ge(s("ix_r"), i + 1)
                        if h == 0:
                            if n > 2 or True:
                                dve.wait_ge(s("d_f"), n)
                            dve.tensor_scalar(score[:, 0:L], RL[:, 0, 0:L], iwt[:, n, 0:1], None, ALU.mult).then_inc(s("ix_s"), 1)
                        else:
                            dve.wait_ge(s("ix_s"), i)
                            dve.scalar_tensor_tensor(score[:, 0:L], RL[:, h % 2, 0:L], iwt[:, n, h:h + 1], score[:, 0:L],
                                                     ALU.mult, ALU.add).then_inc(s("ix_s"), 1)
                    dve.wait_ge(s("ix_c"), n - 1)
                    for i in range(TOPK // 8):
                        src = score if i == 0 else work
                        settled()
                        mark(dve.max(top, src[:, 0:L]))
                        settled()
                        mark(dve.match_replace(work[:, 0:L], top, src[:, 0:L], TAKEN))
                    settled()
                    dve.tensor_scalar(msk[:, 0:L], work[:, 0:L], TAKEN / 2, NEG, ALU.is_ge, ALU.mult).then_inc(s("tk_done"), 1)
                    dve.wait_ge(s("tk_done"), n - 1)
                near = slice((n - 1) * P if n else 0, L)
                for i in range(NH + 1):
                    if i < NH:
                        dve.wait_ge(s("d_l"), NH * n + i + 1)
                        if i >= 2:
                            dve.wait_ge(s("d_t"), NH * n + i - 1)
                        if i == 0:
                            dve.wait_ge(s("a_t"), 4 * n + 4)
                        pair = PSf[:, 1024 * (2 + i % 2):1024 * (2 + i % 2) + L]
                        lg = LG[:, i % 2, :]
                        if n >= 2:
                            mark(dve.scalar_tensor_tensor(lg[:, 0:(n - 1) * P], pair[:, 0:(n - 1) * P], far[:, i:i + 1],
                                                          msk[:, 0:(n - 1) * P], ALU.add, ALU.add))
                        dve.tensor_tensor(lg[:, near], pair[:, near], bias[:, NH + i, w0:], ALU.add).then_inc(s("d_lb"), 1)
                        dve.wait_ge(s("d_lb"), NH * n + i + 1)
                        if n >= 2:
                            mark(dve.tensor_tensor(lg[:, near], lg[:, near], msk[:, near], ALU.add))
                            settled()
                        dve.tensor_reduce(nm[:, i:i + 1], lg[:, 0:L], AX.X, ALU.max, negate=True).then_inc(s("d_m"), 1)
                    if i >= 1:
                        h = i - 1
                        dve.wait_ge(s("d_e"), NH * n + h + 1)
                        mark(dve.reciprocal(den[:, h:h + 1], den[:, h:h + 1]))
                        settled()
                        dve.tensor_scalar(LG[:, h % 2, 0:L], LG[:, h % 2, 0:L], den[:, h:h + 1], None, ALU.mult).then_inc(s("d_n"), 1)
                dve.wait_ge(s("d_f"), n + 1)
                dve.tensor_copy(Q[:, 4:8, n * P:n * P + P], PS[:, 0, :].rearrange("p (a b) -> p a b", a=4)).then_inc(s("d_fe"), 1)

            def residual(i, name=None):
                dve.wait_ge(rows_in, 32 + 48 * (i + 1))
                for t in range(NT):
                    if name and t % 4 == 0:
                        dve.wait_ge(f_ready, FT[name] + 2 * t + 8)
                    dve.scalar_tensor_tensor(XR[:, t, :], XR[:, t, :], ALPHA, ROW[:, 2, :], ALU.mult,
                                             ALU.add).then_inc(s("resid"), 1)

            def add_tiles(name, i):
                for j in range(2):
                    for t in range(NT):
                        n = TT[name] + 8 * j + t
                        dve.wait_ge(s("resid"), NT * i + t + 1)
                        dve.wait_ge(t_ready, n + 1)
                        v = XR[:, t, BW * j:BW * j + BW]
                        dve.tensor_tensor(v, v, PS[:, 4 + n % 4, :], ALU.add).then_inc(t_free, 1)

            residual(0)
            add_tiles("wo", 0)
            layer_norm(1, 3, lambda t: dve.wait_ge(t_free, TT["wo"] + 8 + t + 1))
            dve.wait_ge(s("mem_in"), 32)
            for j in range(2):
                for t in range(2):
                    n = TT["xv"] + 2 * j + t
                    dve.wait_ge(t_ready, n + 1)
                    dve.tensor_tensor(xv[:, t, BW * j:BW * j + BW], PS[:, 4 + n % 4, :], vrow[:, BW * j:BW * j + BW],
                                      ALU.add).then_inc(t_free, 1)
            residual(1, "xt1")
            for i in range(NT + 2):
                if i < NT:
                    dve.wait_ge(s("x_s"), i + 1)
                    mark(dve.tensor_reduce(xm[:, i % 2, :], PSf[:, 1024 * (i % 2):1024 * (i % 2) + 1024]
                                           .rearrange("p (a b) -> p a b", a=XH), AX.X, ALU.max))
                    settled()
                    dve.tensor_scalar(xn[:, i % 2, :], xm[:, i % 2, :], -XD ** -0.5, None, ALU.mult).then_inc(s("x_m"), 1)
                if 1 <= i <= NT:
                    t = i - 1
                    dve.wait_ge(s("x_p"), t + 1)
                    mark(dve.reciprocal(xd[:, t % 2, :], xd[:, t % 2, :]))
                    settled()
                    v = XP[:, t % 2, :].rearrange("p (a b) -> p a b", a=XH)
                    dve.tensor_tensor(v, v, over_last(xd[:, t % 2, :], MEM), ALU.mult).then_inc(s("x_n"), 1)
                if i >= 2:
                    t = i - 2
                    dve.wait_ge(s("x_o"), t + 1)
                    dve.tensor_copy(Q[:, :, t * P:t * P + P], PSf[:, 2048 + 1024 * (t % 2):3072 + 1024 * (t % 2)]
                                    .rearrange("p (a b) -> p a b", a=8)).then_inc(s("x_oe"), 1)
            add_tiles("xo", 1)
            layer_norm(2, 4, lambda t: dve.wait_ge(t_free, TT["xo"] + 8 + t + 1))
            residual(2, "xt2")
            dve.wait_ge(s("resid"), 3 * NT)
            with dve.Fori(0, N_UP) as g:
                for m in range(16):
                    dve.wait_ge(t_ready, g * 16 + (TT["down"] + m + 1))
                    v = XR[:, m % 8, BW * (m // 8):BW * (m // 8) + BW]
                    dve.tensor_tensor(v, v, PS[:, 4 + (TT["down"] + m) % 4, :], ALU.add).then_inc(t_free, 1)
            layer_norm(3, 5, lambda t: dve.wait_ge(t_free, TT["down"] + 56 + t + 1))

            def mean_square(n, eps):
                settled()
                mark(dve.tensor_tensor(ve[:, 0:n], mv[:, 0:n, 0], mv[:, 0:n, 0], ALU.mult))
                settled()
                dve.scalar_tensor_tensor(ve[:, 0:n], ve[:, 0:n], eps, mv[:, 0:n, 1], ALU.add, ALU.add).then_inc(s("ln_stat"), 1)

            dve.wait_ge(s("modc_in"), 96)
            sh = COLS["sh1"][0]
            mark(dve.tensor_tensor(modc[:, 0:4, :], modc[:, 0:4, :], cols[:, sh:sh + 32].rearrange("p (a b) -> p a b", a=4), ALU.add))
            mark(dve.tensor_tensor(modc[:, 4:6, :], modc[:, 4:6, :], cols[:, sh:sh + 16].rearrange("p (a b) -> p a b", a=2), ALU.add))
            settled()
            for i, name in ((1, "pre_mix"), (3, "pre_ffn"), (5, "pre_mix")):
                ins = dve.scalar_tensor_tensor(modc[:, i, :], modc[:, i, :], 1.0, cols[:, COLS[name][0]:COLS[name][1]],
                                               ALU.add, ALU.mult)
                if i < 5:
                    mark(ins)
                else:
                    ins.then_inc(s("mod_ready"), 1)
            dve.wait_ge(s("ctx_in"), 16)
            for t in range(2):
                stats(t, ctxR[:, t, :], 2)
            mean_square(2, RMS_EPS)
            rstd(2, 6)
            for t in range(2):
                ins = dve.tensor_scalar(ctxR[:, t, :], ctxR[:, t, :], rs[:, t:t + 1], None, ALU.mult)
                if t == 0:
                    mark(ins)
                else:
                    ins.then_inc(s("ctx_rows"), 1)
            mark(dve.memset(ones[0:GR, :], 1.0))
            mark(dve.memset(ms[0:GR, :], 0.0))
            mark(dve.memset(mpc[0:GR, :], 0.0))
            mark(dve.memset(MM[0:GR, :], 0.0))
            settled()

            def gates(i, w, steps, ready):
                dve.wait_ge(f_free, ready)
                n = w // P
                g = slice(0, GR)
                mark(dve.tensor_scalar(tmp[g, 0:w], lf[g, 0:w], 0.0, None, ALU.min))
                settled()
                dve.scalar_tensor_tensor(bb[g, 0:w], tmp[g, 0:w], 2.0, lf[g, 0:w], ALU.mult, ALU.subtract).then_inc(s("g_a"), 1)
                dve.wait_ge(s("g_l"), i + 1)
                mark(dve.tensor_tensor(lf[g, 0:w], tmp[g, 0:w], enm[g, 0:w], ALU.subtract))
                mark(dve.memset(bb[g, 0:w], 0.0))
                settled()

                def piece(v, c, d):
                    x = v[32 * d:32 * d + 4, c * P:c * P + P]
                    return x[:, ::-1] if d else x

                for c, d in steps:
                    mark(dve.tensor_tensor_scan(piece(bb, c, d), piece(ones, 0, d), piece(lf, c, d), 0.0, ALU.mult, ALU.add))
                settled()
                mark(dve.tensor_tensor(uu[g, 0:w], li[g, 0:w], bb[g, 0:w], ALU.subtract))
                settled()
                for d in range(2):
                    c = [c for c, d2 in steps if d2 == d][0]
                    mark(dve.tensor_copy(mpc[32 * d:32 * d + 4, c:c + 1], ms[32 * d:32 * d + 4, :]))
                settled()
                for k in range(0, len(steps), 2):
                    for c, d in steps[k:k + 2]:
                        mark(dve.tensor_tensor_scan(piece(MM, c, d), piece(uu, c, d), piece(uu, c, d),
                                                    mpc[32 * d:32 * d + 4, c:c + 1], ALU.max, ALU.max))
                    settled()
                    for e, (c, d) in enumerate(steps[k:k + 2]):
                        last = c * P + (0 if d else P - 1)
                        if k + 2 < len(steps):
                            c2 = steps[k + 2 + e][0]
                            to = mpc[32 * d:32 * d + 4, c2:c2 + 1]
                        else:
                            to = ms[32 * d:32 * d + 4, :]
                        r = slice(32 * d, 32 * d + 4)
                        mark(dve.tensor_tensor(to, bb[r, last:last + 1], MM[r, last:last + 1], ALU.add))
                    settled()
                mark(dve.tensor_tensor(tmp[g, 0:w], bb[g, 0:w], MM[g, 0:w], ALU.add))
                for d in range(2):
                    r = slice(32 * d, 32 * d + 4)
                    end = MM[r, 0:w].rearrange("p (a b) -> p a b", b=P)[:, :, (0 if d else P - 1)]
                    ins = dve.tensor_tensor(lf[r, 0:w].rearrange("p (a b) -> p a b", b=P), uu[r, 0:w].rearrange("p (a b) -> p a b", b=P),
                                            over_last(end, P), ALU.subtract)
                    if d == 0:
                        mark(ins)
                    else:
                        ins.then_inc(s("g_b"), 1)

            def gate_columns(n, i):
                dve.wait_ge(s("g_t"), i + 1)
                for c in range(0, n, 4):
                    m = min(4, n - c)
                    mark(dve.tensor_copy(COL[:, c:c + m, :, :].rearrange("p a b c -> p (a b c)"), PS[:, c // 4, 0:m * 3 * GR]))
                dve.tensor_copy(MPB[:, :, 0:n], PS[:, 2, 0:2 * MH * NC].rearrange("p (a b) -> p a b", b=NC)[:, :, 0:n]).then_inc(s("g_c"), 1)

            def scan(steps, i0, outs):
                for idx, (c, d) in enumerate(steps):
                    i, j = i0 + idx, idx
                    if outs:
                        dve.wait_ge(s("m_w"), i + 1)
                        if j >= 1:
                            dve.wait_ge(s("m_pt"), j)
                        dve.scalar_tensor_tensor(DD[:, j % 2, :].rearrange("p (a b) -> p a b", a=MH),
                                                 PS[:, 0, :].rearrange("p (a b) -> p a b", a=MH), -1.0,
                                                 over_mid(MASK[:, d, :], MH), ALU.mult, ALU.add).then_inc(s("m_arg"), 1)
                        dve.wait_ge(s("m_e"), j + 1)
                        dve.wait_ge(s("m_st"), j + 1)
                        if j >= 2:
                            dve.wait_ge(s("m_n"), j - 1)
                        dve.tensor_tensor(PP[:, j % 2, :], PS[:, 1, :], DD[:, j % 2, :], ALU.mult).then_inc(s("m_pt"), 1)
                        dve.wait_ge(s("m_n"), j + 1)
                        dn0, dn1 = dn[:, 0, :], dn[:, 1, :]
                        if j >= 1:
                            dve.wait_ge(s("m_h"), j)
                        mark(dve.tensor_copy(dn0, PS[:, 2:6, DV]))
                        settled()
                        mark(dve.scalar_tensor_tensor(dn1, dn0, -1.0, dn0, ALU.mult, ALU.max))
                        settled()
                        mark(dve.tensor_tensor(dn1, dn1, COL[:, c, 1, 32 * d:32 * d + 4], ALU.max))
                        settled()
                        mark(dve.reciprocal(dn0, dn1))
                        settled()
                        first = (d == 0) == (c < NC // 2)
                        for h in range(MH):
                            o = Q[:, c, DV * h:DV * h + DV]
                            if first:
                                ins = dve.tensor_scalar(o, PS[:, 2 + h, 0:DV], dn0[:, h:h + 1], None, ALU.mult)
                            else:
                                ins = dve.scalar_tensor_tensor(o, PS[:, 2 + h, 0:DV], dn0[:, h:h + 1], o, ALU.mult, ALU.add)
                            if h < MH - 1:
                                mark(ins)
                            else:
                                ins.then_inc(s("m_h"), 1)
                    dve.wait_ge(s("m_w"), i + 1)
                    if i == 0:
                        dve.wait_ge(s("c_zero"), 1)
                    else:
                        dve.wait_ge(s("m_cu"), 2 * i)
                    for pair in range(2):
                        dve.wait_ge(s("m_d"), 2 * i + pair + 1)
                        for h in (2 * pair, 2 * pair + 1):
                            cc = CC[:, d * MH + h, :]
                            last = h * P + (0 if d else P - 1)
                            ins = dve.scalar_tensor_tensor(cc, cc, WI[:, i % 2, last:last + 1], PS[:, 6 + h % 2, 0:V1],
                                                           ALU.mult, ALU.add)
                            if h % 2 == 0:
                                mark(ins)
                            else:
                                ins.then_inc(s("m_cu"), 1)

            gates(0, MEM, CTX_STEPS, FT["cg"] + 2)
            dve.wait_ge(s("rows2_in"), 32)
            mark(dve.tensor_scalar(krow, krow, DK ** -0.5, None, ALU.mult))
            settled()

            def keys(name, dst, tiles):
                for t in range(tiles):
                    n = TT[name] + t
                    dve.wait_ge(t_ready, n + 1)
                    dve.scalar_tensor_tensor(dst[:, t, :], PS[:, 4 + n % 4, :], DK ** -0.5, krow, ALU.mult, ALU.add).then_inc(t_free, 1)

            def values(name, dst, tiles):
                for j in range(2):
                    for t in range(tiles):
                        n = TT[name] + tiles * j + t
                        dve.wait_ge(t_ready, n + 1)
                        dve.tensor_tensor(dst[:, t, 2 * j:2 * j + 2, 0:DV], PS[:, 4 + n % 4, :].rearrange("p (a b) -> p a b", a=2),
                                          ROW[:, 2, BW * j:BW * j + BW].rearrange("p (a b) -> p a b", a=2), ALU.add).then_inc(t_free, 1)

            keys("ck", KX, 2)
            values("cv", VX, 2)
            gate_columns(2, 0)
            scan(CTX_STEPS, 0, False)
            dve.wait_ge(s("x_out"), 32)
            for t in range(NT):
                stats(t, XR[:, t, :], 2)
            mean_square(NT, RMS_EPS)
            rstd(NT, 7)
            for t in range(NT):
                dve.tensor_scalar(XR[:, t, :], XR[:, t, :], rs[:, t:t + 1], None, ALU.mult).then_inc(s("xr_norm"), 1)
            gates(1, T, X_STEPS, FT["mg"] + 4)
            keys("mk", KK, NT)
            dve.wait_ge(s("rows2_in"), 48)
            values("mv", VV, NT)
            gate_columns(NC, 1)
            scan(X_STEPS, 4, True)
            dve.wait_ge(s("m_h"), 16)
            for t in range(NT):
                for h in range(MH):
                    mark(dve.bn_stats(st[:, MH * t + h, :], Q[:, t, DV * h:DV * h + DV]))
            settled()
            for i in range(32):
                mark(dve.bn_aggr(mv[:, i, :], st[:, i, :]))
            mean_square(32, RMS_EPS)
            rstd(32, 8)
            for t in range(NT):
                for h in range(MH):
                    v = Q[:, t, DV * h:DV * h + DV]
                    mark(dve.tensor_scalar(v, v, rs[:, MH * t + h:MH * t + h + 1], None, ALU.mult))
            dve.wait_ge(rows2_v, 80)
            settled()
            for t in range(NT):
                mark(dve.tensor_tensor(Q[:, t, :], Q[:, t, :], ROW[:, 2, :], ALU.mult))
            for m in range(17):
                if m < 16:
                    n = TT["mo"] + m
                    dve.wait_ge(t_ready, n + 1)
                    if m >= 2:
                        dve.wait_ge(s("o_y"), m - 1)
                    dve.tensor_tensor(OG[:, m % 2, :], PS[:, 4 + n % 4, :], ROW[:, 0, BW * (m // 8):BW * (m // 8) + BW],
                                      ALU.add).then_inc(t_free, 1)
                if m >= 1:
                    j, t = (m - 1) // 8, (m - 1) % 8
                    dve.wait_ge(s("o_s"), m)
                    if m == 1:
                        settled()
                    v = Q[:, t, BW * j:BW * j + BW]
                    dve.tensor_tensor(v, v, OG[:, (m - 1) % 2, :], ALU.mult).then_inc(s("o_y"), 1)

            def copy_out(name):
                for j in range(2):
                    for t in range(NT):
                        n = TT[name] + 8 * j + t
                        dve.wait_ge(t_ready, n + 1)
                        dve.tensor_copy(Q[:, t, BW * j:BW * j + BW], PS[:, 4 + n % 4, :]).then_inc(t_free, 1)

            def branch_norm(r, rows_at, ready):
                dve.wait_ge(rows2_v, rows_at)
                mark(dve.tensor_tensor(ROW[:, 0, :], ROW[:, 0, :], ROW[:, 1, :], ALU.add))
                settled()
                dve.tensor_tensor(ROW[:, 0, :], ROW[:, 0, :], ROW[:, 2, :], ALU.mult).then_inc(s("gate_row"), 1)
                for t in range(NT):
                    dve.wait_ge(t_free, ready + t + 1)
                    stats(t, Q[:, t, :], 2)
                mean_square(NT, RMS_EPS)
                rstd(NT, r)
                for t in range(NT):
                    dve.tensor_scalar(Q[:, t, :], Q[:, t, :], rs[:, t:t + 1], None, ALU.mult).then_inc(s("b_norm"), 1)

            copy_out("mout")
            branch_norm(9, 128, TT["mout"] + 8)
            for t in range(NT):
                dve.wait_ge(s("x_new"), t + 1)
                stats(t, XR[:, t, :], 2)
            mean_square(NT, RMS_EPS)
            rstd(NT, 10)
            for t in range(NT):
                dve.tensor_scalar(XN[:, t, :], XR[:, t, :], rs[:, t:t + 1], None, ALU.mult).then_inc(s("xn_norm"), 1)

            def rows_of(v):
                return v.rearrange("p (a b) -> p a b", b=GRID)

            def group2(g, n_chunks):
                for c in range(n_chunks):
                    dve.wait_ge(f_free, g * 16 + (FT["up2"] + 4 * c + 4))
                    k = cw[:, c // 2, 4 * (c % 2):4 * (c % 2) + 4]
                    src, dst = rows_of(GG[:, c % 2, :]), rows_of(TC[:, c % 2, :])
                    dve.tensor_scalar(dst, src, k[:, 1:2], k[:, 3:4], ALU.mult, ALU.add).then_inc(s("taps"), 1)
                    dve.wait_ge(s("taps"), g * 8 + (2 * c + 1))
                    dve.scalar_tensor_tensor(dst[:, :, 1:], src[:, :, :-1], k[:, 0:1], dst[:, :, 1:], ALU.mult, ALU.add).then_inc(s("taps"), 1)
                    dve.wait_ge(s("taps"), g * 8 + (2 * c + 2))
                    dve.scalar_tensor_tensor(dst[:, :, :-1], src[:, :, 1:], k[:, 2:3], dst[:, :, :-1], ALU.mult, ALU.add).then_inc(s("conv"), 1)
                for m in range(16):
                    n = TT["down2"] + m
                    dve.wait_ge(t_ready, g * 16 + (n + 1))
                    v = Q[:, m % 8, BW * (m // 8):BW * (m // 8) + BW]
                    dve.tensor_tensor(v, v, PS[:, 4 + n % 4, :], ALU.add).then_inc(t_free, 1)

            dve.wait_ge(s("y_zero"), 1)
            with dve.Fori(0, N_G) as g:
                group2(g, 4)
            group2(N_G, 2)
            branch_norm(11, 176, TT["down2"] + 16 * N_G + 8)

        @block.gpsimd
        def _(pool):
            pool.memset(ident[:, :], 0.0).then_inc(s("pool_c"), 1)
            pool.wait_ge(s("pool_c"), 1)
            pool.affine_select(out=ident[:, :], in_=ident[:, :], compare_op=ALU.not_equal, fill=1.0, base=0,
                               pattern=[[-1, P]], channel_multiplier=1).then_inc(s("ident_ok"), 1)
            pool.memset(relb[0:NB + 1, :], 1.0).then_inc(s("relb_one"), 1)

            def offset(i):
                pool.wait_ge(rows_in, 32 + 48 * i)
                for t in range(NT):
                    pool.wait_ge(s("ln_half"), NT * i + t + 1)
                    pool.tensor_tensor(XR[:, t, :], XR[:, t, :], ROW[:, 1, :], ALU.add).then_inc(s("ln_done"), 1)
            offset(0)
            for n in range(2, NT):
                pool.wait_ge(s("ix_s"), NH * (n - 1))
                v = score[:, n * P:n * P + P]
                pool.affine_select(out=v, in_=v, compare_op=ALU.is_ge, fill=NEG, base=0,
                                   pattern=[[-1, P]], channel_multiplier=1).then_inc(s("ix_c"), 1)
            offset(1)
            offset(2)
            pool.wait_ge(s("x_oe"), NT)
            for i in range(2):
                pool.memset(RU[:, i, :], 0.0).then_inc(s("squared"), 1)
            with pool.Fori(0, N_UP) as g:
                for m in range(16):
                    pool.wait_ge(f_free, g * 16 + (FT["up"] + m + 1))
                    pool.tensor_tensor(Q[:, m // 2, BW * (m % 2):BW * (m % 2) + BW], RU[:, m % 2, :], RU[:, m % 2, :],
                                       ALU.mult).then_inc(s("squared"), 1)
            offset(3)
            pool.wait_ge(s("ln_done"), 4 * NT)
            pool.memset(GW, 0.0).then_inc(s("gw_zero"), 1)
            pool.memset(gb[0:GR, :], 0.0).then_inc(s("gw_zero"), 1)
            pool.memset(SEL[0:GR, :, :], 0.0).then_inc(s("pool_c"), 1)
            pool.memset(MASK, 0.0).then_inc(s("pool_c"), 1)
            pool.wait_ge(s("pool_c"), 3)
            pool.affine_select(out=SEL[0:GR, :, :], in_=SEL[0:GR, :, :], compare_op=ALU.not_equal, fill=1.0, base=0,
                               pattern=[[-32, 2], [-1, MH], [0, P]], channel_multiplier=1).then_inc(s("pool_c"), 1)
            pool.affine_select(out=MASK[:, 0, :], in_=MASK[:, 0, :], compare_op=ALU.is_ge, fill=NEG, base=0,
                               pattern=[[1, P]], channel_multiplier=-1).then_inc(s("pool_c"), 1)
            pool.affine_select(out=MASK[:, 1, :], in_=MASK[:, 1, :], compare_op=ALU.is_ge, fill=NEG, base=0,
                               pattern=[[-1, P]], channel_multiplier=1).then_inc(s("pool_c"), 1)
            pool.memset(CC, 0.0).then_inc(s("c_zero"), 1)
            pool.memset(VX[:, :, :, DV:V1], 1.0).then_inc(s("v_one"), 1)

            def scan(steps, i0, outs, K):
                for idx, (c, d) in enumerate(steps):
                    i, j = i0 + idx, idx
                    if i >= 2:
                        pool.wait_ge(s("m_d"), 2 * i - 2)
                    pool.tensor_tensor(KS[:, i % 2, :].rearrange("p (a b) -> p a b", a=MH), K[:, c, :].rearrange("p (a b) -> p a b", a=MH),
                                       over_last(COL[:, c, 2, 32 * d:32 * d + 4], DK), ALU.mult).then_inc(s("m_ks"), 1)
                    if outs:
                        pool.wait_ge(s("m_w"), i + 1)
                        if j >= 2:
                            pool.wait_ge(s("m_n"), j - 1)
                        pool.tensor_tensor(QS[:, j % 2, :].rearrange("p (a b) -> p a b", a=MH), qT[:, :, c * P:c * P + P],
                                           WI[:, i % 2, :].rearrange("p (a b) -> p a b", a=MH), ALU.mult).then_inc(s("m_qs"), 1)

            pool.wait_ge(s("g_c"), 1)
            pool.wait_ge(t_free, TT["mk"])
            scan(CTX_STEPS, 0, False, KX)
            pool.wait_ge(s("m_d"), 8)
            pool.wait_ge(f_ready, FT["mg"] + 4)
            pool.memset(VV[:, :, :, DV:V1], 1.0).then_inc(s("v_one"), 1)
            pool.wait_ge(s("g_c"), 2)
            pool.wait_ge(t_free, TT["mo"])
            scan(X_STEPS, 4, True, KK)

            def add_branch(i):
                pool.wait_ge(s("gate_row"), i + 1)
                for t in range(NT):
                    pool.wait_ge(s("b_norm"), NT * i + t + 1)
                    pool.tensor_tensor(Q[:, t, :], Q[:, t, :], ROW[:, 0, :], ALU.mult).then_inc(s("b_gain"), 1)
                    pool.wait_ge(s("b_gain"), NT * i + t + 1)
                    pool.tensor_tensor(XR[:, t, :], XR[:, t, :], Q[:, t, :], ALU.add).then_inc(s("x_new"), 1)

            pool.wait_ge(s("x_back"), 32)
            add_branch(0)
            for i in range(2):
                pool.memset(R[:, 14400 + i:14401 + i], 0.0).then_inc(s("hidden"), 1)
            pool.wait_ge(s("x_new"), NT)
            pool.memset(Q[:, :, :], 0.0).then_inc(s("y_zero"), 1)

            def gate2(g, n_chunks):
                for c in range(n_chunks):
                    pool.wait_ge(s("silu"), g * 4 + (c + 1))
                    pool.tensor_tensor(HH[:, c, :], TC[:, c % 2, :], UU[:, c % 2, :], ALU.mult).then_inc(s("hidden"), 1)

            with pool.Fori(0, N_G) as g:
                gate2(g, 4)
            gate2(N_G, 2)
            add_branch(1)


def host_layout(inputs):
    a = {k: np.ascontiguousarray(v) for k, v in inputs.items() if np.asarray(v).size}

    def col(v):
        return v.reshape(-1, P).T

    b_in, ada_b = a["b_in"][0], a["ada_b_2"][0]
    parts = {"qa": col(b_in[0:512]), "qb": col(b_in[768:1280]), "iq": col(b_in[1408:1920]), "ka": col(b_in[512:640]),
             "xq": col(a["xa_bq"][0]), "xk": col(a["xa_bkv"][0, :D]), "mq": col(a["m_in_b_2"][0, :512]),
             "pre_mix": col(a["pre_mix_g_2"][0]), "pre_ffn": col(a["pre_ffn_g_2"][0]),
             "sh1": col(ada_b[0:D]), "sc1": col(ada_b[D:2 * D]), "sh2": col(ada_b[3 * D:4 * D]), "sc2": col(ada_b[4 * D:5 * D]),
             "c": np.stack([col(a["c_2"][0]), col(a["c_ctx_2"])], -1).reshape(P, 16)}
    a["cols_h"] = np.ascontiguousarray(np.concatenate([parts[k] for k in COLS], 1))
    dist = 2 * P - 1 - np.arange(N_BIAS)
    near = np.maximum(dist, 0)
    exact = NB // 2
    far = exact + (np.log(np.maximum(near, 1) / exact) / np.log(MAXD / exact) * (NB - exact) + 1e-6).astype(np.int64)
    bucket = np.where(near < exact, near, np.minimum(far, NB - 1))
    hot = np.zeros((NB + 1, 2, N_BIAS), np.float32)
    hot[bucket, :, np.arange(N_BIAS)] = 1.0
    hot[NB, 0] = np.where((dist < 0) | (dist >= P), NEG, 0.0)
    hot[NB, 1] = np.where(dist < 0, NEG, 0.0)
    a["hot_h"] = hot
    a["bup_h"] = np.ascontiguousarray(a["b_up"][0].reshape(8, 4, P).transpose(0, 2, 1))
    conv = np.concatenate([a["ffn_conv_w_2"][0], a["ffn_conv_b_2"]], 0)
    a["conv_h"] = np.ascontiguousarray(conv.reshape(4, -1, 2, P).transpose(1, 3, 2, 0).reshape(-1, P, 8))
    return a


def kernel(**inputs):
    import concourse.bacc as bacc
    from concourse.bass_utils import run_bass_kernel_spmd

    arrays = host_layout(inputs)
    nc = bacc.Bacc("TRN2", target_bir_lowering=False, num_devices=1)
    aps = {n: nc.dram_tensor(f"in_{n}_dram", v.shape, mybir.dt.from_np(v.dtype), kind="ExternalInput").ap()
           for n, v in arrays.items()}
    out = nc.dram_tensor("out_dram", (1, T, D), F32, kind="ExternalOutput").ap()
    build_program(nc, aps, out)
    r = run_bass_kernel_spmd(nc, [{f"in_{n}_dram": v for n, v in arrays.items()}], core_ids=[0])
    return r.results[0]["out_dram"]
```

```python
from contextlib import ExitStack

import numpy as np

import concourse.bass as bass
from concourse import mybir

F32 = mybir.dt.float32
F32R = mybir.dt.float32r
ALU = mybir.AluOpType
ACT = mybir.ActivationFunctionType
AX = mybir.AxisListType

P = 128
D = 1024
T = 1024
NT = T // P
KC = D // P
MEM = 256
DH = 64
NH = 8
RANK = 128
TOPK = 256
XH, XD = 4, 256
FF = 4096
FF2 = 2816
GRID = 64
MH, DK, DV = 4, 128, 256
NB = 32
MAXD = 128
NEG = -1.0e30
TAKEN = -3.0e38
ALPHA = 2.0 ** 0.25
LN_EPS, RMS_EPS = 1e-5, 1e-6
BW = 512
N_BIAS = 3 * P
ADA_W = 256
ADA_N = 6 * D // NT
MISC = 2 * P + DH + NH

COLS = {}
_at = 0
for _name, _n in (("qa", 4), ("qb", 4), ("iq", 4), ("ka", 1), ("xq", 8), ("xk", 8), ("mq", 4),
                  ("pre_mix", 8), ("pre_ffn", 8), ("sh1", 8), ("sc1", 8), ("sh2", 8), ("sc2", 8),
                  ("c", 16)):
    COLS[_name] = (_at, _at + _n)
    _at += _n
N_COLS = _at


def bases(*stages):
    at, out = 0, {}
    for name, n in stages:
        out[name] = at
        at += n
    out["end"] = at
    return out


FT = bases(("vb", 2), ("xt0", 16), ("qa", 8), ("qb", 8), ("iq", 8), ("ka", 2), ("ukT", 1),
           ("ckT", 4), ("memT", 4), ("xk", 8), ("xt1", 16), ("xq", 16), ("xt2", 16),
           ("up", 64), ("ctxT", 4), ("cg", 2), ("xtm", 16), ("mg", 4), ("mq", 8), ("kT", 8),
           ("yT", 16), ("xtf", 16), ("up2", 88))
TT = bases(("misc", 8), ("wo", 16), ("xv", 4), ("xo", 16), ("down", 128), ("ck", 2), ("cv", 4),
           ("mk", 8), ("mv", 16), ("mo", 16), ("mout", 16), ("down2", 96))


def build_program(nc, I, out):
    with ExitStack() as ctx:
        def sb(name, shape, dt=F32):
            return ctx.enter_context(nc.sbuf_tensor(name, shape, dt))

        def sb_twice(name, shape):
            at = (nc.sbuf_base + 31) // 32 * 32
            t = sb(name, shape)
            assert nc.sbuf_base == at + 4 * int(np.prod(shape[1:]))
            return t, nc.alloc_sbuf_tensor_at(name + "_parts", shape, F32R, offset=at)

        def sem(name):
            return ctx.enter_context(nc.semaphore(name))

        mods_d = nc.dram_tensor("mods_scratch", (2, 6 * D), F32, kind="Internal").ap()
        bias_d = nc.dram_tensor("bias_scratch", (2 * NH, P, N_BIAS), F32, kind="Internal").ap()
        x_d = nc.dram_tensor("x_scratch", (P, NT * D), F32, kind="Internal").ap()

        XR, XR_r = sb_twice("x_rows", [P, NT, D])
        XT, XT_r = sb_twice("x_cols", [P, KC, T])
        WB, WB_r = zip(*[sb_twice(f"weights{i}", [P, KC, BW]) for i in range(2)])
        Q, Q_r = sb_twice("wide", [P, 8, T])
        ROW = sb("rows", [P, 3, D])
        R, R_r = sb_twice("region", [P, 15936])
        ident = sb("ident", [P, P])
        cols = sb("cols", [P, N_COLS])
        modc = sb("modc", [P, 6, KC])
        st = sb("stats", [P, 32, 6])
        mv = sb("mean_var", [P, 32, 2])
        ve = sb("var_eps", [P, 32])
        sdv = sb("std", [P, 32])
        rs = sb("rstd", [P, 32])
        PS = ctx.enter_context(nc.psum_tensor("psum", [P, 8, BW], F32))
        PSf = PS[:, :, :].rearrange("p a b -> p (a b)")

        def view(base, at, shape):
            n = int(np.prod(shape))
            v = base[:, at:at + n]
            if len(shape) == 1:
                return v
            if len(shape) == 2:
                return v.rearrange("p (a b) -> p a b", a=shape[0])
            return v.rearrange("p (a b c) -> p a b c", a=shape[0], b=shape[1])

        def over_last(v, n):
            return v.unsqueeze(2).to_broadcast([v.shape[0], v.shape[1], n])

        def over_mid(v, n):
            return v.unsqueeze(1).to_broadcast([v.shape[0], n, v.shape[1]])

        XTf = XT[:, :, :].rearrange("p a b -> p (a b)")
        XRf = XR[:, :, :].rearrange("p a b -> p (a b)")
        Qf = Q[:, :, :].rearrange("p a b -> p (a b)")
        ROWf = ROW[:, :, :].rearrange("p a b -> p (a b)")
        stf = st[:, :, :].rearrange("p a b -> p (a b)")

        iqT = view(R, 0, (4, T))
        kaT = view(R, 4096, (2, T))
        ikT = view(R, 6144, (T,))
        cT = view(R, 7168, (T,))
        cR = view(R, 8192, (NT, RANK))
        misc = view(R, 9216, (NT, MISC))
        SB = view(R, 11840, (NH, 2 * P))
        LG = view(R, 11840, (2, T))
        PT = view(R, 13888, (16, P))
        RL = view(R, 13888, (2, T))
        bias = view(XTf, 0, (16, 2 * P))
        OL = view(XTf, 4096, (NH, P))
        score = view(XTf, 5120, (T,))
        work = view(XTf, 6144, (T,))
        QL = view(XTf, 7168, (NH, P))
        WB1f = WB[1][:, :, :].rearrange("p a b -> p (a b)")
        WB0f = WB[0][:, :, :].rearrange("p a b -> p (a b)")
        msk = view(WB1f, 0, (2, T))
        modr = view(WB1f, 2 * T, (2, ADA_N))
        adaw = view(WB0f, 0, (2, KC, ADA_W))
        wuk = view(ROWf, 0, (NH, DH))
        wukT = view(ROWf, 512, (4, P))
        wuv = view(ROWf, 1024, (NH, DH))
        mrow = view(ROWf, 1536, (MISC,))
        kvg = view(ROWf, 1864, (RANK,))
        ikg = view(ROWf, 1992, (2, DH))
        far = view(ROWf, 2120, (NH,))
        sink = view(ROWf, 2128, (NH,))
        mx = view(ROWf, 2136, (NH,))
        nm = view(ROWf, 2144, (NH,))
        den = view(ROWf, 2152, (NH,))
        sd = view(ROWf, 2160, (NH,))
        es = view(ROWf, 2168, (NH,))
        top = view(ROWf, 2176, (8,))
        iwt = view(ROWf, 2184, (NT, NH))
        hot = view(R, 15024, (2, N_BIAS))
        cx = sb("cond", [P, KC, 2])
        relb = view(R, 11840, (2 * NH,))
        vb = view(R, 11904, (2, N_BIAS))
        ikn = view(R, 12700, (NT, 2 * DH))
        kaS = view(R, 14000, (2, BW))

        memR = view(R, 0, (2, D))
        memT = view(R, 2048, (KC, MEM))
        xkT = view(R, 4096, (KC, MEM))
        xv = view(R, 6144, (2, D))
        XP = view(R, 8192, (2, XH * MEM))
        XPT = view(R, 10240, (2, 8 * P))
        vrow = view(R, 13312, (D,))
        upb = view(R, 14336, (2, 2))
        WBr_f = [w[:, :, :].rearrange("p a b -> p (a b)") for w in WB_r]
        WRAW = [view(w, 0, (4 * BW,)) for w in (WB0f, WB1f)]
        WLO = [view(w, 0, (4 * BW,)) for w in WBr_f]
        WHI = [view(w, 4 * BW, (4 * BW,)) for w in WBr_f]
        X_HI = XT_r
        X_LO1 = Q_r
        X_LO2 = XR_r
        H_HI = view(R_r, 0, (4, T))
        H_LO = view(R_r, 4096, (4, T))
        RU = view(R, 8192, (4, BW))

        xm = view(R, 14344, (2, XH))
        xn = view(R, 14352, (2, XH))
        xd = view(R, 14360, (2, XH))

        NC = NT
        V1 = DV + 1
        GR = 36
        ctxR = view(R, 0, (2, D))
        hcT = view(R, 2048, (KC, MEM))
        KX = view(R, 4096, (2, MH * DK))
        VX = view(R, 5120, (2, MH, V1))
        GW = view(R, 7232, (KC, 2, GR))
        VV = view(R, 0, (NC, MH, V1))
        KK = view(R, 8224, (NC, MH * DK))
        CC = view(R, 12320, (2 * MH, V1))
        COL = view(R, 14376, (NC, 3, GR))
        MPB = view(R, 15240, (2 * MH, NC))
        MASK = view(R, 15304, (2, P))
        gb = view(R, 15560, (2,))
        ms = view(R, 15562, (1,))
        mpc = view(R, 15563, (NC,))
        dn = view(R, 15571, (2, MH))
        li, lf, bb, uu, tmp, enm, wsr = [view(Qf, i * T, (T,)) for i in range(7)]
        ones = view(Qf, 7 * T, (P,))
        krow = view(Qf, 7 * T + BW, (BW,))
        MM = ROW[:, 0, :]
        SEL = view(ROWf, T, (2 * MH, P))
        KS = view(ROWf, 2 * T, (2, BW))
        DD = view(WB0f, 0, (2, BW))
        PP = view(WB0f, 1024, (2, BW))
        WI = view(WB0f, 2048, (2, BW))
        QS = view(WB0f, 3072, (2, BW))
        qT = view(XRf, 0, (MH, T))
        kT = view(XRf, 4 * T, (MH, T))
        OG = view(ROWf, T, (2, BW))

        XN = view(R, 0, (NT, D))
        UU = view(R, 8192, (2, T))
        GG = view(R, 10240, (2, T))
        TC = view(R, 12288, (2, T))
        cw = view(R, 14336, (4, 4))
        XS = view(R, 12288, (4, BW))

        S = {}

        def s(name):
            if name not in S:
                S[name] = sem(name)
            return S[name]

        f_ready, f_free, t_ready, t_free = s("f_ready"), s("f_free"), s("t_ready"), s("t_free")
        w_in = [s("w_in0"), s("w_in1")]
        rows_in, x_in, cols_in, own_dve, own_act = s("rows_in"), s("x_in"), s("cols_in"), s("own_dve"), s("own_act")

        def cols_of(w, a, b):
            return w[:, a:b].rearrange("(k p) n -> p k n", p=P)

        w_in_w = I["w_in"][0]
        blocks = []

        def block_of(pieces, done_sem, done_at):
            blocks.append((pieces, done_sem, done_at))

        for name, a in (("qa", 0), ("qb", 768), ("iq", 1408)):
            block_of([(0, BW, cols_of(w_in_w, a, a + BW))], f_ready, FT[name] + 8)
        block_of([(0, 256, cols_of(w_in_w, 512, 768)), (256, 384, cols_of(w_in_w, 1280, 1408)),
                  (384, 456, cols_of(w_in_w, 1920, 1992))], t_ready, TT["misc"] + 8)
        WO0 = len(blocks)
        for j in range(2):
            block_of([(0, BW, cols_of(I["w_o"][0], BW * j, BW * j + BW))], t_ready, TT["wo"] + 8 * j + 8)

        for name, w, a0, n, ds_, tiles in (("xk", "xa_wkv", 0, 2, f_ready, 4), ("xv", "xa_wkv", D, 2, t_ready, 2),
                                           ("xq", "xa_wq", 0, 2, f_ready, 8), ("xo", "xa_wo", 0, 2, t_ready, 8)):
            for j in range(n):
                block_of([(0, BW, cols_of(I[w][0], a0 + BW * j, a0 + BW * j + BW))], ds_,
                         (FT if ds_ is f_ready else TT)[name] + tiles * (j + 1))
        UP0 = len(blocks)
        N_UP = FF // BW
        for g in range(N_UP):
            for j in range(2):
                block_of([None, None], f_ready, FT["up"] + 8 * g + 4 * j + 4)
            for j in range(2):
                block_of([None], t_ready, TT["down"] + 16 * g + 8 * j + 8)
        assert UP0 % 2 == 0
        M0 = len(blocks)
        m_w = I["m_in_w_2"][0]
        for name, a0, n, ds_, tiles in (("ck", 512, 1, t_ready, 2), ("cv", 1024, 2, t_ready, 2), ("mq", 0, 1, f_ready, 8),
                                        ("mk", 512, 1, t_ready, 8), ("mv", 1024, 2, t_ready, 8), ("mo", 2048, 2, t_ready, 8)):
            for j in range(n):
                block_of([(0, BW, cols_of(m_w, a0 + BW * j, a0 + BW * j + BW))], ds_,
                         (FT if ds_ is f_ready else TT)[name] + tiles * (j + 1))
        for j in range(2):
            block_of([(0, BW, cols_of(I["m_out_w_2"][0], BW * j, BW * j + BW))], t_ready, TT["mout"] + 8 * j + 8)
        G0 = len(blocks)
        assert G0 % 2 == 1
        N_G = FF2 // BW
        for g in range(N_G):
            for n in (3, 3, 3, 3, 1, 1):
                block_of([None] * n, f_ready, 0)
        for n in (3, 3, 1, 1):
            block_of([None] * n, f_ready, 0)

        def loaded(b):
            return 16 * sum(len(p) for i, (p, _, _) in enumerate(blocks[:b + 1]) if i % 2 == b % 2)

        CTX_STEPS = [(c if d == 0 else 1 - c, d) for c in range(2) for d in range(2)]
        X_STEPS = [(c if d == 0 else NC - 1 - c, d) for c in range(NC) for d in range(2)]

        block = ctx.enter_context(nc.Block())

        @block.sync
        def _(sp):
            for h in range(2):
                sp.dma_start(XR[:, 4 * h:4 * h + 4, :],
                             I["x"][0, 512 * h:512 * h + 512, :].rearrange("(t p) d -> p t d", p=P)).then_inc(x_in, 16)

            def load(b):
                if b >= 2:
                    sp.wait_ge(blocks[b - 2][1], blocks[b - 2][2])
                for a, z, src in blocks[b][0]:
                    sp.dma_start(WB[b % 2][:, :, a:z], src).then_inc(w_in[b % 2], 16)

            for b in range(WO0):
                load(b)
            sp.wait_ge(f_ready, FT["iq"] + 8)
            for n in range(NT):
                for j in range(ADA_N // ADA_W * n, ADA_N // ADA_W * (n + 1)):
                    if j >= 2:
                        sp.wait_ge(s("ada_mm"), j - 1)
                    sp.dma_start(adaw[:, j % 2], cols_of(I["ada_w_2"][0], ADA_W * j, ADA_W * j + ADA_W)).then_inc(s(f"ada_in{j % 2}"), 16)
                if n > 0:
                    sp.wait_ge(s("ada_e"), n)
                    sp.dma_start(mods_d[:, ADA_N * (n - 1):ADA_N * n], modr[0:2, (n - 1) % 2, :]).then_inc(s(f"mods_out{(n - 1) % 2}"), 16)
            sp.wait_ge(s("ada_e"), NT)
            sp.dma_start(mods_d[:, ADA_N * (NT - 1):6 * D], modr[0:2, (NT - 1) % 2, :]).then_inc(s(f"mods_out{(NT - 1) % 2}"), 16)
            load(WO0)
            for j in range(2):
                sp.wait_ge(s(f"mods_out{j}"), 64)
            for i, (row, part) in enumerate(((0, 0), (0, 1), (0, 3), (0, 4), (1, 0), (1, 1))):
                sp.dma_start(modc[:, i, :], mods_d[row, D * part:D * part + D].rearrange("(k p) -> p k", p=P),
                             allow_slow_non_contiguous=True).then_inc(s("modc_in"), 16)
            sp.wait_ge(s("d_fe"), NT)
            load(WO0 + 1)
            sp.dma_start(memR, I["mem"][0].rearrange("(t p) d -> p t d", p=P)).then_inc(s("mem_in"), 16)
            sp.dma_start(vrow, I["xa_bkv"][0, D:2 * D].partition_broadcast(P)).then_inc(s("mem_in"), 16)
            for b in range(WO0 + 2, UP0):
                load(b)
            with sp.Fori(0, N_UP) as g:
                for j in range(2):
                    sp.wait_ge(t_ready, g * 16 + (TT["down"] - 8 + 8 * j))
                    sp.dma_start(WRAW[j].rearrange("p (k n) -> p k n", k=KC), I["w_up"][0][:, bass.ds(g * BW + 256 * j, 256)]
                                 .rearrange("(k p) n -> p k n", p=P)).then_inc(w_in[j], 16)
                    sp.dma_start(upb[:, j, :], I["bup_h"][bass.ds(g * 2 + j, 1)]
                                 .rearrange("a p c -> p (a c)")).then_inc(w_in[j], 16)
                for j in range(2):
                    sp.wait_ge(f_ready, g * 8 + (FT["up"] + 4 + 4 * j))
                    sp.dma_start(WRAW[j].rearrange("p (k n) -> p k n", k=4), I["w_down"][0][bass.ds(g * BW, BW), BW * j:BW * j + BW]
                                 .rearrange("(k p) n -> p k n", p=P)).then_inc(w_in[j], 16)
            sp.wait_ge(s("ln_done"), 4 * NT)
            for h in range(2):
                sp.dma_start(x_d[:, 4 * D * h:4 * D * h + 4 * D], XRf[:, 4 * D * h:4 * D * h + 4 * D]).then_inc(s("x_out"), 16)
            sp.dma_start(ctxR, I["ctx_2"][0].rearrange("(t p) d -> p t d", p=P)).then_inc(s("ctx_in"), 16)
            sp.wait_ge(s("gw_zero"), 2)
            for gi in range(2):
                for d in range(2):
                    a = 3072 + 8 * d + 4 * gi
                    sp.dma_start(GW[:, :, gi, 32 * d:32 * d + 4], cols_of(m_w, a, a + 4)).then_inc(s("gw_in"), 16)
                    sp.dma_start(gb[32 * d:32 * d + 4, gi:gi + 1], I["m_in_b_2"][0, a:a + 4].rearrange("(p c) -> p c", c=1)).then_inc(s("gw_in"), 16)
            for b in range(M0, M0 + 4):
                load(b)
            sp.wait_ge(s("m_cu"), 8)
            for b in range(M0 + 4, M0 + 8):
                load(b)
            sp.wait_ge(s("m_cu"), 40)
            sp.wait_ge(s("m_h"), 16)
            load(M0 + 8)
            for h in range(2):
                sp.dma_start(XRf[:, 4 * D * h:4 * D * h + 4 * D], x_d[:, 4 * D * h:4 * D * h + 4 * D]).then_inc(s("x_back"), 16)
            load(M0 + 9)
            load(M0 + 10)
            w_u, w_d = I["ffn_up_w_2"][0], I["ffn_down_w_2"][0]

            for t in range(NT):
                sp.wait_ge(s("x_new"), t + 1)
                sp.dma_start(x_d[:, D * t:D * t + D], XR[:, t, :]).then_inc(s("x_out2"), 16)

            def load_up(g, c):
                buf = 1 - c % 2
                for half in range(2):
                    sp.dma_start(WRAW[buf].rearrange("p (k n) -> p k n", k=KC)[:, :, P * half:P * half + P],
                                 w_u[:, bass.ds(g * BW + (P * c + FF2 * half), P)].rearrange("(k p) n -> p k n", p=P)).then_inc(w_in[buf], 16)
                sp.dma_start(cw[:, c, :], I["conv_h"][bass.ds(g * 4 + c, 1)].rearrange("a p c -> p (a c)")).then_inc(w_in[buf], 16)

            with sp.Fori(0, N_G) as g:
                for c in range(4):
                    if c < 2:
                        sp.wait_ge(t_ready, g * 16 + (TT["down2"] - 8 + 8 * c))
                    else:
                        sp.wait_ge(f_ready, g * 16 + (FT["up2"] + 4 * c - 4))
                    load_up(g, c)
                for j in range(2):
                    sp.wait_ge(f_ready, g * 16 + (FT["up2"] + 12 + 4 * j))
                    sp.dma_start(WRAW[1 - j].rearrange("p (k n) -> p k n", k=4), w_d[bass.ds(g * BW, BW), BW * j:BW * j + BW]
                                 .rearrange("(k p) n -> p k n", p=P)).then_inc(w_in[1 - j], 16)
            for c in range(2):
                sp.wait_ge(t_ready, TT["down2"] + 16 * N_G - 8 + 8 * c)
                load_up(N_G, c)
            for j in range(2):
                sp.wait_ge(f_ready, FT["up2"] + 16 * N_G + 4 + 4 * j)
                sp.dma_start(WRAW[1 - j][:, 0:2 * BW].rearrange("p (k n) -> p k n", k=2), w_d[N_G * BW:FF2, BW * j:BW * j + BW]
                             .rearrange("(k p) n -> p k n", p=P)).then_inc(w_in[1 - j], 16)
            for h in range(2):
                sp.dma_start(XRf[:, 4 * D * h:4 * D * h + 4 * D], x_d[:, 4 * D * h:4 * D * h + 4 * D]).then_inc(s("x_back2"), 16)
            for t in range(NT):
                sp.wait_ge(s("x_new"), NT + t + 1)
                sp.dma_start(out[0, t * P:t * P + P, :], XR[:, t, :]).then_inc(s("out_done"), 16)
            sp.wait_ge(s("out_done"), 16 * NT)

        @block.tensor
        def _(pe):
            def bank(n):
                if n >= 4:
                    pe.wait_ge(f_free, n - 3)
                return PS[:, n % 4, :]

            def bank_t(n):
                if n >= 4:
                    pe.wait_ge(t_free, n - 3)
                return PS[:, 4 + n % 4, :]

            def transposes(name, src, ready, ready_at):
                for h in range(2):
                    pe.wait_ge(ready, ready_at(h))
                    for k in range(KC):
                        n = FT[name] + 8 * h + k
                        o = bank(n)
                        for j in range(4):
                            m = pe.transpose(o[:, j * P:j * P + P], src[:, 4 * h + j, k * P:k * P + P], ident[:, :])
                        m.then_inc(f_ready, 1)

            def gemm_f(name, n0, w, chunks, x=XT, halves=2, width=BW):
                n = n0
                for f in chunks:
                    for h in range(halves):
                        o = bank(n)
                        for k in range(KC):
                            m = pe.matmul(o[:, 0:width], lhsT=w[:, k, f * P:f * P + P], rhs=x[:, k, h * width:h * width + width],
                                          start=(k == 0), stop=(k == KC - 1))
                        m.then_inc(f_ready, 1)
                        n += 1

            def gemm_t(n0, w, x=XT, tiles=NT, a=0, z=BW, kc=KC):
                for t in range(tiles):
                    o = bank_t(n0 + t)
                    for k in range(kc):
                        m = pe.matmul(o[:, 0:z - a], lhsT=x[:, k, t * P:t * P + P], rhs=w[:, k, a:z],
                                      start=(k == 0), stop=(k == kc - 1))
                    m.then_inc(t_ready, 1)

            def weights(b):
                pe.wait_ge(w_in[b % 2], loaded(b))
                return WB[b % 2]

            pe.wait_ge(s("relb_in"), 32)
            for g in range(2):
                o = bank(FT["vb"] + g)
                pe.matmul(o[0:NH, 0:N_BIAS], lhsT=relb[0:NB + 1, g * NH:g * NH + NH], rhs=hot[0:NB + 1, g, :],
                          start=True, stop=True).then_inc(f_ready, 1)
            pe.wait_ge(s("ident_ok"), 1)
            transposes("xt0", XR, s("ln_done"), lambda h: 4 * h + 4)
            pe.wait_ge(f_free, FT["qa"])
            for b, name in enumerate(("qa", "qb", "iq")):
                gemm_f(name, FT[name], weights(b), range(4))
            gemm_f("ka", FT["ka"], weights(3), range(1))
            gemm_t(TT["misc"], weights(3), a=P, z=P + MISC)
            pe.wait_ge(s("wuk_in"), 16)
            o = bank(FT["ukT"])
            for c in range(4):
                m = pe.transpose(o[:, c * P:c * P + P], wuk[:, 2 * c:2 * c + 2, :].rearrange("p a b -> p (a b)"), ident[:, :])
            m.then_inc(f_ready, 1)
            pe.wait_ge(s("ck_ready"), 2)
            for i, src in ((0, cR), (2, ikn)):
                for h in range(2):
                    o = bank(FT["ckT"] + i + h)
                    for j in range(4):
                        m = pe.transpose(o[:, j * P:j * P + P], src[:, 4 * h + j, :], ident[:, :])
                    m.then_inc(f_ready, 1)
            pe.wait_ge(f_free, FT["memT"])
            pe.wait_ge(t_free, TT["wo"])
            pe.wait_ge(s("attn_in"), 16 * 7)
            for n in range(NT):
                lo = 0 if n == 0 else n - 1
                q = slice(n * P, n * P + P)
                keys = slice(lo * P, n * P + P)
                width = (n + 1 - lo) * P
                if n > 0:
                    pe.wait_ge(s("d_fe"), n)
                for c in range(4):
                    for r in range(2):
                        hp = slice(DH * r, DH * r + DH)
                        m = pe.matmul(PS[:, 2 * r + c // 2, (c % 2) * 256 + 256 - width:(c % 2) * 256 + 256], lhsT=Q[hp, c, q],
                                      rhs=kaT[hp, c // 2, keys], start=True, stop=True)
                        if c % 2 == 1:
                            m.then_inc(s("a_s"), 1)
                if n == 0:
                    pe.wait_ge(s("cx_ready"), 1)
                for j in range(ADA_N // ADA_W * n, ADA_N // ADA_W * (n + 1)):
                    pe.wait_ge(s(f"ada_in{j % 2}"), 16 * (j // 2 + 1))
                    at = 5 * BW + ADA_W * (j % (ADA_N // ADA_W))
                    for k in range(KC):
                        m = pe.matmul(PSf[0:2, at:at + ADA_W], lhsT=cx[:, k, :], rhs=adaw[:, j % 2, k, :], start=(k == 0), stop=(k == KC - 1))
                    m.then_inc(s("ada_mm"), 1)
                pe.wait_ge(s("a_r"), n + 1)
                for b in range(4):
                    pe.wait_ge(s("a_sb"), 4 * n + 4)
                    for j in range(4):
                        h, kt = (4 * b + j) // 2, (4 * b + j) % 2
                        if n == 0 and kt == 0:
                            continue
                        m = pe.transpose(PS[:, b, j * P:j * P + P], SB[:, h, kt * P:kt * P + P], ident[:, :])
                    m.then_inc(s("a_t"), 1)
                pe.wait_ge(s("a_te"), 4 * n + 4)
                for h in range(NH):
                    kts = (1,) if n == 0 else (0, 1)
                    for kt in kts:
                        m = pe.matmul(PS[DH * (h % 2):DH * (h % 2) + DH, 4, (h // 2) * P:(h // 2) * P + P],
                                      lhsT=misc[:, lo + kt - (n == 0), DH * (h // 4):DH * (h // 4) + DH],
                                      rhs=PT[:, 2 * h + kt, :], start=(kt == kts[0]), stop=(kt == 1))
                m.then_inc(s("a_o"), 1)
                L = (n + 1) * P
                pe.wait_ge(s("ada_e"), n + 1)
                if 1 <= n < NT - 1:
                    q1, L1 = slice((n + 1) * P, (n + 2) * P), (n + 2) * P
                    pe.wait_ge(s("a_oe"), n + 1)
                    for h in range(NH):
                        i = NH * (n - 1) + h
                        if h >= 4:
                            pe.wait_ge(s("ix_r"), i - 3)
                        hp = slice(DH * (h % 2), DH * (h % 2) + DH)
                        for a in range(0, L1, BW):
                            z = min(L1, a + BW)
                            m = pe.matmul(PS[:, 2 * (h % 4) + a // BW, 0:z - a], lhsT=iqT[hp, h // 2, q1], rhs=ikT[hp, a:z],
                                          start=True, stop=True)
                        m.then_inc(s("ix_d"), 1)
                    pe.wait_ge(s("ix_r"), NH * n)
                for h in range(NH):
                    hp = slice(DH * (h % 2), DH * (h % 2) + DH)
                    m = pe.matmul(PS[:, h % 2, (h // 2) * P:(h // 2) * P + P], lhsT=wukT[hp, h // 2, :], rhs=Q[hp, 4 + h // 2, q],
                                  start=True, stop=True)
                    if h >= NH - 2:
                        m.then_inc(s("d_q"), 1)
                pe.wait_ge(s("d_qe"), 2 * n + 2)
                pe.wait_ge(s("a_oe"), n + 1)
                for i in range(-1, NH + 2):
                    if i + 1 < NH:
                        if i >= 1:
                            pe.wait_ge(s("d_lb"), NH * n + i)
                        for a in range(0, L, BW):
                            z = min(L, a + BW)
                            m = pe.matmul(PS[:, 4 + 2 * ((i + 1) % 2) + a // BW, 0:z - a], lhsT=QL[:, i + 1, :], rhs=cT[:, a:z],
                                          start=True, stop=True)
                        m.then_inc(s("d_l"), 1)
                    if 1 <= i <= NH:
                        h = i - 1
                        pe.wait_ge(s("d_n"), NH * n + h + 1)
                        if h >= 2:
                            pe.wait_ge(s("d_oe"), NH * n + h - 1)
                        for kt in range(n + 1):
                            m = pe.transpose(PS[:, 2 * (h % 2) + kt // 4, (kt % 4) * P:(kt % 4) * P + P],
                                             LG[:, h % 2, kt * P:kt * P + P], ident[:, :])
                        m.then_inc(s("d_t"), 1)
                    if i >= 2:
                        h = i - 2
                        pe.wait_ge(s("d_te"), NH * n + h + 1)
                        for kt in range(n + 1):
                            m = pe.matmul(PS[:, 2 * (h % 2), 0:P], lhsT=cR[:, kt, :], rhs=PT[:, 8 * (h % 2) + kt, :],
                                          start=(kt == 0), stop=(kt == n))
                        m.then_inc(s("d_o"), 1)
                pe.wait_ge(s("d_oe"), NH * n + NH)
                for h in range(NH):
                    m = pe.matmul(PS[DH * (h % 2):DH * (h % 2) + DH, 0, (h // 2) * P:(h // 2) * P + P],
                                  lhsT=wuv[:, h, :], rhs=OL[:, h, :], start=True, stop=True)
                m.then_inc(s("d_f"), 1)
            pe.wait_ge(s("d_fe"), NT)
            for j in range(2):
                gemm_t(TT["wo"] + 8 * j, weights(WO0 + j), x=Q)
            pe.wait_ge(s("mem_in"), 32)
            for k in range(0, KC, 2):
                o = bank(FT["memT"] + k // 2)
                for i in range(2):
                    for t in range(2):
                        m = pe.transpose(o[:, (2 * i + t) * P:(2 * i + t) * P + P], memR[:, t, (k + i) * P:(k + i) * P + P], ident[:, :])
                m.then_inc(f_ready, 1)
            pe.wait_ge(f_free, FT["xk"])
            for j in range(2):
                gemm_f("xk", FT["xk"] + 4 * j, weights(WO0 + 2 + j), range(4), x=memT, halves=1, width=MEM)
            for j in range(2):
                gemm_t(TT["xv"] + 2 * j, weights(WO0 + 4 + j), x=memT, tiles=2)
            transposes("xt1", XR, s("ln_done"), lambda h: NT + 4 * h + 4)
            pe.wait_ge(f_free, FT["xq"])
            for j in range(2):
                gemm_f("xq", FT["xq"] + 8 * j, weights(WO0 + 6 + j), range(4))
            pe.wait_ge(f_free, FT["xq"] + 16)
            pe.wait_ge(t_free, TT["xo"])
            for i in range(NT + 1):
                if i < NT:
                    if i >= 2:
                        pe.wait_ge(s("x_p"), i - 1)
                    for h in range(XH):
                        for kk in range(2):
                            m = pe.matmul(PS[:, 2 * (i % 2) + h // 2, (h % 2) * MEM:(h % 2) * MEM + MEM],
                                          lhsT=Q[:, 2 * h + kk, i * P:i * P + P], rhs=xkT[:, 2 * h + kk, :],
                                          start=(kk == 0), stop=(kk == 1))
                    m.then_inc(s("x_s"), 1)
                if i >= 1:
                    t, b0 = i - 1, 4 + 2 * ((i - 1) % 2)
                    pe.wait_ge(s("x_n"), t + 1)
                    if t >= 2:
                        pe.wait_ge(s("x_oe"), t - 1)
                    for j in range(8):
                        m = pe.transpose(PS[:, b0 + j // 4, (j % 4) * P:(j % 4) * P + P], XP[:, t % 2, j * P:j * P + P], ident[:, :])
                    m.then_inc(s("x_t"), 1)
                    pe.wait_ge(s("x_te"), t + 1)
                    for h in range(XH):
                        for dd in range(2):
                            for mt in range(2):
                                m = pe.matmul(PS[:, b0 + h // 2, ((h % 2) * 2 + dd) * P:((h % 2) * 2 + dd) * P + P],
                                              lhsT=xv[:, mt, (2 * h + dd) * P:(2 * h + dd) * P + P],
                                              rhs=XPT[:, t % 2, (2 * h + mt) * P:(2 * h + mt) * P + P],
                                              start=(mt == 0), stop=(mt == 1))
                    m.then_inc(s("x_o"), 1)
            pe.wait_ge(s("x_oe"), NT)
            for j in range(2):
                gemm_t(TT["xo"] + 8 * j, weights(WO0 + 8 + j), x=Q)
            transposes("xt2", XR, s("ln_done"), lambda h: 2 * NT + 4 * h + 4)
            pe.wait_ge(f_free, FT["up"])
            def product(o, terms, first=True, last=True):
                for i, ((a_hi, a_lo), (b_hi, b_lo)) in enumerate(terms):
                    pe.matmul(o, lhsT=a_hi, rhs=b_hi, start=(first and i == 0), stop=False)
                    pe.matmul(o, lhsT=a_hi, rhs=b_lo, start=False, stop=False)
                    m = pe.matmul(o, lhsT=a_lo, rhs=b_hi, start=False, stop=(last and i == len(terms) - 1))
                return m

            def pair(v_hi, v_lo, *at):
                return v_hi[at], v_lo[at]

            W_UP = [[w[i].rearrange("p (k n) -> p k n", k=KC) for w in (WHI, WLO)] for i in range(2)]
            W_DOWN = [[w[i].rearrange("p (k n) -> p k n", k=4) for w in (WHI, WLO)] for i in range(2)]
            every = slice(None)
            with pe.Fori(0, N_UP) as g:
                for j in range(2):
                    pe.wait_ge(s("w_lo"), g * 4 + (1 + j))
                    for f in range(2):
                        for h in range(2):
                            n = FT["up"] + 4 * j + 2 * f + h
                            pe.wait_ge(f_free, g * 8 + (n - 3))
                            product(PS[:, n % 4, :], [(pair(*W_UP[j], every, k, slice(f * P, f * P + P)),
                                                       pair(X_HI, X_LO1, every, k, slice(h * BW, h * BW + BW))) for k in range(KC)]
                                    ).then_inc(f_ready, 1)
                for j in range(2):
                    pe.wait_ge(s("w_lo"), g * 4 + (3 + j))
                    for t in range(NT):
                        if j == 0 and t % 4 == 0:
                            pe.wait_ge(s("hidden1"), g * 8 + (11 + t // 4))
                        n = TT["down"] + 8 * j + t
                        pe.wait_ge(t_free, g * 16 + (n - 3))
                        product(PS[:, 4 + n % 4, :], [(pair(H_HI, H_LO, every, k, slice(t * P, t * P + P)),
                                                       pair(*W_DOWN[j], every, k, every)) for k in range(4)]).then_inc(t_ready, 1)

            pe.wait_ge(s("ctx_rows"), 1)
            for k in range(0, KC, 2):
                o = bank(FT["ctxT"] + k // 2)
                for i in range(2):
                    for t in range(2):
                        m = pe.transpose(o[:, (2 * i + t) * P:(2 * i + t) * P + P], ctxR[:, t, (k + i) * P:(k + i) * P + P], ident[:, :])
                m.then_inc(f_ready, 1)
            pe.wait_ge(f_free, FT["cg"])
            pe.wait_ge(s("gw_in"), 128)

            def gates(name, x, halves, width):
                n = FT[name]
                for h in range(halves):
                    for gi in range(2):
                        o = bank(n)
                        for k in range(KC):
                            m = pe.matmul(o[0:GR, 0:width], lhsT=GW[:, k, gi, :], rhs=x[:, k, h * width:h * width + width],
                                          start=(k == 0), stop=(k == KC - 1))
                        m.then_inc(f_ready, 1)
                        n += 1

            def gate_columns(nc_, free, i):
                pe.wait_ge(f_free, free)
                pe.wait_ge(s("g_e"), i + 1)
                for c in range(nc_):
                    for j, row in enumerate((uu, enm, wsr)):
                        m = pe.transpose(PS[:, c // 4, ((c % 4) * 3 + j) * GR:((c % 4) * 3 + j) * GR + GR],
                                         row[0:GR, c * P:c * P + P], ident[0:GR, 0:GR])
                for dh in range(2 * MH):
                    m = pe.matmul(PS[:, 2, dh * NC:dh * NC + nc_], lhsT=SEL[0:GR, dh, :], rhs=mpc[0:GR, 0:nc_],
                                  start=True, stop=True)
                m.then_inc(s("g_t"), 1)
                pe.wait_ge(s("g_c"), i + 1)

            def scan(steps, i0, j0, V):
                for idx, (c, d) in enumerate(steps):
                    i = i0 + idx
                    outs = j0 is not None
                    j = idx
                    if i >= 1:
                        pe.wait_ge(s("m_w"), i)
                    if outs and j >= 1:
                        pe.wait_ge(s("m_arg"), j)
                    for h in range(MH):
                        m = pe.matmul(PS[:, 0, h * P:h * P + P], lhsT=SEL[0:GR, d * MH + h, :], rhs=MM[0:GR, c * P:c * P + P],
                                      start=True, stop=True)
                    m.then_inc(s("m_b"), 1)
                    if outs:
                        if j >= 1:
                            pe.wait_ge(s("m_pt"), j)
                        for h in range(MH):
                            m = pe.matmul(PS[:, 1, h * P:h * P + P], lhsT=kT[:, h, c * P:c * P + P], rhs=qT[:, h, c * P:c * P + P],
                                          start=True, stop=True)
                        m.then_inc(s("m_st"), 1)
                        pe.wait_ge(s("m_qs"), j + 1)
                        pe.wait_ge(s("m_cu"), 2 * i - 2)
                        pe.wait_ge(s("m_pt"), j + 1)
                        if j >= 1:
                            pe.wait_ge(s("m_h"), j)
                        for h in range(MH):
                            pe.matmul(PS[:, 2 + h, 0:V1], lhsT=QS[:, j % 2, h * P:h * P + P], rhs=CC[:, d * MH + h, :],
                                      start=True, stop=False)
                            m = pe.matmul(PS[:, 2 + h, 0:V1], lhsT=PP[:, j % 2, h * P:h * P + P], rhs=V[:, c, h, :],
                                          start=False, stop=True)
                        m.then_inc(s("m_n"), 1)
                    pe.wait_ge(s("m_ks"), i + 1)
                    for pair in range(2):
                        if 2 * i + pair >= 1:
                            pe.wait_ge(s("m_cu"), 2 * i + pair)
                        for h in (2 * pair, 2 * pair + 1):
                            m = pe.matmul(PS[:, 6 + h % 2, 0:V1], lhsT=KS[:, i % 2, h * P:h * P + P], rhs=V[:, c, h, :],
                                          start=True, stop=True)
                        m.then_inc(s("m_d"), 1)

            gates("cg", hcT, 1, MEM)
            gemm_t(TT["ck"], weights(M0), x=hcT, tiles=2)
            for j in range(2):
                gemm_t(TT["cv"] + 2 * j, weights(M0 + 1 + j), x=hcT, tiles=2)
            pe.wait_ge(s("v_one"), 1)
            gate_columns(2, FT["xtm"], 0)
            pe.wait_ge(t_free, TT["mk"])
            scan(CTX_STEPS, 0, None, VX)
            pe.wait_ge(s("m_w"), 4)
            pe.wait_ge(s("m_cu"), 8)
            transposes("xtm", XR, s("xr_norm"), lambda h: 4 * h + 4)
            pe.wait_ge(f_free, FT["mg"])
            gates("mg", XT, 2, BW)
            gemm_f("mq", FT["mq"], weights(M0 + 3), range(4))
            gemm_t(TT["mk"], weights(M0 + 4))
            for h in range(MH):
                for half in range(2):
                    pe.wait_ge(t_free, TT["mk"] + 4 * half + 4)
                    o = bank(FT["kT"] + 2 * h + half)
                    for j in range(4):
                        m = pe.transpose(o[:, j * P:j * P + P], KK[:, 4 * half + j, h * P:h * P + P], ident[:, :])
                    m.then_inc(f_ready, 1)
            for j in range(2):
                gemm_t(TT["mv"] + 8 * j, weights(M0 + 5 + j))
            gate_columns(NC, FT["yT"], 1)
            pe.wait_ge(t_free, TT["mo"])
            pe.wait_ge(s("v_one"), 2)
            scan(X_STEPS, 4, 0, VV)
            pe.wait_ge(s("m_h"), 16)
            pe.wait_ge(s("m_cu"), 40)
            for j in range(2):
                gemm_t(TT["mo"] + 8 * j, weights(M0 + 7 + j))
            transposes("yT", Q, s("o_y"), lambda h: NT + 4 * h + 4)
            pe.wait_ge(f_free, FT["xtf"])
            for j in range(2):
                gemm_t(TT["mout"] + 8 * j, weights(M0 + 9 + j))
            transposes("xtf", XN, s("xn_norm"), lambda h: 4 * h + 4)
            pe.wait_ge(s("xf_lo"), 16)

            def up2(g, c, at):
                pe.wait_ge(s("w_lo"), g * 6 + at)
                for m_ in range(4):
                    n = FT["up2"] + 4 * c + m_
                    a, h = P * (m_ // 2), m_ % 2
                    pe.wait_ge(f_free, g * 16 + (n - 3))
                    product(PS[:, n % 4, :], [(pair(*W_UP[1 - c % 2], every, k, slice(a, a + P)),
                                               pair(X_HI, X_LO2, every, k, slice(h * BW, h * BW + BW))) for k in range(KC)]
                            ).then_inc(f_ready, 1)

            def down2(g, j, kc, at, hid):
                pe.wait_ge(s("w_lo"), g * 6 + at)

                def terms(t, ks):
                    return [(pair(H_HI, H_LO, every, k, slice(t * P, t * P + P)), pair(*W_DOWN[1 - j], every, k, every)) for k in ks]

                if j == 0:
                    pe.wait_ge(s("hidden"), g * 4 + (hid - 1))
                    for t in range(4):
                        n = TT["down2"] + t
                        pe.wait_ge(t_free, g * 16 + (n - 3))
                        product(PS[:, 4 + n % 4, :], terms(t, range(kc - 1)), last=False)
                    pe.wait_ge(s("hidden"), g * 4 + hid)
                    for t in range(4):
                        product(PS[:, 4 + (TT["down2"] + t) % 4, :], terms(t, [kc - 1]), first=False).then_inc(t_ready, 1)
                for t in range(4 if j == 0 else 0, NT):
                    n = TT["down2"] + 8 * j + t
                    pe.wait_ge(t_free, g * 16 + (n - 3))
                    product(PS[:, 4 + n % 4, :], terms(t, range(kc))).then_inc(t_ready, 1)

            W0 = 4 * N_UP
            with pe.Fori(0, N_G) as g:
                for c in range(4):
                    up2(g, c, W0 + c + 1)
                for j in range(2):
                    down2(g, j, 4, W0 + 5 + j, 6)
            for c in range(2):
                up2(N_G, c, W0 + c + 1)
            for j in range(2):
                down2(N_G, j, 2, W0 + 3 + j, 4)

        @block.scalar
        def _(act):
            own = [0]

            def mark(ins):
                ins.then_inc(own_act, 1)
                own[0] += 1

            def settled():
                act.wait_ge(own_act, own[0])

            def load_rows(*rows):
                for i, v in rows:
                    act.dma_start(ROW[:, i, :], v.partition_broadcast(P)).then_inc(rows_in, 16)

            act.dma_start(cols[:, :], I["cols_h"]).then_inc(cols_in, 16)
            load_rows((0, I["ln_emb_g"]), (1, I["ln_emb_b"]))
            act.dma_start(hot[0:NB + 1, :, :], I["hot_h"]).then_inc(s("relb_in"), 16)
            act.wait_ge(s("relb_one"), 1)
            act.dma_start(relb[0:NB, :], I["rel_bias"]).then_inc(s("relb_in"), 16)

            def root(r, n=NT):
                act.wait_ge(s("ln_stat"), r)
                act.activation(sdv[:, 0:n], ve[:, 0:n], ACT.Sqrt).then_inc(s("ln_sd"), 1)

            def empty(n, out_ap, bias=0.0, scale=1.0, width=BW, rows=P, func=ACT.Identity):
                act.wait_ge(f_ready, n + 1)
                act.activation(out_ap, PS[0:rows, n % 4, 0:width], func, bias=bias, scale=scale).then_inc(f_free, 1)

            def empty_xt(name, scale=None, bias=None):
                for h in range(2):
                    for k in range(KC):
                        o = XT[:, k, BW * h:BW * h + BW]
                        if scale is None:
                            empty(FT[name] + 8 * h + k, o)
                        else:
                            empty(FT[name] + 8 * h + k, o, bias=bias(k), scale=scale(k))

            for g in range(2):
                empty(FT["vb"] + g, vb[0:NH, g, :], width=N_BIAS, rows=NH)
            act.wait_ge(f_free, FT["vb"] + 2)
            for g in range(2):
                act.dma_start(bias_d[g * NH:g * NH + NH], vb[0:NH, g, :].unsqueeze(1).to_broadcast([NH, P, N_BIAS])
                              ).then_inc(s("vb_out"), 16)
            root(1)
            act.wait_ge(cols_in, 16)
            act.activation(cx[:, :, :].rearrange("p k c -> p (k c)"), cols[:, COLS["c"][0]:COLS["c"][1]],
                           ACT.Silu).then_inc(s("cx_ready"), 1)
            empty_xt("xt0")
            act.wait_ge(s("ln_done"), NT)
            attn_in = s("attn_in")
            act.dma_start(mrow[:, 0:P], I["b_in"][0, 640:768].partition_broadcast(P)).then_inc(s("misc_in"), 16)
            act.dma_start(mrow[:, P:2 * P], I["b_in"][0, 1280:1408].partition_broadcast(P)).then_inc(s("misc_in"), 16)
            act.dma_start(mrow[:, 2 * P:MISC], I["b_in"][0, 1920:1992].partition_broadcast(P)).then_inc(s("misc_in"), 16)
            act.dma_start(kvg, I["dsa_kv_norm_g"][0].partition_broadcast(P)).then_inc(s("misc_in"), 16)
            act.dma_start(ikg[:, 0, :], I["idx_k_ln_g"][0].partition_broadcast(P)).then_inc(s("misc_in"), 16)
            act.dma_start(ikg[:, 1, :], I["idx_k_ln_b"][0].partition_broadcast(P)).then_inc(s("misc_in"), 16)
            act.dma_start(wuk, I["dsa_w_uk"][0].rearrange("h c d -> c h d")).then_inc(s("wuk_in"), 16)
            act.dma_start(wuv, I["dsa_w_uv"][0].rearrange("h c d -> c h d")).then_inc(attn_in, 16)
            act.dma_start(sink, I["swa_sinks"][0].partition_broadcast(P)).then_inc(attn_in, 16)
            for name, dst in (("qa", Q[:, 0:4, :]), ("qb", Q[:, 4:8, :]), ("iq", iqT)):
                for f in range(4):
                    for h in range(2):
                        empty(FT[name] + 2 * f + h, dst[:, f, BW * h:BW * h + BW],
                              bias=cols[:, COLS[name][0] + f:COLS[name][0] + f + 1])
            for h in range(2):
                a, z = BW * h, BW * h + BW
                empty(FT["ka"] + h, kaS[:, h, :], bias=cols[:, COLS["ka"][0]:COLS["ka"][1]])
                act.wait_ge(f_free, FT["ka"] + h + 1)
                for kv in range(2):
                    for r in range(2):
                        mark(act.activation(kaT[DH * r:DH * r + DH, kv, a:z], kaS[DH * kv:DH * kv + DH, h, :], ACT.Copy))
            empty(FT["ukT"], wukT.rearrange("p a b -> p (a b)"))
            root(2, 16)
            for i, dst in ((0, cT), (2, ikT)):
                for h in range(2):
                    empty(FT["ckT"] + i + h, dst[:, BW * h:BW * h + BW])
            act.wait_ge(s("vb_out"), 32)
            bt = bias_d.tensor
            act.wait_ge(f_ready, FT["ka"] + 1)
            act.wait_ge(t_ready, TT["misc"] + 8)
            for g in range(2):
                for h4 in range(2):
                    act.dma_start(bias[:, g * NH + 4 * h4:g * NH + 4 * h4 + 4, :],
                                  bass.AP(bt, (g * NH + 4 * h4) * P * N_BIAS + P - 1,
                                          [[N_BIAS - 1, P], [P * N_BIAS, 4], [1, 2 * P]])).then_inc(attn_in, 16)
            act.dma_start(far, bass.AP(bt, NH * P * N_BIAS, [[0, P], [P * N_BIAS, NH]]), allow_slow_non_contiguous=True).then_inc(attn_in, 16)
            for n in range(NT):
                w0 = P if n == 0 else 0
                act.wait_ge(s("a_m"), n + 1)
                for h in range(NH):
                    mark(act.activation(SB[:, h, w0:], SB[:, h, w0:], ACT.Exp, bias=nm[:, h:h + 1],
                                        accum_out=den[:, h:h + 1]))
                act.activation(es, sd, ACT.Exp).then_inc(s("a_p"), 1)
                act.wait_ge(s("ada_mm"), ADA_N // ADA_W * (n + 1))
                if n >= 2:
                    act.wait_ge(s(f"mods_out{n % 2}"), 16 * (n // 2))
                act.activation(modr[0:2, n % 2, :], PSf[0:2, 5 * BW:5 * BW + ADA_N], ACT.Copy).then_inc(s("ada_e"), 1)
                for b in range(4):
                    act.wait_ge(s("a_t"), 4 * n + b + 1)
                    if n == 0:
                        v = PS[:, b, :].rearrange("p (a b c) -> p a b c", a=2, b=2)
                        act.activation(PT[:, 4 * b + 1:4 * b + 4:2, :], v[:, :, 1, :], ACT.Copy).then_inc(s("a_te"), 1)
                    else:
                        act.activation(PT[:, 4 * b:4 * b + 4, :].rearrange("p a b -> p (a b)"), PS[:, b, :],
                                       ACT.Copy).then_inc(s("a_te"), 1)
                L = (n + 1) * P
                if 1 <= n < NT - 1:
                    act.wait_ge(s("a_o"), n + 1)
                    L1 = (n + 2) * P
                    for h in range(NH):
                        i = NH * (n - 1) + h
                        act.wait_ge(s("ix_d"), i + 1)
                        if h >= 2:
                            act.wait_ge(s("ix_s"), i - 1)
                        act.activation(RL[:, h % 2, 0:L1], PSf[:, 1024 * (h % 4):1024 * (h % 4) + L1], ACT.Relu,
                                       scale=DH ** -0.5).then_inc(s("ix_r"), 1)
                for b in range(2):
                    act.wait_ge(s("d_q"), 2 * n + b + 1)
                    act.activation(QL[:, b:NH:2, :], PS[:, b, :].rearrange("p (a b) -> p a b", a=4), ACT.Copy,
                                   scale=DH ** -0.5).then_inc(s("d_qe"), 1)
                for i in range(NH + 3):
                    if i < NH:
                        act.wait_ge(s("d_m"), NH * n + i + 1)
                        act.activation(LG[:, i % 2, 0:L], LG[:, i % 2, 0:L], ACT.Exp, bias=nm[:, i:i + 1],
                                       accum_out=den[:, i:i + 1]).then_inc(s("d_e"), 1)
                    if 1 <= i <= NH:
                        h = i - 1
                        act.wait_ge(s("d_r"), NH * n + h + 1)
                        act.activation(LG[:, h % 2, 0:L], LG[:, h % 2, 0:L], ACT.Copy, scale=den[:, h:h + 1]).then_inc(s("d_n"), 1)
                    if 2 <= i <= NH + 1:
                        h = i - 2
                        act.wait_ge(s("d_t"), NH * n + h + 1)
                        if 1 <= n < NT - 1 and h < 2:
                            act.wait_ge(s("ix_s"), NH * n)
                        act.activation(PT[:, 8 * (h % 2):8 * (h % 2) + n + 1, :].rearrange("p a b -> p (a b)"),
                                       PSf[:, 1024 * (h % 2):1024 * (h % 2) + L], ACT.Copy).then_inc(s("d_te"), 1)
                    if i >= 3:
                        h = i - 3
                        act.wait_ge(s("d_o"), NH * n + h + 1)
                        act.activation(OL[:, h, :], PS[:, 2 * (h % 2), 0:P], ACT.Copy).then_inc(s("d_oe"), 1)
            act.wait_ge(s("d_fe"), NT)
            for j in range(2):
                act.wait_ge(s(f"mods_out{j}"), 64)
            act.wait_ge(s("d_oe"), NH * NT)
            load_rows((0, I["ln1_g"][0]), (1, I["ln1_b"][0]), (2, I["b_o"][0]))
            for k in range(0, KC, 2):
                empty(FT["memT"] + k // 2, memT[:, k:k + 2, :].rearrange("p a b -> p (a b)"))
            for f in range(KC):
                empty(FT["xk"] + f, xkT[:, f, :], bias=cols[:, COLS["xk"][0] + f:COLS["xk"][0] + f + 1], width=MEM)
            root(3)
            empty_xt("xt1")
            load_rows((0, I["ln2_g"][0]), (1, I["ln2_b"][0]), (2, I["xa_bo"][0]))
            for f in range(KC):
                for h in range(2):
                    empty(FT["xq"] + 2 * f + h, Q[:, f, BW * h:BW * h + BW], bias=cols[:, COLS["xq"][0] + f:COLS["xq"][0] + f + 1])
            for i in range(NT + 1):
                if i < NT:
                    act.wait_ge(s("x_m"), i + 1)
                    if i >= 2:
                        act.wait_ge(s("x_t"), i - 1)
                    for h in range(XH):
                        ins = act.activation(XP[:, i % 2, h * MEM:h * MEM + MEM],
                                             PSf[:, 1024 * (i % 2) + h * MEM:1024 * (i % 2) + h * MEM + MEM], ACT.Exp,
                                             bias=xn[:, i % 2, h:h + 1], scale=XD ** -0.5, accum_out=xd[:, i % 2, h:h + 1])
                    ins.then_inc(s("x_p"), 1)
                if i >= 1:
                    t = i - 1
                    act.wait_ge(s("x_t"), t + 1)
                    act.activation(XPT[:, t % 2, :], PSf[:, 2048 + 1024 * (t % 2):3072 + 1024 * (t % 2)], ACT.Copy).then_inc(s("x_te"), 1)
            root(4)
            for i in range(16):
                n = FT["xt2"] + i
                act.wait_ge(f_ready, n + 1)
                act.activation(X_HI[:, i % KC, BW * (i // KC):BW * (i // KC) + BW], PS[:, n % 4, :], ACT.Copy).then_inc(s("x_hi"), 1)
            load_rows((0, I["ln3_g"][0]), (1, I["ln3_b"][0]), (2, I["b_down"][0]))

            def split(buf, at, width=4 * BW):
                act.wait_ge(w_in[buf], at)
                act.activation(WHI[buf][:, 0:width], WRAW[buf][:, 0:width], ACT.Copy).then_inc(s("w_hi"), 1)

            with act.Fori(0, N_UP) as g:
                def rectify(m):
                    act.wait_ge(s("hidden1"), g * 8 + (m + 1))
                    act.wait_ge(f_ready, g * 8 + (FT["up"] + m + 1))
                    act.activation(RU[:, m % 4, :], PS[:, (FT["up"] + m) % 4, :], ACT.Relu,
                                   bias=upb[:, m // 4, (m % 4) // 2:(m % 4) // 2 + 1]).then_inc(f_free, 1)

                split(0, g * 48 + loaded(UP0))
                for m in (0, 1):
                    rectify(m)
                split(1, g * 48 + loaded(UP0 + 1))
                for m in (2, 3, 4, 5):
                    rectify(m)
                split(0, g * 48 + loaded(UP0 + 2))
                for m in (6, 7):
                    rectify(m)
                split(1, g * 48 + loaded(UP0 + 3))
            root(5)
            rows2_in = s("rows2_in")

            def load_rows2(*rows):
                for dst, v in rows:
                    act.dma_start(dst, v.partition_broadcast(P)).then_inc(rows2_in, 16)

            mb = I["m_in_b_2"][0]
            act.wait_ge(s("ln_done"), 4 * NT)
            load_rows2((krow, mb[512:1024]), (ROW[:, 2, :], mb[1024:2048]))
            root(6, 2)
            act.wait_ge(s("mod_ready"), 1)
            for k in range(KC):
                act.wait_ge(f_ready, FT["ctxT"] + k // 2 + 1)
                n = FT["ctxT"] + k // 2
                ins = act.activation(hcT[:, k, :], PS[:, n % 4, MEM * (k % 2):MEM * (k % 2) + MEM], ACT.Identity,
                                     bias=modc[:, 4, k:k + 1], scale=modc[:, 5, k:k + 1])
                if k % 2 == 1:
                    ins.then_inc(f_free, 1)

            def gates(name, i, halves, width):
                n = FT[name]
                act.wait_ge(s("gw_in"), 128)
                for h in range(halves):
                    for row in (li, lf):
                        empty(n, row[0:GR, h * width:h * width + width], bias=gb[0:GR, (n - FT[name]) % 2:(n - FT[name]) % 2 + 1],
                              width=width, rows=GR)
                        n += 1
                w = halves * width
                act.wait_ge(s("g_a"), i + 1)
                mark(act.activation(enm[0:GR, 0:w], bb[0:GR, 0:w], ACT.Exp))
                settled()
                act.activation(enm[0:GR, 0:w], enm[0:GR, 0:w], ACT.Ln, bias=1.0).then_inc(s("g_l"), 1)

            def gates_exp(i, w):
                act.wait_ge(s("g_b"), i + 1)
                mark(act.activation(enm[0:GR, 0:w], tmp[0:GR, 0:w], ACT.Exp, scale=-1.0))
                act.activation(wsr[0:GR, 0:w], lf[0:GR, 0:w], ACT.Exp).then_inc(s("g_e"), 1)

            def scan(steps, i0, outs):
                for idx, (c, d) in enumerate(steps):
                    i, j = i0 + idx, idx
                    act.wait_ge(s("m_b"), i + 1)
                    if i >= 2:
                        act.wait_ge(s("m_cu"), 2 * i - 2)
                    if outs and j >= 2:
                        act.wait_ge(s("m_qs"), j - 1)
                    for h in range(MH):
                        ins = act.activation(WI[:, i % 2, h * P:h * P + P], PS[:, 0, h * P:h * P + P], ACT.Exp,
                                             bias=MPB[:, d * MH + h, c:c + 1], scale=-1.0)
                    ins.then_inc(s("m_w"), 1)
                    if outs:
                        act.wait_ge(s("m_arg"), j + 1)
                        for h in range(MH):
                            ins = act.activation(DD[:, j % 2, h * P:h * P + P], DD[:, j % 2, h * P:h * P + P], ACT.Exp,
                                                 bias=COL[:, c, 0, 32 * d + h:32 * d + h + 1])
                        ins.then_inc(s("m_e"), 1)

            gates("cg", 0, 1, MEM)
            gates_exp(0, MEM)
            act.wait_ge(s("g_c"), 1)
            scan(CTX_STEPS, 0, False)
            act.wait_ge(s("m_d"), 8)
            load_rows2((ROW[:, 2, :], mb[1024:2048]))
            root(7)
            empty_xt("xtm", scale=lambda k: modc[:, 1, k:k + 1], bias=lambda k: modc[:, 0, k:k + 1])
            n = FT["mg"]
            gates("mg", 1, 2, BW)
            for f in range(MH):
                for h in range(2):
                    empty(FT["mq"] + 2 * f + h, qT[:, f, BW * h:BW * h + BW], bias=cols[:, COLS["mq"][0] + f:COLS["mq"][0] + f + 1])
            gates_exp(1, T)
            for h in range(MH):
                for half in range(2):
                    empty(FT["kT"] + 2 * h + half, kT[:, h, BW * half:BW * half + BW])
            act.wait_ge(s("g_c"), 2)
            scan(X_STEPS, 4, True)
            act.wait_ge(s("m_h"), 16)
            act.wait_ge(s("m_d"), 40)
            load_rows2((ROW[:, 0, :], mb[2048:3072]), (ROW[:, 2, :], I["m_norm_g_2"][0]))
            root(8, 32)
            for m in range(16):
                act.wait_ge(t_free, TT["mo"] + m + 1)
                act.activation(OG[:, m % 2, :], OG[:, m % 2, :], ACT.Sigmoid).then_inc(s("o_s"), 1)
            act.wait_ge(s("o_y"), 16)
            load_rows2((ROW[:, 0, :], mods_d[0, 2 * D:3 * D]), (ROW[:, 1, :], I["ada_b_2"][0, 2 * D:3 * D]),
                       (ROW[:, 2, :], I["post_mix_g_2"][0]))
            empty_xt("yT")
            root(9)
            act.wait_ge(s("x_new"), NT)
            load_rows2((ROW[:, 0, :], mods_d[0, 5 * D:6 * D]), (ROW[:, 1, :], I["ada_b_2"][0, 5 * D:6 * D]),
                       (ROW[:, 2, :], I["post_ffn_g_2"][0]))
            root(10)
            for i in range(16):
                n, k = FT["xtf"] + i, i % KC
                act.wait_ge(f_ready, n + 1)
                if i == 0:
                    act.wait_ge(s("b_gain"), NT)
                if i >= 4:
                    act.wait_ge(s("xf_lo"), i - 3)
                act.activation(XS[:, i % 4, :], PS[:, n % 4, :], ACT.Identity, bias=modc[:, 2, k:k + 1],
                               scale=modc[:, 3, k:k + 1]).then_inc(f_free, 1)

            def chunks2(g, n_chunks, later):
                split(1, g * 112 + loaded(G0))
                for c in range(n_chunks):
                    act.wait_ge(s("hidden"), g * 4 + (c + 1))
                    for m in range(4):
                        n = FT["up2"] + 4 * c + m
                        dst = (UU, GG)[m // 2]
                        act.wait_ge(f_ready, g * 16 + (n + 1))
                        act.activation(dst[:, c % 2, BW * (m % 2):BW * (m % 2) + BW], PS[:, n % 4, :], ACT.Copy).then_inc(f_free, 1)
                        if m == 1:
                            later[c](g)
                    act.wait_ge(s("conv"), g * 4 + (c + 1))
                    act.activation(TC[:, c % 2, :], TC[:, c % 2, :], ACT.Silu).then_inc(s("silu"), 1)
                later[n_chunks](g)

            with act.Fori(0, N_G) as g:
                chunks2(g, 4, [lambda g, i=i: split(1 - i % 2, g * 112 + loaded(G0 + i)) for i in range(1, 6)])
            E0 = G0 + 6 * N_G
            split_rest = {1: lambda g: split(0, loaded(E0 + 1)), 2: lambda g: split(1, loaded(E0 + 2), 2 * BW),
                          3: lambda g: split(0, loaded(E0 + 3), 2 * BW)}
            chunks2(N_G, 2, [split_rest[1], split_rest[2], split_rest[3]])
            root(11)

        @block.vector
        def _(dve):
            own = [0]

            def mark(ins):
                ins.then_inc(own_dve, 1)
                own[0] += 1

            def settled():
                dve.wait_ge(own_dve, own[0])

            def stats(t0, rows, parts):
                w = rows.shape[1] // parts
                for j in range(parts):
                    mark(dve.bn_stats(st[:, 2 * t0 + j if parts == 2 else t0, :], rows[:, j * w:j * w + w]))
                settled()
                if parts == 2:
                    mark(dve.bn_aggr(mv[:, t0, :], stf[:, 12 * t0:12 * t0 + 12]))
                else:
                    mark(dve.bn_aggr(mv[:, t0, :], stf[:, 6 * t0:6 * t0 + 6]))

            def rstd(n, r):
                dve.wait_ge(s("ln_sd"), r)
                mark(dve.reciprocal(rs[:, 0:n], sdv[:, 0:n]))
                settled()

            def layer_norm(i, r, ready):
                for t in range(NT):
                    ready(t)
                    stats(t, XR[:, t, :], 2)
                settled()
                dve.tensor_scalar(ve[:, 0:NT], mv[:, 0:NT, 1], LN_EPS, None, ALU.add).then_inc(s("ln_stat"), 1)
                rstd(NT, r)
                for t in range(NT):
                    mark(dve.tensor_scalar(XR[:, t, :], XR[:, t, :], mv[:, t, 0:1], rs[:, t:t + 1], ALU.subtract, ALU.mult))
                    settled()
                    dve.tensor_tensor(XR[:, t, :], XR[:, t, :], ROW[:, 0, :], ALU.mult).then_inc(s("ln_half"), 1)

            def ready0(t):
                if t % 4 == 0:
                    dve.wait_ge(x_in, 32)
            ready0(0)
            rows2_v = s("rows2_in")
            dve.wait_ge(rows_in, 32)
            layer_norm(0, 1, ready0)

            dve.wait_ge(s("misc_in"), 96)
            for t in range(NT):
                n = TT["misc"] + t
                dve.wait_ge(t_ready, n + 1)
                dve.tensor_tensor(misc[:, t, :], PS[:, 4 + n % 4, 0:MISC], mrow, ALU.add).then_inc(t_free, 1)
            for t in range(NT):
                dve.wait_ge(t_free, TT["misc"] + t + 1)
                stats(t, misc[:, t, P:2 * P], 1)
                stats(NT + t, misc[:, t, 2 * P:2 * P + DH], 1)
            settled()
            mark(dve.tensor_tensor(ve[:, 0:NT], mv[:, 0:NT, 0], mv[:, 0:NT, 0], ALU.mult))
            settled()
            mark(dve.scalar_tensor_tensor(ve[:, 0:NT], ve[:, 0:NT], LN_EPS, mv[:, 0:NT, 1], ALU.add, ALU.add))
            dve.tensor_scalar(ve[:, NT:2 * NT], mv[:, NT:2 * NT, 1], LN_EPS, None, ALU.add).then_inc(s("ln_stat"), 1)
            rstd(2 * NT, 2)
            for t in range(NT):
                mark(dve.tensor_scalar(cR[:, t, :], misc[:, t, P:2 * P], rs[:, t:t + 1], None, ALU.mult))
                mark(dve.tensor_scalar(ikn[:, t, 0:DH], misc[:, t, 2 * P:2 * P + DH], mv[:, NT + t, 0:1],
                                       rs[:, NT + t:NT + t + 1], ALU.subtract, ALU.mult))
            mark(dve.tensor_scalar(iwt, misc[:, :, 2 * P + DH:MISC], NH ** -0.5, None, ALU.mult))
            settled()
            mark(dve.tensor_tensor(ikn[:, :, 0:DH], ikn[:, :, 0:DH], over_mid(ikg[:, 0, :], NT), ALU.mult))
            dve.tensor_tensor(cR, cR, over_mid(kvg, NT), ALU.mult).then_inc(s("ck_ready"), 1)
            settled()
            mark(dve.tensor_tensor(ikn[:, :, 0:DH], ikn[:, :, 0:DH], over_mid(ikg[:, 1, :], NT), ALU.add))
            settled()
            dve.tensor_copy(ikn[:, :, DH:2 * DH], ikn[:, :, 0:DH]).then_inc(s("ck_ready"), 1)

            dve.wait_ge(s("attn_in"), 16 * 7)
            dve.wait_ge(s("ck_ready"), 2)
            R8 = TOPK // 8

            def pick(m, first, last):
                w = (m + 1) * P
                for i in range(first, last):
                    if i == 0:
                        dve.wait_ge(s("ix_c"), m - 1)
                    src = score if i == 0 else work
                    settled()
                    mark(dve.max(top, src[:, 0:w]))
                    settled()
                    mark(dve.match_replace(work[:, 0:w], top, src[:, 0:w], TAKEN))
                    if i == R8 - 1:
                        settled()
                        mark(dve.tensor_scalar(msk[:, m % 2, 0:w], work[:, 0:w], TAKEN / 2, NEG, ALU.is_ge, ALU.mult))
                        settled()

            BEFORE, WINDOW = 16, 26
            for n in range(NT):
                w0 = P if n == 0 else 0
                L = (n + 1) * P
                for e in range(4):
                    dve.wait_ge(s("a_s"), 4 * n + e + 1)
                    if n > 0 and e == 0:
                        dve.wait_ge(s("d_t"), NH * n)
                    r, h0 = e % 2, 4 * (e // 2) + e % 2
                    v = PS[:, 2 * r + e // 2, :].rearrange("p (a b) -> p a b", a=2)
                    dve.scalar_tensor_tensor(SB[:, h0:h0 + 3:2, w0:], v[:, :, w0:], DH ** -0.5,
                                             bias[:, h0:h0 + 3:2, w0:], ALU.mult, ALU.add).then_inc(s("a_sb"), 1)
                dve.wait_ge(s("a_sb"), 4 * n + 4)
                mark(dve.tensor_reduce(mx, SB[:, :, w0:], AX.X, ALU.max))
                settled()
                mark(dve.tensor_tensor(mx, mx, sink, ALU.max))
                settled()
                mark(dve.tensor_scalar(nm, mx, -1.0, None, ALU.mult))
                dve.tensor_tensor(sd, sink, mx, ALU.subtract).then_inc(s("a_m"), 1)
                if n >= 2:
                    pick(n, BEFORE, (BEFORE + WINDOW) // 2)
                dve.wait_ge(s("a_p"), n + 1)
                mark(dve.tensor_tensor(den, den, es, ALU.add))
                settled()
                mark(dve.reciprocal(den, den))
                settled()
                dve.tensor_tensor(SB[:, :, w0:], SB[:, :, w0:], over_last(den, 2 * P - w0), ALU.mult).then_inc(s("a_r"), 1)
                if n >= 2:
                    pick(n, (BEFORE + WINDOW) // 2, WINDOW if n < NT - 1 else R8)
                dve.wait_ge(s("a_o"), n + 1)
                dve.tensor_copy(Q[:, 0:4, n * P:n * P + P], PS[:, 4, :].rearrange("p (a b) -> p a b", a=4)).then_inc(s("a_oe"), 1)
                ahead = 1 <= n < NT - 1
                L1 = (n + 2) * P
                if ahead:
                    for h in range(NH):
                        i = NH * (n - 1) + h
                        dve.wait_ge(s("ix_r"), i + 1)
                        if h == 0:
                            dve.tensor_scalar(score[:, 0:L1], RL[:, 0, 0:L1], iwt[:, n + 1, 0:1], None, ALU.mult).then_inc(s("ix_s"), 1)
                        else:
                            if n >= 2:
                                pick(n, WINDOW + (R8 - WINDOW) * (h - 1) // (NH - 1), WINDOW + (R8 - WINDOW) * h // (NH - 1))
                            dve.wait_ge(s("ix_s"), i)
                            dve.scalar_tensor_tensor(score[:, 0:L1], RL[:, h % 2, 0:L1], iwt[:, n + 1, h:h + 1], score[:, 0:L1],
                                                     ALU.mult, ALU.add).then_inc(s("ix_s"), 1)

                near = slice((n - 1) * P if n else 0, L)
                far_w = (n - 1) * P
                for i in range(NH + 1):
                    if i >= 1:
                        h = i - 1
                        dve.wait_ge(s("d_e"), NH * n + h + 1)
                        dve.reciprocal(den[:, h:h + 1], den[:, h:h + 1]).then_inc(s("d_r"), 1)
                    if i < NH:
                        dve.wait_ge(s("d_l"), NH * n + i + 1)
                        if i >= 2:
                            dve.wait_ge(s("d_t"), NH * n + i - 1)
                        if i == 0:
                            dve.wait_ge(s("a_t"), 4 * n + 4)
                        pair = PSf[:, 1024 * (2 + i % 2):1024 * (2 + i % 2) + L]
                        lg = LG[:, i % 2, :]
                        if n >= 2:
                            mark(dve.scalar_tensor_tensor(lg[:, 0:far_w], pair[:, 0:far_w], far[:, i:i + 1],
                                                          msk[:, n % 2, 0:far_w], ALU.add, ALU.add))
                        dve.tensor_tensor(lg[:, near], pair[:, near], bias[:, NH + i, w0:], ALU.add).then_inc(s("d_lb"), 1)
                        dve.wait_ge(s("d_lb"), NH * n + i + 1)
                        if n >= 2:
                            mark(dve.tensor_tensor(lg[:, near], lg[:, near], msk[:, n % 2, near], ALU.add))
                            settled()
                        dve.tensor_reduce(nm[:, i:i + 1], lg[:, 0:L], AX.X, ALU.max, negate=True).then_inc(s("d_m"), 1)
                    if ahead and i < NH:
                        pick(n + 1, BEFORE * i // NH, BEFORE * (i + 1) // NH)
                dve.wait_ge(s("d_f"), n + 1)
                dve.tensor_copy(Q[:, 4:8, n * P:n * P + P], PS[:, 0, :].rearrange("p (a b) -> p a b", a=4)).then_inc(s("d_fe"), 1)

            def residual(i, name=None):
                dve.wait_ge(rows_in, 32 + 48 * (i + 1))
                for t in range(NT):
                    if name and t % 4 == 0:
                        dve.wait_ge(f_ready, FT[name] + 2 * t + 8)
                    dve.scalar_tensor_tensor(XR[:, t, :], XR[:, t, :], ALPHA, ROW[:, 2, :], ALU.mult,
                                             ALU.add).then_inc(s("resid"), 1)

            def add_tiles(name, i):
                for j in range(2):
                    for t in range(NT):
                        n = TT[name] + 8 * j + t
                        dve.wait_ge(s("resid"), NT * i + t + 1)
                        dve.wait_ge(t_ready, n + 1)
                        v = XR[:, t, BW * j:BW * j + BW]
                        dve.tensor_tensor(v, v, PS[:, 4 + n % 4, :], ALU.add).then_inc(t_free, 1)

            residual(0)
            add_tiles("wo", 0)
            layer_norm(1, 3, lambda t: dve.wait_ge(t_free, TT["wo"] + 8 + t + 1))
            dve.wait_ge(s("mem_in"), 32)
            for j in range(2):
                for t in range(2):
                    n = TT["xv"] + 2 * j + t
                    dve.wait_ge(t_ready, n + 1)
                    dve.tensor_tensor(xv[:, t, BW * j:BW * j + BW], PS[:, 4 + n % 4, :], vrow[:, BW * j:BW * j + BW],
                                      ALU.add).then_inc(t_free, 1)
            residual(1, "xt1")
            for i in range(NT + 2):
                if i < NT:
                    dve.wait_ge(s("x_s"), i + 1)
                    mark(dve.tensor_reduce(xm[:, i % 2, :], PSf[:, 1024 * (i % 2):1024 * (i % 2) + 1024]
                                           .rearrange("p (a b) -> p a b", a=XH), AX.X, ALU.max))
                    settled()
                    dve.tensor_scalar(xn[:, i % 2, :], xm[:, i % 2, :], -XD ** -0.5, None, ALU.mult).then_inc(s("x_m"), 1)
                if 1 <= i <= NT:
                    t = i - 1
                    dve.wait_ge(s("x_p"), t + 1)
                    mark(dve.reciprocal(xd[:, t % 2, :], xd[:, t % 2, :]))
                    settled()
                    v = XP[:, t % 2, :].rearrange("p (a b) -> p a b", a=XH)
                    dve.tensor_tensor(v, v, over_last(xd[:, t % 2, :], MEM), ALU.mult).then_inc(s("x_n"), 1)
                if i >= 2:
                    t = i - 2
                    dve.wait_ge(s("x_o"), t + 1)
                    dve.tensor_copy(Q[:, :, t * P:t * P + P], PSf[:, 2048 + 1024 * (t % 2):3072 + 1024 * (t % 2)]
                                    .rearrange("p (a b) -> p a b", a=8)).then_inc(s("x_oe"), 1)
            add_tiles("xo", 1)
            layer_norm(2, 4, lambda t: dve.wait_ge(t_free, TT["xo"] + 8 + t + 1))
            for h in range(2):
                for k in range(KC):
                    n = FT["xt2"] + KC * h + k
                    dve.wait_ge(s("x_hi"), KC * h + k + 1)
                    v = slice(BW * h, BW * h + BW)
                    dve.tensor_tensor(X_LO1[:, k, v], PS[:, n % 4, :], X_HI[:, k, v], ALU.subtract).then_inc(f_free, 1)
            residual(2, "xt2")
            dve.wait_ge(s("resid"), 3 * NT)
            with dve.Fori(0, N_UP) as g:
                for m in range(8):
                    dve.wait_ge(s("squared"), g * 8 + (m + 1))
                    at = (slice(None), m // 2, slice(BW * (m % 2), BW * (m % 2) + BW))
                    dve.tensor_copy(H_HI[at], RU[:, m % 4, :]).then_inc(s("h_hi"), 1)
                    dve.wait_ge(s("h_hi"), g * 8 + (m + 1))
                    dve.tensor_tensor(H_LO[at], RU[:, m % 4, :], H_HI[at], ALU.subtract).then_inc(s("hidden1"), 1)
                for m in range(16):
                    dve.wait_ge(t_ready, g * 16 + (TT["down"] + m + 1))
                    v = XR[:, m % 8, BW * (m // 8):BW * (m // 8) + BW]
                    dve.tensor_tensor(v, v, PS[:, 4 + (TT["down"] + m) % 4, :], ALU.add).then_inc(t_free, 1)
            layer_norm(3, 5, lambda t: dve.wait_ge(t_free, TT["down"] + 120 + t + 1))

            def mean_square(n, eps):
                settled()
                mark(dve.tensor_tensor(ve[:, 0:n], mv[:, 0:n, 0], mv[:, 0:n, 0], ALU.mult))
                settled()
                dve.scalar_tensor_tensor(ve[:, 0:n], ve[:, 0:n], eps, mv[:, 0:n, 1], ALU.add, ALU.add).then_inc(s("ln_stat"), 1)

            dve.wait_ge(s("modc_in"), 96)
            sh = COLS["sh1"][0]
            mark(dve.tensor_tensor(modc[:, 0:4, :], modc[:, 0:4, :], cols[:, sh:sh + 32].rearrange("p (a b) -> p a b", a=4), ALU.add))
            mark(dve.tensor_tensor(modc[:, 4:6, :], modc[:, 4:6, :], cols[:, sh:sh + 16].rearrange("p (a b) -> p a b", a=2), ALU.add))
            settled()
            for i, name in ((1, "pre_mix"), (3, "pre_ffn"), (5, "pre_mix")):
                ins = dve.scalar_tensor_tensor(modc[:, i, :], modc[:, i, :], 1.0, cols[:, COLS[name][0]:COLS[name][1]],
                                               ALU.add, ALU.mult)
                if i < 5:
                    mark(ins)
                else:
                    ins.then_inc(s("mod_ready"), 1)
            dve.wait_ge(s("ctx_in"), 16)
            for t in range(2):
                stats(t, ctxR[:, t, :], 2)
            mean_square(2, RMS_EPS)
            rstd(2, 6)
            for t in range(2):
                ins = dve.tensor_scalar(ctxR[:, t, :], ctxR[:, t, :], rs[:, t:t + 1], None, ALU.mult)
                if t == 0:
                    mark(ins)
                else:
                    ins.then_inc(s("ctx_rows"), 1)
            mark(dve.memset(ones[0:GR, :], 1.0))
            mark(dve.memset(ms[0:GR, :], 0.0))
            mark(dve.memset(mpc[0:GR, :], 0.0))
            mark(dve.memset(MM[0:GR, :], 0.0))
            settled()

            def gates(i, w, steps, ready):
                dve.wait_ge(f_free, ready)
                n = w // P
                g = slice(0, GR)
                mark(dve.tensor_scalar(tmp[g, 0:w], lf[g, 0:w], 0.0, None, ALU.min))
                settled()
                dve.scalar_tensor_tensor(bb[g, 0:w], tmp[g, 0:w], 2.0, lf[g, 0:w], ALU.mult, ALU.subtract).then_inc(s("g_a"), 1)
                dve.wait_ge(s("g_l"), i + 1)
                mark(dve.tensor_tensor(lf[g, 0:w], tmp[g, 0:w], enm[g, 0:w], ALU.subtract))
                mark(dve.memset(bb[g, 0:w], 0.0))
                settled()

                def piece(v, c, d):
                    x = v[32 * d:32 * d + 4, c * P:c * P + P]
                    return x[:, ::-1] if d else x

                for c, d in steps:
                    mark(dve.tensor_tensor_scan(piece(bb, c, d), piece(ones, 0, d), piece(lf, c, d), 0.0, ALU.mult, ALU.add))
                settled()
                mark(dve.tensor_tensor(uu[g, 0:w], li[g, 0:w], bb[g, 0:w], ALU.subtract))
                settled()
                for d in range(2):
                    c = [c for c, d2 in steps if d2 == d][0]
                    mark(dve.tensor_copy(mpc[32 * d:32 * d + 4, c:c + 1], ms[32 * d:32 * d + 4, :]))
                settled()
                for k in range(0, len(steps), 2):
                    for c, d in steps[k:k + 2]:
                        mark(dve.tensor_tensor_scan(piece(MM, c, d), piece(uu, c, d), piece(uu, c, d),
                                                    mpc[32 * d:32 * d + 4, c:c + 1], ALU.max, ALU.max))
                    settled()
                    for e, (c, d) in enumerate(steps[k:k + 2]):
                        last = c * P + (0 if d else P - 1)
                        if k + 2 < len(steps):
                            c2 = steps[k + 2 + e][0]
                            to = mpc[32 * d:32 * d + 4, c2:c2 + 1]
                        else:
                            to = ms[32 * d:32 * d + 4, :]
                        r = slice(32 * d, 32 * d + 4)
                        mark(dve.tensor_tensor(to, bb[r, last:last + 1], MM[r, last:last + 1], ALU.add))
                    settled()
                mark(dve.tensor_tensor(tmp[g, 0:w], bb[g, 0:w], MM[g, 0:w], ALU.add))
                for d in range(2):
                    r = slice(32 * d, 32 * d + 4)
                    end = MM[r, 0:w].rearrange("p (a b) -> p a b", b=P)[:, :, (0 if d else P - 1)]
                    ins = dve.tensor_tensor(lf[r, 0:w].rearrange("p (a b) -> p a b", b=P), uu[r, 0:w].rearrange("p (a b) -> p a b", b=P),
                                            over_last(end, P), ALU.subtract)
                    if d == 0:
                        mark(ins)
                    else:
                        ins.then_inc(s("g_b"), 1)

            def gate_columns(n, i):
                dve.wait_ge(s("g_t"), i + 1)
                for c in range(0, n, 4):
                    m = min(4, n - c)
                    mark(dve.tensor_copy(COL[:, c:c + m, :, :].rearrange("p a b c -> p (a b c)"), PS[:, c // 4, 0:m * 3 * GR]))
                dve.tensor_copy(MPB[:, :, 0:n], PS[:, 2, 0:2 * MH * NC].rearrange("p (a b) -> p a b", b=NC)[:, :, 0:n]).then_inc(s("g_c"), 1)

            def scan(steps, i0, outs):
                for idx, (c, d) in enumerate(steps):
                    i, j = i0 + idx, idx
                    if outs:
                        dve.wait_ge(s("m_w"), i + 1)
                        if j >= 1:
                            dve.wait_ge(s("m_pt"), j)
                        dve.scalar_tensor_tensor(DD[:, j % 2, :].rearrange("p (a b) -> p a b", a=MH),
                                                 PS[:, 0, :].rearrange("p (a b) -> p a b", a=MH), -1.0,
                                                 over_mid(MASK[:, d, :], MH), ALU.mult, ALU.add).then_inc(s("m_arg"), 1)
                        dve.wait_ge(s("m_e"), j + 1)
                        dve.wait_ge(s("m_st"), j + 1)
                        if j >= 2:
                            dve.wait_ge(s("m_n"), j - 1)
                        dve.tensor_tensor(PP[:, j % 2, :], PS[:, 1, :], DD[:, j % 2, :], ALU.mult).then_inc(s("m_pt"), 1)
                        dve.wait_ge(s("m_n"), j + 1)
                        dn0, dn1 = dn[:, 0, :], dn[:, 1, :]
                        if j >= 1:
                            dve.wait_ge(s("m_h"), j)
                        mark(dve.tensor_copy(dn0, PS[:, 2:6, DV]))
                        settled()
                        mark(dve.scalar_tensor_tensor(dn1, dn0, -1.0, dn0, ALU.mult, ALU.max))
                        settled()
                        mark(dve.tensor_tensor(dn1, dn1, COL[:, c, 1, 32 * d:32 * d + 4], ALU.max))
                        settled()
                        mark(dve.reciprocal(dn0, dn1))
                        settled()
                        first = (d == 0) == (c < NC // 2)
                        for h in range(MH):
                            o = Q[:, c, DV * h:DV * h + DV]
                            if first:
                                ins = dve.tensor_scalar(o, PS[:, 2 + h, 0:DV], dn0[:, h:h + 1], None, ALU.mult)
                            else:
                                ins = dve.scalar_tensor_tensor(o, PS[:, 2 + h, 0:DV], dn0[:, h:h + 1], o, ALU.mult, ALU.add)
                            if h < MH - 1:
                                mark(ins)
                            else:
                                ins.then_inc(s("m_h"), 1)
                    dve.wait_ge(s("m_w"), i + 1)
                    if i == 0:
                        dve.wait_ge(s("c_zero"), 1)
                    else:
                        dve.wait_ge(s("m_cu"), 2 * i)
                    for pair in range(2):
                        dve.wait_ge(s("m_d"), 2 * i + pair + 1)
                        for h in (2 * pair, 2 * pair + 1):
                            cc = CC[:, d * MH + h, :]
                            last = h * P + (0 if d else P - 1)
                            ins = dve.scalar_tensor_tensor(cc, cc, WI[:, i % 2, last:last + 1], PS[:, 6 + h % 2, 0:V1],
                                                           ALU.mult, ALU.add)
                            if h % 2 == 0:
                                mark(ins)
                            else:
                                ins.then_inc(s("m_cu"), 1)

            gates(0, MEM, CTX_STEPS, FT["cg"] + 2)
            dve.wait_ge(s("rows2_in"), 32)
            mark(dve.tensor_scalar(krow, krow, DK ** -0.5, None, ALU.mult))
            settled()

            def keys(name, dst, tiles):
                for t in range(tiles):
                    n = TT[name] + t
                    dve.wait_ge(t_ready, n + 1)
                    dve.scalar_tensor_tensor(dst[:, t, :], PS[:, 4 + n % 4, :], DK ** -0.5, krow, ALU.mult, ALU.add).then_inc(t_free, 1)

            def values(name, dst, tiles):
                for j in range(2):
                    for t in range(tiles):
                        n = TT[name] + tiles * j + t
                        dve.wait_ge(t_ready, n + 1)
                        dve.tensor_tensor(dst[:, t, 2 * j:2 * j + 2, 0:DV], PS[:, 4 + n % 4, :].rearrange("p (a b) -> p a b", a=2),
                                          ROW[:, 2, BW * j:BW * j + BW].rearrange("p (a b) -> p a b", a=2), ALU.add).then_inc(t_free, 1)

            keys("ck", KX, 2)
            values("cv", VX, 2)
            gate_columns(2, 0)
            scan(CTX_STEPS, 0, False)
            dve.wait_ge(s("x_out"), 32)
            for t in range(NT):
                stats(t, XR[:, t, :], 2)
            mean_square(NT, RMS_EPS)
            rstd(NT, 7)
            for t in range(NT):
                dve.tensor_scalar(XR[:, t, :], XR[:, t, :], rs[:, t:t + 1], None, ALU.mult).then_inc(s("xr_norm"), 1)
            gates(1, T, X_STEPS, FT["mg"] + 4)
            keys("mk", KK, NT)
            dve.wait_ge(s("rows2_in"), 48)
            values("mv", VV, NT)
            gate_columns(NC, 1)
            scan(X_STEPS, 4, True)
            dve.wait_ge(s("m_h"), 16)
            for t in range(NT):
                for h in range(MH):
                    mark(dve.bn_stats(st[:, MH * t + h, :], Q[:, t, DV * h:DV * h + DV]))
            settled()
            for i in range(32):
                mark(dve.bn_aggr(mv[:, i, :], st[:, i, :]))
            mean_square(32, RMS_EPS)
            rstd(32, 8)
            for t in range(NT):
                for h in range(MH):
                    v = Q[:, t, DV * h:DV * h + DV]
                    mark(dve.tensor_scalar(v, v, rs[:, MH * t + h:MH * t + h + 1], None, ALU.mult))
            dve.wait_ge(rows2_v, 80)
            settled()
            for t in range(NT):
                mark(dve.tensor_tensor(Q[:, t, :], Q[:, t, :], ROW[:, 2, :], ALU.mult))
            for m in range(17):
                if m < 16:
                    n = TT["mo"] + m
                    dve.wait_ge(t_ready, n + 1)
                    if m >= 2:
                        dve.wait_ge(s("o_y"), m - 1)
                    dve.tensor_tensor(OG[:, m % 2, :], PS[:, 4 + n % 4, :], ROW[:, 0, BW * (m // 8):BW * (m // 8) + BW],
                                      ALU.add).then_inc(t_free, 1)
                if m >= 1:
                    j, t = (m - 1) // 8, (m - 1) % 8
                    dve.wait_ge(s("o_s"), m)
                    if m == 1:
                        settled()
                    v = Q[:, t, BW * j:BW * j + BW]
                    dve.tensor_tensor(v, v, OG[:, (m - 1) % 2, :], ALU.mult).then_inc(s("o_y"), 1)

            def copy_out(name):
                for j in range(2):
                    for t in range(NT):
                        n = TT[name] + 8 * j + t
                        dve.wait_ge(t_ready, n + 1)
                        dve.tensor_copy(Q[:, t, BW * j:BW * j + BW], PS[:, 4 + n % 4, :]).then_inc(t_free, 1)

            def branch_norm(r, rows_at, ready):
                dve.wait_ge(rows2_v, rows_at)
                mark(dve.tensor_tensor(ROW[:, 0, :], ROW[:, 0, :], ROW[:, 1, :], ALU.add))
                settled()
                dve.tensor_tensor(ROW[:, 0, :], ROW[:, 0, :], ROW[:, 2, :], ALU.mult).then_inc(s("gate_row"), 1)
                for t in range(NT):
                    dve.wait_ge(t_free, ready + t + 1)
                    stats(t, Q[:, t, :], 2)
                mean_square(NT, RMS_EPS)
                rstd(NT, r)
                for t in range(NT):
                    dve.tensor_scalar(Q[:, t, :], Q[:, t, :], rs[:, t:t + 1], None, ALU.mult).then_inc(s("b_norm"), 1)

            copy_out("mout")
            branch_norm(9, 128, TT["mout"] + 8)
            for t in range(NT):
                dve.wait_ge(s("x_new"), t + 1)
                stats(t, XR[:, t, :], 2)
            mean_square(NT, RMS_EPS)
            rstd(NT, 10)
            for t in range(NT):
                dve.tensor_scalar(XN[:, t, :], XR[:, t, :], rs[:, t:t + 1], None, ALU.mult).then_inc(s("xn_norm"), 1)

            for i in range(16):
                dve.wait_ge(f_free, FT["xtf"] + i + 1)
                dve.tensor_copy(X_HI[:, i % KC, BW * (i // KC):BW * (i // KC) + BW], XS[:, i % 4, :]).then_inc(s("xf_hi"), 1)

            def rows_of(v):
                return v.rearrange("p (a b) -> p a b", b=GRID)

            def group2(g, n_chunks):
                for c in range(n_chunks):
                    dve.wait_ge(f_free, g * 16 + (FT["up2"] + 4 * c + 4))
                    k = cw[:, c, :]
                    src, dst = rows_of(GG[:, c % 2, :]), rows_of(TC[:, c % 2, :])
                    dve.tensor_scalar(dst, src, k[:, 1:2], k[:, 3:4], ALU.mult, ALU.add).then_inc(s("taps"), 1)
                    dve.wait_ge(s("taps"), g * 8 + (2 * c + 1))
                    dve.scalar_tensor_tensor(dst[:, :, 1:], src[:, :, :-1], k[:, 0:1], dst[:, :, 1:], ALU.mult, ALU.add).then_inc(s("taps"), 1)
                    dve.wait_ge(s("taps"), g * 8 + (2 * c + 2))
                    dve.scalar_tensor_tensor(dst[:, :, :-1], src[:, :, 1:], k[:, 2:3], dst[:, :, :-1], ALU.mult, ALU.add).then_inc(s("conv"), 1)
                    dve.wait_ge(s("gated"), g * 4 + (c + 1))
                    dve.tensor_copy(H_HI[:, c, :], TC[:, c % 2, :]).then_inc(s("h2_hi"), 1)
                    dve.wait_ge(s("h2_hi"), g * 4 + (c + 1))
                    dve.tensor_tensor(H_LO[:, c, :], TC[:, c % 2, :], H_HI[:, c, :], ALU.subtract).then_inc(s("hidden"), 1)
                for m in range(16):
                    n = TT["down2"] + m
                    dve.wait_ge(t_ready, g * 16 + (n + 1))
                    v = Q[:, m % 8, BW * (m // 8):BW * (m // 8) + BW]
                    dve.tensor_tensor(v, v, PS[:, 4 + n % 4, :], ALU.add).then_inc(t_free, 1)

            dve.wait_ge(s("y_zero"), 1)
            with dve.Fori(0, N_G) as g:
                group2(g, 4)
            group2(N_G, 2)
            branch_norm(11, 176, TT["down2"] + 16 * N_G + 8)

        @block.gpsimd
        def _(pool):
            pool.memset(relb[0:NB + 1, :], 1.0).then_inc(s("relb_one"), 1)
            pool.memset(ident[:, :], 0.0).then_inc(s("pool_c"), 1)
            pool.wait_ge(s("pool_c"), 1)
            pool.affine_select(out=ident[:, :], in_=ident[:, :], compare_op=ALU.not_equal, fill=1.0, base=0,
                               pattern=[[-1, P]], channel_multiplier=1).then_inc(s("ident_ok"), 1)

            def offset(i):
                pool.wait_ge(rows_in, 32 + 48 * i)
                for t in range(NT):
                    pool.wait_ge(s("ln_half"), NT * i + t + 1)
                    pool.tensor_tensor(XR[:, t, :], XR[:, t, :], ROW[:, 1, :], ALU.add).then_inc(s("ln_done"), 1)
            offset(0)
            for n in range(2, NT):
                pool.wait_ge(s("ix_s"), NH * (n - 1))
                v = score[:, n * P:n * P + P]
                pool.affine_select(out=v, in_=v, compare_op=ALU.is_ge, fill=NEG, base=0,
                                   pattern=[[-1, P]], channel_multiplier=1).then_inc(s("ix_c"), 1)
            offset(1)
            offset(2)
            pool.wait_ge(s("x_oe"), NT)
            for i in range(4):
                pool.memset(RU[:, i, :], 0.0).then_inc(s("hidden1"), 1)

            def low(buf, at, width=4 * BW):
                pool.wait_ge(s("w_hi"), at)
                pool.tensor_tensor(WLO[buf][:, 0:width], WRAW[buf][:, 0:width], WHI[buf][:, 0:width], ALU.subtract).then_inc(s("w_lo"), 1)

            with pool.Fori(0, N_UP) as g:
                def square(m):
                    pool.wait_ge(f_free, g * 8 + (FT["up"] + m + 1))
                    v = RU[:, m % 4, :]
                    pool.tensor_tensor(v, v, v, ALU.mult).then_inc(s("squared"), 1)

                low(0, g * 4 + 1)
                for m in (0, 1):
                    square(m)
                low(1, g * 4 + 2)
                for m in (2, 3, 4, 5):
                    square(m)
                low(0, g * 4 + 3)
                for m in (6, 7):
                    square(m)
                low(1, g * 4 + 4)
            offset(3)
            pool.wait_ge(s("ln_done"), 4 * NT)
            pool.memset(GW, 0.0).then_inc(s("gw_zero"), 1)
            pool.memset(gb[0:GR, :], 0.0).then_inc(s("gw_zero"), 1)
            pool.memset(SEL[0:GR, :, :], 0.0).then_inc(s("pool_c"), 1)
            pool.memset(MASK, 0.0).then_inc(s("pool_c"), 1)
            pool.wait_ge(s("pool_c"), 3)
            pool.affine_select(out=SEL[0:GR, :, :], in_=SEL[0:GR, :, :], compare_op=ALU.not_equal, fill=1.0, base=0,
                               pattern=[[-32, 2], [-1, MH], [0, P]], channel_multiplier=1).then_inc(s("pool_c"), 1)
            pool.affine_select(out=MASK[:, 0, :], in_=MASK[:, 0, :], compare_op=ALU.is_ge, fill=NEG, base=0,
                               pattern=[[1, P]], channel_multiplier=-1).then_inc(s("pool_c"), 1)
            pool.affine_select(out=MASK[:, 1, :], in_=MASK[:, 1, :], compare_op=ALU.is_ge, fill=NEG, base=0,
                               pattern=[[-1, P]], channel_multiplier=1).then_inc(s("pool_c"), 1)
            pool.memset(CC, 0.0).then_inc(s("c_zero"), 1)
            pool.memset(VX[:, :, :, DV:V1], 1.0).then_inc(s("v_one"), 1)

            def scan(steps, i0, outs, K):
                for idx, (c, d) in enumerate(steps):
                    i, j = i0 + idx, idx
                    if i >= 2:
                        pool.wait_ge(s("m_d"), 2 * i - 2)
                    pool.tensor_tensor(KS[:, i % 2, :].rearrange("p (a b) -> p a b", a=MH), K[:, c, :].rearrange("p (a b) -> p a b", a=MH),
                                       over_last(COL[:, c, 2, 32 * d:32 * d + 4], DK), ALU.mult).then_inc(s("m_ks"), 1)
                    if outs:
                        pool.wait_ge(s("m_w"), i + 1)
                        if j >= 2:
                            pool.wait_ge(s("m_n"), j - 1)
                        pool.tensor_tensor(QS[:, j % 2, :].rearrange("p (a b) -> p a b", a=MH), qT[:, :, c * P:c * P + P],
                                           WI[:, i % 2, :].rearrange("p (a b) -> p a b", a=MH), ALU.mult).then_inc(s("m_qs"), 1)

            pool.wait_ge(s("g_c"), 1)
            pool.wait_ge(t_free, TT["mk"])
            scan(CTX_STEPS, 0, False, KX)
            pool.wait_ge(s("m_d"), 8)
            pool.wait_ge(f_ready, FT["mg"] + 4)
            pool.memset(VV[:, :, :, DV:V1], 1.0).then_inc(s("v_one"), 1)
            pool.wait_ge(s("g_c"), 2)
            pool.wait_ge(t_free, TT["mo"])
            scan(X_STEPS, 4, True, KK)

            def add_branch(i):
                pool.wait_ge(s("gate_row"), i + 1)
                for t in range(NT):
                    pool.wait_ge(s("b_norm"), NT * i + t + 1)
                    pool.tensor_tensor(Q[:, t, :], Q[:, t, :], ROW[:, 0, :], ALU.mult).then_inc(s("b_gain"), 1)
                    pool.wait_ge(s("b_gain"), NT * i + t + 1)
                    pool.tensor_tensor(XR[:, t, :], XR[:, t, :], Q[:, t, :], ALU.add).then_inc(s("x_new"), 1)

            pool.wait_ge(s("x_back"), 32)
            add_branch(0)
            for i in range(2):
                pool.memset(R[:, 14400 + i:14401 + i], 0.0).then_inc(s("hidden"), 1)
            pool.wait_ge(s("x_new"), NT)
            pool.memset(Q[:, :, :], 0.0).then_inc(s("y_zero"), 1)

            pool.wait_ge(s("x_out2"), 16 * NT)
            pool.wait_ge(s("xn_norm"), NT)
            for i in range(16):
                pool.wait_ge(s("xf_hi"), i + 1)
                v = (slice(None), i % KC, slice(BW * (i // KC), BW * (i // KC) + BW))
                pool.tensor_tensor(X_LO2[v], XS[:, i % 4, :], X_HI[v], ALU.subtract).then_inc(s("xf_lo"), 1)

            def gate2(g, c):
                pool.wait_ge(s("silu"), g * 4 + (c + 1))
                pool.tensor_tensor(TC[:, c % 2, :], TC[:, c % 2, :], UU[:, c % 2, :], ALU.mult).then_inc(s("gated"), 1)

            W0 = 4 * N_UP
            with pool.Fori(0, N_G) as g:
                low(1, g * 6 + (W0 + 1))
                low(0, g * 6 + (W0 + 2))
                for c in range(4):
                    gate2(g, c)
                    if c < 3:
                        low(1 - c % 2, g * 6 + (W0 + 3 + c))
                low(0, g * 6 + (W0 + 6))
            W0 += 6 * N_G
            low(1, W0 + 1)
            low(0, W0 + 2)
            gate2(N_G, 0)
            low(1, W0 + 3, 2 * BW)
            gate2(N_G, 1)
            low(0, W0 + 4, 2 * BW)
            pool.wait_ge(s("x_back2"), 32)
            add_branch(1)


def host_layout(inputs):
    a = {k: np.ascontiguousarray(v) for k, v in inputs.items() if np.asarray(v).size}

    def col(v):
        return v.reshape(-1, P).T

    b_in, ada_b = a["b_in"][0], a["ada_b_2"][0]
    parts = {"qa": col(b_in[0:512]), "qb": col(b_in[768:1280]), "iq": col(b_in[1408:1920]), "ka": col(b_in[512:640]),
             "xq": col(a["xa_bq"][0]), "xk": col(a["xa_bkv"][0, :D]), "mq": col(a["m_in_b_2"][0, :512]),
             "pre_mix": col(a["pre_mix_g_2"][0]), "pre_ffn": col(a["pre_ffn_g_2"][0]),
             "sh1": col(ada_b[0:D]), "sc1": col(ada_b[D:2 * D]), "sh2": col(ada_b[3 * D:4 * D]), "sc2": col(ada_b[4 * D:5 * D]),
             "c": np.stack([col(a["c_2"][0]), col(a["c_ctx_2"])], -1).reshape(P, 16)}
    a["cols_h"] = np.ascontiguousarray(np.concatenate([parts[k] for k in COLS], 1))
    dist = 2 * P - 1 - np.arange(N_BIAS)
    near = np.maximum(dist, 0)
    exact = NB // 2
    far = exact + (np.log(np.maximum(near, 1) / exact) / np.log(MAXD / exact) * (NB - exact) + 1e-6).astype(np.int64)
    bucket = np.where(near < exact, near, np.minimum(far, NB - 1))
    hot = np.zeros((NB + 1, 2, N_BIAS), np.float32)
    hot[bucket, :, np.arange(N_BIAS)] = 1.0
    hot[NB, 0] = np.where((dist < 0) | (dist >= P), NEG, 0.0)
    hot[NB, 1] = np.where(dist < 0, NEG, 0.0)
    a["hot_h"] = hot
    a["bup_h"] = np.ascontiguousarray(a["b_up"][0].reshape(16, 2, P).transpose(0, 2, 1))
    conv = np.concatenate([a["ffn_conv_w_2"][0], a["ffn_conv_b_2"]], 0)
    a["conv_h"] = np.ascontiguousarray(conv.reshape(4, -1, P).transpose(1, 2, 0))
    return a


def kernel(**inputs):
    import concourse.bacc as bacc
    from concourse.bass_utils import run_bass_kernel_spmd

    arrays = host_layout(inputs)
    nc = bacc.Bacc("TRN2", target_bir_lowering=False, num_devices=1)
    aps = {n: nc.dram_tensor(f"in_{n}_dram", v.shape, mybir.dt.from_np(v.dtype), kind="ExternalInput").ap()
           for n, v in arrays.items()}
    out = nc.dram_tensor("out_dram", (1, T, D), F32, kind="ExternalOutput").ap()
    build_program(nc, aps, out)
    r = run_bass_kernel_spmd(nc, [{f"in_{n}_dram": v for n, v in arrays.items()}], core_ids=[0])
    return r.results[0]["out_dram"]
```

```python
from contextlib import ExitStack

import numpy as np

import concourse.bass as bass
from concourse import mybir

F32 = mybir.dt.float32
F32R = mybir.dt.float32r
ALU = mybir.AluOpType
ACT = mybir.ActivationFunctionType
AX = mybir.AxisListType

P = 128
D = 1024
T = 1024
NT = T // P
KC = D // P
MEM = 256
DH = 64
NH = 8
RANK = 128
TOPK = 256
XH, XD = 4, 256
FF = 4096
FF2 = 2816
GRID = 64
MH, DK, DV = 4, 128, 256
NB = 32
MAXD = 128
NEG = -1.0e30
TAKEN = -3.0e38
ALPHA = 2.0 ** 0.25
LN_EPS, RMS_EPS = 1e-5, 1e-6
BW = 512
N_BIAS = 3 * P
ADA_W = 256
ADA_N = 6 * D // NT
MISC = 2 * P + DH + NH

COLS = {}
_at = 0
for _name, _n in (("qa", 4), ("qb", 4), ("iq", 4), ("ka", 1), ("xq", 8), ("xk", 8), ("mq", 4),
                  ("pre_mix", 8), ("pre_ffn", 8), ("sh1", 8), ("sc1", 8), ("sh2", 8), ("sc2", 8),
                  ("c", 16)):
    COLS[_name] = (_at, _at + _n)
    _at += _n
N_COLS = _at


def bases(*stages):
    at, out = 0, {}
    for name, n in stages:
        out[name] = at
        at += n
    out["end"] = at
    return out


FT = bases(("vb", 2), ("xt0", 16), ("qa", 8), ("qb", 8), ("iq", 8), ("ka", 2), ("ukT", 1),
           ("ckT", 4), ("memT", 4), ("xk", 8), ("xt1", 16), ("xq", 16), ("xt2", 16),
           ("up", 64), ("ctxT", 4), ("cg", 2), ("xtm", 16), ("mg", 4), ("mq", 8), ("kT", 8),
           ("yT", 16), ("xtf", 16), ("up2", 88))
TT = bases(("misc", 8), ("wo", 32), ("xv", 4), ("xo", 32), ("down", 128), ("ck", 2), ("cv", 4),
           ("mk", 8), ("mv", 16), ("mo", 16), ("mout", 32), ("down2", 96))


def build_program(nc, I, out):
    with ExitStack() as ctx:
        def sb(name, shape, dt=F32):
            return ctx.enter_context(nc.sbuf_tensor(name, shape, dt))

        def sb_twice(name, shape):
            at = (nc.sbuf_base + 31) // 32 * 32
            t = sb(name, shape)
            assert nc.sbuf_base == at + 4 * int(np.prod(shape[1:]))
            return t, nc.alloc_sbuf_tensor_at(name + "_parts", shape, F32R, offset=at)

        def sem(name):
            return ctx.enter_context(nc.semaphore(name))

        mods_d = nc.dram_tensor("mods_scratch", (2, 6 * D), F32, kind="Internal").ap()
        bias_d = nc.dram_tensor("bias_scratch", (2 * NH, P, N_BIAS), F32, kind="Internal").ap()
        x_d = nc.dram_tensor("x_scratch", (P, NT * D), F32, kind="Internal").ap()

        XR, XR_r = sb_twice("x_rows", [P, NT, D])
        XT, XT_r = sb_twice("x_cols", [P, KC, T])
        WB, WB_r = zip(*[sb_twice(f"weights{i}", [P, KC, BW]) for i in range(2)])
        Q, Q_r = sb_twice("wide", [P, 8, T])
        ROW = sb("rows", [P, 3, D])
        R, R_r = sb_twice("region", [P, 15936])
        ident = sb("ident", [P, P])
        cols = sb("cols", [P, N_COLS])
        modc = sb("modc", [P, 6, KC])
        st = sb("stats", [P, 32, 6])
        mv = sb("mean_var", [P, 32, 2])
        ve = sb("var_eps", [P, 32])
        sdv = sb("std", [P, 32])
        rs = sb("rstd", [P, 32])
        PS = ctx.enter_context(nc.psum_tensor("psum", [P, 8, BW], F32))
        PSf = PS[:, :, :].rearrange("p a b -> p (a b)")

        def view(base, at, shape):
            n = int(np.prod(shape))
            v = base[:, at:at + n]
            if len(shape) == 1:
                return v
            if len(shape) == 2:
                return v.rearrange("p (a b) -> p a b", a=shape[0])
            return v.rearrange("p (a b c) -> p a b c", a=shape[0], b=shape[1])

        def over_last(v, n):
            return v.unsqueeze(2).to_broadcast([v.shape[0], v.shape[1], n])

        def over_mid(v, n):
            return v.unsqueeze(1).to_broadcast([v.shape[0], n, v.shape[1]])

        XTf = XT[:, :, :].rearrange("p a b -> p (a b)")
        XRf = XR[:, :, :].rearrange("p a b -> p (a b)")
        Qf = Q[:, :, :].rearrange("p a b -> p (a b)")
        ROWf = ROW[:, :, :].rearrange("p a b -> p (a b)")
        stf = st[:, :, :].rearrange("p a b -> p (a b)")

        iqT = view(R, 0, (4, T))
        kaT = view(R, 4096, (2, T))
        ikT = view(R, 6144, (T,))
        cT = view(R, 7168, (T,))
        cR = view(R, 8192, (NT, RANK))
        misc = view(R, 9216, (NT, MISC))
        SB = view(R, 11840, (NH, 2 * P))
        LG = view(R, 11840, (2, T))
        PT = view(R, 13888, (16, P))
        RL = view(R, 13888, (2, T))
        bias = view(XTf, 0, (16, 2 * P))
        OL = view(XTf, 4096, (NH, P))
        score = view(XTf, 5120, (T,))
        work = view(XTf, 6144, (T,))
        QL = view(XTf, 7168, (NH, P))
        WB1f = WB[1][:, :, :].rearrange("p a b -> p (a b)")
        WB0f = WB[0][:, :, :].rearrange("p a b -> p (a b)")
        msk = view(WB1f, 0, (2, T))
        modr = view(WB1f, 2 * T, (2, ADA_N))
        adaw = view(WB0f, 0, (2, KC, ADA_W))
        wuk = view(ROWf, 0, (NH, DH))
        wukT = view(ROWf, 512, (4, P))
        wuv = view(ROWf, 1024, (NH, DH))
        mrow = view(ROWf, 1536, (MISC,))
        kvg = view(ROWf, 1864, (RANK,))
        ikg = view(ROWf, 1992, (2, DH))
        far = view(ROWf, 2120, (NH,))
        sink = view(ROWf, 2128, (NH,))
        mx = view(ROWf, 2136, (NH,))
        nm = view(ROWf, 2144, (NH,))
        den = view(ROWf, 2152, (NH,))
        sd = view(ROWf, 2160, (NH,))
        es = view(ROWf, 2168, (NH,))
        top = view(ROWf, 2176, (8,))
        iwt = view(ROWf, 2184, (NT, NH))
        hot = view(R, 15024, (2, N_BIAS))
        cx = sb("cond", [P, KC, 2])
        relb = view(R, 11840, (2 * NH,))
        vb = view(R, 11904, (2, N_BIAS))
        ikn = view(R, 12700, (NT, 2 * DH))
        kaS = view(R, 14000, (2, BW))

        memR = view(R, 0, (2, D))
        memT = view(R, 2048, (KC, MEM))
        xkT = view(R, 4096, (KC, MEM))
        xv = view(R, 6144, (2, D))
        XP = view(R, 8192, (2, XH * MEM))
        XPT = view(R, 10240, (2, 8 * P))
        vrow = view(R, 13312, (D,))
        upb = view(R, 14336, (2, 2))
        WBr_f = [w[:, :, :].rearrange("p a b -> p (a b)") for w in WB_r]
        WRAW = [view(w, 0, (4 * BW,)) for w in (WB0f, WB1f)]
        WLO = [view(w, 0, (4 * BW,)) for w in WBr_f]
        WHI = [view(w, 4 * BW, (4 * BW,)) for w in WBr_f]
        X_HI = XT_r
        X_LO1 = Q_r
        X_LO2 = XR_r
        H_HI = view(R_r, 0, (4, T))
        H_LO = view(R_r, 4096, (4, T))
        X_LO3 = view(R_r, 0, (KC, T))
        X_LO0 = [view(R_r, at + k * T, (T,)) for at, ks in ((0, 4), (8192, 4)) for k in range(ks)]
        Q_HI, Q_LO = X_HI, X_LO1
        HALF = BW // 2
        RU = view(R, 8192, (4, BW))

        xm = view(R, 14344, (2, XH))
        xn = view(R, 14352, (2, XH))
        xd = view(R, 14360, (2, XH))

        NC = NT
        V1 = DV + 1
        GR = 36
        ctxR = view(R, 11392, (2, D))
        hcT = view(R, 2048, (KC, MEM))
        KX = view(R, 4096, (2, MH * DK))
        VX = view(R, 5120, (2, MH, V1))
        GW = view(R, 10240, (KC, 2, GR))
        VV = view(R, 0, (NC, MH, V1))
        KK = view(R, 8224, (NC, MH * DK))
        CC = view(R, 12320, (2 * MH, V1))
        COL = view(R, 14376, (NC, 3, GR))
        MPB = view(R, 15240, (2 * MH, NC))
        MASK = view(R, 15304, (2, P))
        gb = view(R, 15560, (2,))
        ms = view(R, 15562, (1,))
        mpc = view(R, 15563, (NC,))
        dn = view(R, 15571, (2, MH))
        li, lf, bb, uu, tmp, enm, wsr = [view(Qf, i * T, (T,)) for i in range(7)]
        ones = view(Qf, 7 * T, (P,))
        krow = view(Qf, 7 * T + BW, (BW,))
        MM = ROW[:, 0, :]
        SEL = view(ROWf, T, (2 * MH, P))
        KS = view(ROWf, 2 * T, (2, BW))
        DD = view(WB0f, 0, (2, BW))
        PP = view(WB0f, 1024, (2, BW))
        WI = view(WB0f, 2048, (2, BW))
        QS = view(WB0f, 3072, (2, BW))
        qT = view(XRf, 0, (MH, T))
        kT = view(XRf, 4 * T, (MH, T))
        OG = view(ROWf, T, (2, BW))

        XN = view(R, 0, (NT, D))
        UU = view(R, 8192, (2, T))
        GG = view(R, 10240, (2, T))
        TC = view(R, 12288, (2, T))
        cw = view(R, 14336, (4, 4))
        XS = view(R, 12288, (4, BW))

        S = {}

        def s(name):
            if name not in S:
                S[name] = sem(name)
            return S[name]

        f_ready, f_free, t_ready, t_free = s("f_ready"), s("f_free"), s("t_ready"), s("t_free")
        w_in = [s("w_in0"), s("w_in1")]
        rows_in, cols_in, own_dve, own_act = s("rows_in"), s("cols_in"), s("own_dve"), s("own_act")

        def cols_of(w, a, b):
            return w[:, a:b].rearrange("(k p) n -> p k n", p=P)

        w_in_w = I["w_in"][0]
        fine = []
        blocks = []

        def block_of(pieces, done_sem, done_at):
            blocks.append((pieces, done_sem, done_at))

        for name, a in (("qa", 0), ("qb", 768), ("iq", 1408)):
            block_of([(0, BW, cols_of(w_in_w, a, a + BW))], f_ready, FT[name] + 8)
        block_of([(0, 256, cols_of(w_in_w, 512, 768)), (256, 384, cols_of(w_in_w, 1280, 1408)),
                  (384, 456, cols_of(w_in_w, 1920, 1992))], t_ready, TT["misc"] + 8)
        WO0 = len(blocks)

        def fine_blocks(w, sem_, at, tiles):
            for j in range(4):
                fine.append(len(blocks))
                block_of([cols_of(w, 256 * j, 256 * j + 256)], sem_, at + tiles * (j + 1))

        fine_blocks(I["w_o"][0], t_ready, TT["wo"], 8)

        for name, w, a0, n, ds_, tiles in (("xk", "xa_wkv", 0, 2, f_ready, 4), ("xv", "xa_wkv", D, 2, t_ready, 2)):
            for j in range(n):
                block_of([(0, BW, cols_of(I[w][0], a0 + BW * j, a0 + BW * j + BW))], ds_,
                         (FT if ds_ is f_ready else TT)[name] + tiles * (j + 1))
        XQ0 = len(blocks)
        fine_blocks(I["xa_wq"][0], f_ready, FT["xq"], 4)
        XO0 = len(blocks)
        fine_blocks(I["xa_wo"][0], t_ready, TT["xo"], 8)
        UP0 = len(blocks)
        N_UP = FF // BW
        for g in range(N_UP):
            for j in range(2):
                block_of([None, None], f_ready, FT["up"] + 8 * g + 4 * j + 4)
            for j in range(2):
                block_of([None], t_ready, TT["down"] + 16 * g + 8 * j + 8)
        assert UP0 % 2 == 0
        M0 = len(blocks)
        m_w = I["m_in_w_2"][0]
        for name, a0, n, ds_, tiles in (("ck", 512, 1, t_ready, 2), ("cv", 1024, 2, t_ready, 2), ("mq", 0, 1, f_ready, 8),
                                        ("mk", 512, 1, t_ready, 8), ("mv", 1024, 2, t_ready, 8), ("mo", 2048, 2, t_ready, 8)):
            for j in range(n):
                block_of([(0, BW, cols_of(m_w, a0 + BW * j, a0 + BW * j + BW))], ds_,
                         (FT if ds_ is f_ready else TT)[name] + tiles * (j + 1))
        MO0 = len(blocks)
        fine_blocks(I["m_out_w_2"][0], t_ready, TT["mout"], 8)
        G0 = len(blocks)
        assert G0 % 2 == 1
        N_G = FF2 // BW
        for g in range(N_G):
            for n in (3, 3, 3, 3, 1, 1):
                block_of([None] * n, f_ready, 0)
        for n in (3, 3, 1, 1):
            block_of([None] * n, f_ready, 0)

        F1, F2 = fine.index(MO0), len(fine) + 4 * N_UP

        def split_count(b):
            return fine.index(b) + 1 + (4 * N_UP if b >= MO0 else 0)

        def loaded(b):
            return 16 * sum(len(p) for i, (p, _, _) in enumerate(blocks[:b + 1]) if i % 2 == b % 2)

        CTX_STEPS = [(c if d == 0 else 1 - c, d) for c in range(2) for d in range(2)]
        X_STEPS = [(c if d == 0 else NC - 1 - c, d) for c in range(NC) for d in range(2)]

        block = ctx.enter_context(nc.Block())

        @block.sync
        def _(sp):
            for t in range(NT):
                sp.dma_start(XR[:, t, :], I["x"][0, t * P:t * P + P, :]).then_inc(s(f"x_in{t}"), 16)

            def load(b):
                if b >= 2:
                    sp.wait_ge(blocks[b - 2][1], blocks[b - 2][2])
                if b in fine:
                    sp.dma_start(WRAW[b % 2].rearrange("p (k n) -> p k n", k=KC), blocks[b][0][0]).then_inc(w_in[b % 2], 16)
                    return
                for a, z, src in blocks[b][0]:
                    sp.dma_start(WB[b % 2][:, :, a:z], src).then_inc(w_in[b % 2], 16)

            for b in range(WO0):
                load(b)
            sp.wait_ge(f_ready, FT["iq"] + 8)
            for n in range(NT):
                for j in range(ADA_N // ADA_W * n, ADA_N // ADA_W * (n + 1)):
                    if j >= 2:
                        sp.wait_ge(s("ada_mm"), j - 1)
                    sp.dma_start(adaw[:, j % 2], cols_of(I["ada_w_2"][0], ADA_W * j, ADA_W * j + ADA_W)).then_inc(s(f"ada_in{j % 2}"), 16)
                if n > 0:
                    sp.wait_ge(s("ada_e"), n)
                    sp.dma_start(mods_d[:, ADA_N * (n - 1):ADA_N * n], modr[0:2, (n - 1) % 2, :]).then_inc(s(f"mods_out{(n - 1) % 2}"), 16)
            sp.wait_ge(s("ada_e"), NT)
            sp.dma_start(mods_d[:, ADA_N * (NT - 1):6 * D], modr[0:2, (NT - 1) % 2, :]).then_inc(s(f"mods_out{(NT - 1) % 2}"), 16)
            load(WO0)
            for j in range(2):
                sp.wait_ge(s(f"mods_out{j}"), 64)
            for i, (row, part) in enumerate(((0, 0), (0, 1), (0, 3), (0, 4), (1, 0), (1, 1))):
                sp.dma_start(modc[:, i, :], mods_d[row, D * part:D * part + D].rearrange("(k p) -> p k", p=P),
                             allow_slow_non_contiguous=True).then_inc(s("modc_in"), 16)
            sp.wait_ge(s("d_fe"), NT)
            load(WO0 + 1)
            sp.dma_start(memR, I["mem"][0].rearrange("(t p) d -> p t d", p=P)).then_inc(s("mem_in"), 16)
            sp.dma_start(vrow, I["xa_bkv"][0, D:2 * D].partition_broadcast(P)).then_inc(s("mem_in"), 16)
            for b in range(WO0 + 2, XO0 + 2):
                load(b)
            sp.wait_ge(s("x_oe"), NT)
            sp.dma_start(ctxR, I["ctx_2"][0].rearrange("(t p) d -> p t d", p=P)).then_inc(s("ctx_in"), 16)
            sp.wait_ge(s("gw_zero"), 2)
            for gi in range(2):
                for d in range(2):
                    a = 3072 + 8 * d + 4 * gi
                    sp.dma_start(GW[:, :, gi, 32 * d:32 * d + 4], cols_of(m_w, a, a + 4)).then_inc(s("gw_in"), 16)
                    sp.dma_start(gb[32 * d:32 * d + 4, gi:gi + 1], I["m_in_b_2"][0, a:a + 4].rearrange("(p c) -> p c", c=1)).then_inc(s("gw_in"), 16)
            load(XO0 + 2)
            load(XO0 + 3)
            with sp.Fori(0, N_UP) as g:
                for j in range(2):
                    sp.wait_ge(t_ready, g * 16 + (TT["down"] - 8 + 8 * j))
                    sp.dma_start(WRAW[j].rearrange("p (k n) -> p k n", k=KC), I["w_up"][0][:, bass.ds(g * BW + 256 * j, 256)]
                                 .rearrange("(k p) n -> p k n", p=P)).then_inc(w_in[j], 16)
                    sp.dma_start(upb[:, j, :], I["bup_h"][bass.ds(g * 2 + j, 1)]
                                 .rearrange("a p c -> p (a c)")).then_inc(w_in[j], 16)
                for j in range(2):
                    sp.wait_ge(f_ready, g * 8 + (FT["up"] + 4 + 4 * j))
                    sp.dma_start(WRAW[j].rearrange("p (k n) -> p k n", k=4), I["w_down"][0][bass.ds(g * BW, BW), BW * j:BW * j + BW]
                                 .rearrange("(k p) n -> p k n", p=P)).then_inc(w_in[j], 16)
            sp.wait_ge(s("ln_done"), 4 * NT)
            for h in range(2):
                sp.dma_start(x_d[:, 4 * D * h:4 * D * h + 4 * D], XRf[:, 4 * D * h:4 * D * h + 4 * D]).then_inc(s("x_out"), 16)
            for b in range(M0, M0 + 4):
                load(b)
            sp.wait_ge(s("m_cu"), 8)
            for b in range(M0 + 4, M0 + 8):
                load(b)
            sp.wait_ge(s("m_cu"), 40)
            sp.wait_ge(s("m_h"), 16)
            load(M0 + 8)
            for h in range(2):
                sp.dma_start(XRf[:, 4 * D * h:4 * D * h + 4 * D], x_d[:, 4 * D * h:4 * D * h + 4 * D]).then_inc(s("x_back"), 16)
            for b in range(MO0, MO0 + 4):
                load(b)
            w_u, w_d = I["ffn_up_w_2"][0], I["ffn_down_w_2"][0]

            for t in range(NT):
                sp.wait_ge(s("x_new"), t + 1)
                sp.dma_start(x_d[:, D * t:D * t + D], XR[:, t, :]).then_inc(s("x_out2"), 16)

            def load_up(g, c):
                buf = 1 - c % 2
                for half in range(2):
                    sp.dma_start(WRAW[buf].rearrange("p (k n) -> p k n", k=KC)[:, :, P * half:P * half + P],
                                 w_u[:, bass.ds(g * BW + (P * c + FF2 * half), P)].rearrange("(k p) n -> p k n", p=P)).then_inc(w_in[buf], 16)
                sp.dma_start(cw[:, c, :], I["conv_h"][bass.ds(g * 4 + c, 1)].rearrange("a p c -> p (a c)")).then_inc(w_in[buf], 16)

            with sp.Fori(0, N_G) as g:
                for c in range(4):
                    if c < 2:
                        sp.wait_ge(t_ready, g * 16 + (TT["down2"] - 8 + 8 * c))
                    else:
                        sp.wait_ge(f_ready, g * 16 + (FT["up2"] + 4 * c - 4))
                    load_up(g, c)
                for j in range(2):
                    sp.wait_ge(f_ready, g * 16 + (FT["up2"] + 12 + 4 * j))
                    sp.dma_start(WRAW[1 - j].rearrange("p (k n) -> p k n", k=4), w_d[bass.ds(g * BW, BW), BW * j:BW * j + BW]
                                 .rearrange("(k p) n -> p k n", p=P)).then_inc(w_in[1 - j], 16)
            for c in range(2):
                sp.wait_ge(t_ready, TT["down2"] + 16 * N_G - 8 + 8 * c)
                load_up(N_G, c)
            for j in range(2):
                sp.wait_ge(f_ready, FT["up2"] + 16 * N_G + 4 + 4 * j)
                sp.dma_start(WRAW[1 - j][:, 0:2 * BW].rearrange("p (k n) -> p k n", k=2), w_d[N_G * BW:FF2, BW * j:BW * j + BW]
                             .rearrange("(k p) n -> p k n", p=P)).then_inc(w_in[1 - j], 16)
            for h in range(2):
                sp.dma_start(XRf[:, 4 * D * h:4 * D * h + 4 * D], x_d[:, 4 * D * h:4 * D * h + 4 * D]).then_inc(s("x_back2"), 16)
            for t in range(NT):
                sp.wait_ge(s("x_new"), NT + t + 1)
                sp.dma_start(out[0, t * P:t * P + P, :], XR[:, t, :]).then_inc(s("out_done"), 16)
            sp.wait_ge(s("out_done"), 16 * NT)

        @block.tensor
        def _(pe):
            def bank(n):
                if n >= 4:
                    pe.wait_ge(f_free, n - 3)
                return PS[:, n % 4, :]

            def bank_t(n):
                if n >= 4:
                    pe.wait_ge(t_free, n - 3)
                return PS[:, 4 + n % 4, :]

            def transposes(name, src, ready, ready_at):
                for h in range(2):
                    pe.wait_ge(ready, ready_at(h))
                    for k in range(KC):
                        n = FT[name] + 8 * h + k
                        o = bank(n)
                        for j in range(4):
                            m = pe.transpose(o[:, j * P:j * P + P], src[:, 4 * h + j, k * P:k * P + P], ident[:, :])
                        m.then_inc(f_ready, 1)

            def gemm_f(name, n0, w, chunks, x=XT, halves=2, width=BW):
                n = n0
                for f in chunks:
                    for h in range(halves):
                        o = bank(n)
                        for k in range(KC):
                            m = pe.matmul(o[:, 0:width], lhsT=w[:, k, f * P:f * P + P], rhs=x[:, k, h * width:h * width + width],
                                          start=(k == 0), stop=(k == KC - 1))
                        m.then_inc(f_ready, 1)
                        n += 1

            def gemm_t(n0, w, x=XT, tiles=NT, a=0, z=BW, kc=KC):
                for t in range(tiles):
                    o = bank_t(n0 + t)
                    for k in range(kc):
                        m = pe.matmul(o[:, 0:z - a], lhsT=x[:, k, t * P:t * P + P], rhs=w[:, k, a:z],
                                      start=(k == 0), stop=(k == kc - 1))
                    m.then_inc(t_ready, 1)

            def product(o, terms, first=True, last=True):
                for i, ((a_hi, a_lo), (b_hi, b_lo)) in enumerate(terms):
                    pe.matmul(o, lhsT=a_hi, rhs=b_hi, start=(first and i == 0), stop=False)
                    pe.matmul(o, lhsT=a_hi, rhs=b_lo, start=False, stop=False)
                    m = pe.matmul(o, lhsT=a_lo, rhs=b_hi, start=False, stop=(last and i == len(terms) - 1))
                return m

            def pair(v_hi, v_lo, *at):
                return v_hi[at], v_lo[at]

            W_UP = [[w[i].rearrange("p (k n) -> p k n", k=KC) for w in (WHI, WLO)] for i in range(2)]
            W_DOWN = [[w[i].rearrange("p (k n) -> p k n", k=4) for w in (WHI, WLO)] for i in range(2)]
            every = slice(None)
            def split_weights(b):
                pe.wait_ge(s("w_lo"), split_count(b))
                return W_UP[b % 2]

            def product_t(n0, b0, x_hi, x_lo, ready=None):
                for j in range(4):
                    w = split_weights(b0 + j)
                    for t in range(NT):
                        if j == 0 and ready:
                            ready(t)
                        product(bank_t(n0 + 8 * j + t)[:, 0:HALF], [(pair(x_hi, x_lo, every, k, slice(t * P, t * P + P)),
                                                                     pair(*w, every, k, every)) for k in range(KC)]).then_inc(t_ready, 1)

            def weights(b):
                pe.wait_ge(w_in[b % 2], loaded(b))
                return WB[b % 2]

            pe.wait_ge(s("relb_in"), 32)
            for g in range(2):
                o = bank(FT["vb"] + g)
                pe.matmul(o[0:NH, 0:N_BIAS], lhsT=relb[0:NB + 1, g * NH:g * NH + NH], rhs=hot[0:NB + 1, g, :],
                          start=True, stop=True).then_inc(f_ready, 1)
            pe.wait_ge(s("ident_ok"), 1)
            transposes("xt0", XR, s("ln_done"), lambda h: 4 * h + 4)
            pe.wait_ge(f_free, FT["qa"])
            for b, name in enumerate(("qa", "qb", "iq")):
                gemm_f(name, FT[name], weights(b), range(4))
            gemm_f("ka", FT["ka"], weights(3), range(1))
            gemm_t(TT["misc"], weights(3), a=P, z=P + MISC)
            pe.wait_ge(s("wuk_in"), 16)
            o = bank(FT["ukT"])
            for c in range(4):
                m = pe.transpose(o[:, c * P:c * P + P], wuk[:, 2 * c:2 * c + 2, :].rearrange("p a b -> p (a b)"), ident[:, :])
            m.then_inc(f_ready, 1)
            pe.wait_ge(s("ck_ready"), 2)
            for i, src in ((0, cR), (2, ikn)):
                for h in range(2):
                    o = bank(FT["ckT"] + i + h)
                    for j in range(4):
                        m = pe.transpose(o[:, j * P:j * P + P], src[:, 4 * h + j, :], ident[:, :])
                    m.then_inc(f_ready, 1)
            pe.wait_ge(f_free, FT["memT"])
            pe.wait_ge(t_free, TT["wo"])
            pe.wait_ge(s("attn_in"), 16 * 7)
            for n in range(NT):
                lo = 0 if n == 0 else n - 1
                q = slice(n * P, n * P + P)
                keys = slice(lo * P, n * P + P)
                width = (n + 1 - lo) * P
                if n > 0:
                    pe.wait_ge(s("d_fe"), n)
                for c in range(4):
                    for r in range(2):
                        hp = slice(DH * r, DH * r + DH)
                        m = pe.matmul(PS[:, 2 * r + c // 2, (c % 2) * 256 + 256 - width:(c % 2) * 256 + 256], lhsT=Q[hp, c, q],
                                      rhs=kaT[hp, c // 2, keys], start=True, stop=True)
                        if c % 2 == 1:
                            m.then_inc(s("a_s"), 1)
                if n == 0:
                    pe.wait_ge(s("cx_ready"), 1)
                for j in range(ADA_N // ADA_W * n, ADA_N // ADA_W * (n + 1)):
                    pe.wait_ge(s(f"ada_in{j % 2}"), 16 * (j // 2 + 1))
                    at = 5 * BW + ADA_W * (j % (ADA_N // ADA_W))
                    for k in range(KC):
                        m = pe.matmul(PSf[0:2, at:at + ADA_W], lhsT=cx[:, k, :], rhs=adaw[:, j % 2, k, :], start=(k == 0), stop=(k == KC - 1))
                    m.then_inc(s("ada_mm"), 1)
                pe.wait_ge(s("a_r"), n + 1)
                for b in range(4):
                    pe.wait_ge(s("a_sb"), 4 * n + 4)
                    for j in range(4):
                        h, kt = (4 * b + j) // 2, (4 * b + j) % 2
                        if n == 0 and kt == 0:
                            continue
                        m = pe.transpose(PS[:, b, j * P:j * P + P], SB[:, h, kt * P:kt * P + P], ident[:, :])
                    m.then_inc(s("a_t"), 1)
                pe.wait_ge(s("a_te"), 4 * n + 4)
                for h in range(NH):
                    kts = (1,) if n == 0 else (0, 1)
                    for kt in kts:
                        m = pe.matmul(PS[DH * (h % 2):DH * (h % 2) + DH, 4, (h // 2) * P:(h // 2) * P + P],
                                      lhsT=misc[:, lo + kt - (n == 0), DH * (h // 4):DH * (h // 4) + DH],
                                      rhs=PT[:, 2 * h + kt, :], start=(kt == kts[0]), stop=(kt == 1))
                m.then_inc(s("a_o"), 1)
                L = (n + 1) * P
                pe.wait_ge(s("ada_e"), n + 1)
                if 1 <= n < NT - 1:
                    q1, L1 = slice((n + 1) * P, (n + 2) * P), (n + 2) * P
                    pe.wait_ge(s("a_oe"), n + 1)
                    for h in range(NH):
                        i = NH * (n - 1) + h
                        if h >= 4:
                            pe.wait_ge(s("ix_r"), i - 3)
                        hp = slice(DH * (h % 2), DH * (h % 2) + DH)
                        for a in range(0, L1, BW):
                            z = min(L1, a + BW)
                            m = pe.matmul(PS[:, 2 * (h % 4) + a // BW, 0:z - a], lhsT=iqT[hp, h // 2, q1], rhs=ikT[hp, a:z],
                                          start=True, stop=True)
                        m.then_inc(s("ix_d"), 1)
                    pe.wait_ge(s("ix_r"), NH * n)
                for h in range(NH):
                    hp = slice(DH * (h % 2), DH * (h % 2) + DH)
                    m = pe.matmul(PS[:, h % 2, (h // 2) * P:(h // 2) * P + P], lhsT=wukT[hp, h // 2, :], rhs=Q[hp, 4 + h // 2, q],
                                  start=True, stop=True)
                    if h >= NH - 2:
                        m.then_inc(s("d_q"), 1)
                pe.wait_ge(s("d_qe"), 2 * n + 2)
                pe.wait_ge(s("a_oe"), n + 1)
                for i in range(-1, NH + 2):
                    if i + 1 < NH:
                        if i >= 1:
                            pe.wait_ge(s("d_lb"), NH * n + i)
                        for a in range(0, L, BW):
                            z = min(L, a + BW)
                            m = pe.matmul(PS[:, 4 + 2 * ((i + 1) % 2) + a // BW, 0:z - a], lhsT=QL[:, i + 1, :], rhs=cT[:, a:z],
                                          start=True, stop=True)
                        m.then_inc(s("d_l"), 1)
                    if 1 <= i <= NH:
                        h = i - 1
                        pe.wait_ge(s("d_n"), NH * n + h + 1)
                        if h >= 2:
                            pe.wait_ge(s("d_oe"), NH * n + h - 1)
                        for kt in range(n + 1):
                            m = pe.transpose(PS[:, 2 * (h % 2) + kt // 4, (kt % 4) * P:(kt % 4) * P + P],
                                             LG[:, h % 2, kt * P:kt * P + P], ident[:, :])
                        m.then_inc(s("d_t"), 1)
                    if i >= 2:
                        h = i - 2
                        pe.wait_ge(s("d_te"), NH * n + h + 1)
                        for kt in range(n + 1):
                            m = pe.matmul(PS[:, 2 * (h % 2), 0:P], lhsT=cR[:, kt, :], rhs=PT[:, 8 * (h % 2) + kt, :],
                                          start=(kt == 0), stop=(kt == n))
                        m.then_inc(s("d_o"), 1)
                pe.wait_ge(s("d_oe"), NH * n + NH)
                for h in range(NH):
                    m = pe.matmul(PS[DH * (h % 2):DH * (h % 2) + DH, 0, (h // 2) * P:(h // 2) * P + P],
                                  lhsT=wuv[:, h, :], rhs=OL[:, h, :], start=True, stop=True)
                m.then_inc(s("d_f"), 1)
            pe.wait_ge(s("d_fe"), NT)
            product_t(TT["wo"], WO0, Q_HI, Q_LO, lambda t: pe.wait_ge(s("q_lo"), t + 1))
            pe.wait_ge(s("mem_in"), 32)
            for k in range(0, KC, 2):
                o = bank(FT["memT"] + k // 2)
                for i in range(2):
                    for t in range(2):
                        m = pe.transpose(o[:, (2 * i + t) * P:(2 * i + t) * P + P], memR[:, t, (k + i) * P:(k + i) * P + P], ident[:, :])
                m.then_inc(f_ready, 1)
            pe.wait_ge(f_free, FT["xk"])
            for j in range(2):
                gemm_f("xk", FT["xk"] + 4 * j, weights(WO0 + 4 + j), range(4), x=memT, halves=1, width=MEM)
            for j in range(2):
                gemm_t(TT["xv"] + 2 * j, weights(WO0 + 6 + j), x=memT, tiles=2)
            transposes("xt1", XR, s("ln_done"), lambda h: NT + 4 * h + 4)
            pe.wait_ge(f_free, FT["xq"])
            for j in range(2):
                for j2 in (2 * j, 2 * j + 1):
                    w = split_weights(XQ0 + j2)
                    for f in range(2):
                        for h in range(2):
                            o = bank(FT["xq"] + 4 * j2 + 2 * f + h)
                            product(o, [(pair(*w, every, k, slice(f * P, f * P + P)),
                                         (X_HI[:, k, h * BW:h * BW + BW], X_LO0[k][:, h * BW:h * BW + BW])) for k in range(KC)]
                                    ).then_inc(f_ready, 1)
            pe.wait_ge(f_free, FT["xq"] + 16)
            pe.wait_ge(t_free, TT["xo"])
            for i in range(NT + 1):
                if i < NT:
                    if i >= 2:
                        pe.wait_ge(s("x_p"), i - 1)
                    for h in range(XH):
                        for kk in range(2):
                            m = pe.matmul(PS[:, 2 * (i % 2) + h // 2, (h % 2) * MEM:(h % 2) * MEM + MEM],
                                          lhsT=Q[:, 2 * h + kk, i * P:i * P + P], rhs=xkT[:, 2 * h + kk, :],
                                          start=(kk == 0), stop=(kk == 1))
                    m.then_inc(s("x_s"), 1)
                if i >= 1:
                    t, b0 = i - 1, 4 + 2 * ((i - 1) % 2)
                    pe.wait_ge(s("x_n"), t + 1)
                    if t >= 2:
                        pe.wait_ge(s("x_oe"), t - 1)
                    for j in range(8):
                        m = pe.transpose(PS[:, b0 + j // 4, (j % 4) * P:(j % 4) * P + P], XP[:, t % 2, j * P:j * P + P], ident[:, :])
                    m.then_inc(s("x_t"), 1)
                    pe.wait_ge(s("x_te"), t + 1)
                    for h in range(XH):
                        for dd in range(2):
                            for mt in range(2):
                                m = pe.matmul(PS[:, b0 + h // 2, ((h % 2) * 2 + dd) * P:((h % 2) * 2 + dd) * P + P],
                                              lhsT=xv[:, mt, (2 * h + dd) * P:(2 * h + dd) * P + P],
                                              rhs=XPT[:, t % 2, (2 * h + mt) * P:(2 * h + mt) * P + P],
                                              start=(mt == 0), stop=(mt == 1))
                    m.then_inc(s("x_o"), 1)
            pe.wait_ge(s("x_oe"), NT)
            product_t(TT["xo"], XO0, Q_HI, Q_LO)
            transposes("xt2", XR, s("ln_done"), lambda h: 2 * NT + 4 * h + 4)
            pe.wait_ge(f_free, FT["up"])
            with pe.Fori(0, N_UP) as g:
                for j in range(2):
                    pe.wait_ge(s("w_lo"), g * 4 + (F1 + 1 + j))
                    for f in range(2):
                        for h in range(2):
                            n = FT["up"] + 4 * j + 2 * f + h
                            pe.wait_ge(f_free, g * 8 + (n - 3))
                            product(PS[:, n % 4, :], [(pair(*W_UP[j], every, k, slice(f * P, f * P + P)),
                                                       pair(X_HI, X_LO1, every, k, slice(h * BW, h * BW + BW))) for k in range(KC)]
                                    ).then_inc(f_ready, 1)
                for j in range(2):
                    pe.wait_ge(s("w_lo"), g * 4 + (F1 + 3 + j))
                    for t in range(NT):
                        if j == 0 and t % 4 == 0:
                            pe.wait_ge(s("hidden1"), g * 8 + (11 + t // 4))
                        n = TT["down"] + 8 * j + t
                        pe.wait_ge(t_free, g * 16 + (n - 3))
                        product(PS[:, 4 + n % 4, :], [(pair(H_HI, H_LO, every, k, slice(t * P, t * P + P)),
                                                       pair(*W_DOWN[j], every, k, every)) for k in range(4)]).then_inc(t_ready, 1)

            pe.wait_ge(s("ctx_rows"), 1)
            for k in range(0, KC, 2):
                o = bank(FT["ctxT"] + k // 2)
                for i in range(2):
                    for t in range(2):
                        m = pe.transpose(o[:, (2 * i + t) * P:(2 * i + t) * P + P], ctxR[:, t, (k + i) * P:(k + i) * P + P], ident[:, :])
                m.then_inc(f_ready, 1)
            pe.wait_ge(f_free, FT["cg"])
            pe.wait_ge(s("gw_in"), 128)

            def gates(name, x, halves, width):
                n = FT[name]
                for h in range(halves):
                    for gi in range(2):
                        o = bank(n)
                        for k in range(KC):
                            m = pe.matmul(o[0:GR, 0:width], lhsT=GW[:, k, gi, :], rhs=x[:, k, h * width:h * width + width],
                                          start=(k == 0), stop=(k == KC - 1))
                        m.then_inc(f_ready, 1)
                        n += 1

            def gate_columns(nc_, free, i):
                pe.wait_ge(f_free, free)
                pe.wait_ge(s("g_e"), i + 1)
                for c in range(nc_):
                    for j, row in enumerate((uu, enm, wsr)):
                        m = pe.transpose(PS[:, c // 4, ((c % 4) * 3 + j) * GR:((c % 4) * 3 + j) * GR + GR],
                                         row[0:GR, c * P:c * P + P], ident[0:GR, 0:GR])
                for dh in range(2 * MH):
                    m = pe.matmul(PS[:, 2, dh * NC:dh * NC + nc_], lhsT=SEL[0:GR, dh, :], rhs=mpc[0:GR, 0:nc_],
                                  start=True, stop=True)
                m.then_inc(s("g_t"), 1)
                pe.wait_ge(s("g_c"), i + 1)

            def scan(steps, i0, j0, V):
                outs = j0 is not None

                def begin(idx):
                    c, d = steps[idx]
                    i, j = i0 + idx, idx
                    if i >= 1:
                        pe.wait_ge(s("m_w"), i)
                    if outs and j >= 1:
                        pe.wait_ge(s("m_arg"), j)
                    for h in range(MH):
                        m = pe.matmul(PS[:, 0, h * P:h * P + P], lhsT=SEL[0:GR, d * MH + h, :], rhs=MM[0:GR, c * P:c * P + P],
                                      start=True, stop=True)
                    m.then_inc(s("m_b"), 1)
                    if outs:
                        if j >= 1:
                            pe.wait_ge(s("m_pt"), j)
                        for h in range(MH):
                            m = pe.matmul(PS[:, 1, h * P:h * P + P], lhsT=kT[:, h, c * P:c * P + P], rhs=qT[:, h, c * P:c * P + P],
                                          start=True, stop=True)
                        m.then_inc(s("m_st"), 1)

                begin(0)
                for idx, (c, d) in enumerate(steps):
                    i, j = i0 + idx, idx
                    if idx + 1 < len(steps):
                        begin(idx + 1)
                    if outs:
                        pe.wait_ge(s("m_qs"), j + 1)
                        pe.wait_ge(s("m_cu"), 2 * i - 2)
                        pe.wait_ge(s("m_pt"), j + 1)
                        if j >= 1:
                            pe.wait_ge(s("m_h"), j)
                        for h in range(MH):
                            pe.matmul(PS[:, 2 + h, 0:V1], lhsT=QS[:, j % 2, h * P:h * P + P], rhs=CC[:, d * MH + h, :],
                                      start=True, stop=False)
                            m = pe.matmul(PS[:, 2 + h, 0:V1], lhsT=PP[:, j % 2, h * P:h * P + P], rhs=V[:, c, h, :],
                                          start=False, stop=True)
                        m.then_inc(s("m_n"), 1)
                    pe.wait_ge(s("m_ks"), i + 1)
                    for pair in range(2):
                        if 2 * i + pair >= 1:
                            pe.wait_ge(s("m_cu"), 2 * i + pair)
                        for h in (2 * pair, 2 * pair + 1):
                            m = pe.matmul(PS[:, 6 + h % 2, 0:V1], lhsT=KS[:, i % 2, h * P:h * P + P], rhs=V[:, c, h, :],
                                          start=True, stop=True)
                        m.then_inc(s("m_d"), 1)

            gates("cg", hcT, 1, MEM)
            gemm_t(TT["ck"], weights(M0), x=hcT, tiles=2)
            for j in range(2):
                gemm_t(TT["cv"] + 2 * j, weights(M0 + 1 + j), x=hcT, tiles=2)
            pe.wait_ge(s("v_one"), 1)
            gate_columns(2, FT["xtm"], 0)
            pe.wait_ge(t_free, TT["mk"])
            scan(CTX_STEPS, 0, None, VX)
            pe.wait_ge(s("m_w"), 4)
            pe.wait_ge(s("m_cu"), 8)
            transposes("xtm", XR, s("xr_norm"), lambda h: 4 * h + 4)
            pe.wait_ge(f_free, FT["mg"])
            gates("mg", XT, 2, BW)
            gemm_f("mq", FT["mq"], weights(M0 + 3), range(4))
            gemm_t(TT["mk"], weights(M0 + 4))
            for h in range(MH):
                for half in range(2):
                    pe.wait_ge(t_free, TT["mk"] + 4 * half + 4)
                    o = bank(FT["kT"] + 2 * h + half)
                    for j in range(4):
                        m = pe.transpose(o[:, j * P:j * P + P], KK[:, 4 * half + j, h * P:h * P + P], ident[:, :])
                    m.then_inc(f_ready, 1)
            for j in range(2):
                gemm_t(TT["mv"] + 8 * j, weights(M0 + 5 + j))
            gate_columns(NC, FT["yT"], 1)
            pe.wait_ge(t_free, TT["mo"])
            pe.wait_ge(s("v_one"), 2)
            scan(X_STEPS, 4, 0, VV)
            pe.wait_ge(s("m_h"), 16)
            pe.wait_ge(s("m_cu"), 40)
            for j in range(2):
                gemm_t(TT["mo"] + 8 * j, weights(M0 + 7 + j))
            transposes("yT", Q, s("o_y"), lambda h: NT + 4 * h + 4)
            pe.wait_ge(f_free, FT["xtf"])
            product_t(TT["mout"], MO0, X_HI, X_LO3)
            transposes("xtf", XN, s("xn_norm"), lambda h: 4 * h + 4)
            pe.wait_ge(s("xf_lo"), 16)

            def up2(g, c, at):
                pe.wait_ge(s("w_lo"), g * 6 + at)
                for m_ in range(4):
                    n = FT["up2"] + 4 * c + m_
                    a, h = P * (m_ // 2), m_ % 2
                    pe.wait_ge(f_free, g * 16 + (n - 3))
                    product(PS[:, n % 4, :], [(pair(*W_UP[1 - c % 2], every, k, slice(a, a + P)),
                                               pair(X_HI, X_LO2, every, k, slice(h * BW, h * BW + BW))) for k in range(KC)]
                            ).then_inc(f_ready, 1)

            def down2(g, j, kc, at, hid):
                pe.wait_ge(s("w_lo"), g * 6 + at)

                def terms(t, ks):
                    return [(pair(H_HI, H_LO, every, k, slice(t * P, t * P + P)), pair(*W_DOWN[1 - j], every, k, every)) for k in ks]

                if j == 0:
                    pe.wait_ge(s("hidden"), g * 4 + (hid - 1))
                    for t in range(4):
                        n = TT["down2"] + t
                        pe.wait_ge(t_free, g * 16 + (n - 3))
                        product(PS[:, 4 + n % 4, :], terms(t, range(kc - 1)), last=False)
                    pe.wait_ge(s("hidden"), g * 4 + hid)
                    for t in range(4):
                        product(PS[:, 4 + (TT["down2"] + t) % 4, :], terms(t, [kc - 1]), first=False).then_inc(t_ready, 1)
                for t in range(4 if j == 0 else 0, NT):
                    n = TT["down2"] + 8 * j + t
                    pe.wait_ge(t_free, g * 16 + (n - 3))
                    product(PS[:, 4 + n % 4, :], terms(t, range(kc))).then_inc(t_ready, 1)

            W0 = F2
            with pe.Fori(0, N_G) as g:
                for c in range(4):
                    up2(g, c, W0 + c + 1)
                for j in range(2):
                    down2(g, j, 4, W0 + 5 + j, 6)
            for c in range(2):
                up2(N_G, c, W0 + c + 1)
            for j in range(2):
                down2(N_G, j, 2, W0 + 3 + j, 4)

        @block.scalar
        def _(act):
            own = [0]

            def mark(ins):
                ins.then_inc(own_act, 1)
                own[0] += 1

            def settled():
                act.wait_ge(own_act, own[0])

            def load_rows(*rows):
                for i, v in rows:
                    act.dma_start(ROW[:, i, :], v.partition_broadcast(P)).then_inc(rows_in, 16)

            act.dma_start(cols[:, :], I["cols_h"]).then_inc(cols_in, 16)
            load_rows((0, I["ln_emb_g"]), (1, I["ln_emb_b"]))
            act.dma_start(hot[0:NB + 1, :, :], I["hot_h"]).then_inc(s("relb_in"), 16)
            act.wait_ge(s("relb_one"), 1)
            act.dma_start(relb[0:NB, :], I["rel_bias"]).then_inc(s("relb_in"), 16)

            def split(buf, at, width=4 * BW):
                act.wait_ge(w_in[buf], at)
                act.activation(WHI[buf][:, 0:width], WRAW[buf][:, 0:width], ACT.Copy).then_inc(s("w_hi"), 1)

            def split_block(b):
                split(b % 2, loaded(b))

            def empty_high(name, sem_):
                for i in range(16):
                    n = FT[name] + i
                    act.wait_ge(f_ready, n + 1)
                    act.activation(X_HI[:, i % KC, BW * (i // KC):BW * (i // KC) + BW], PS[:, n % 4, :], ACT.Copy).then_inc(s(sem_), 1)

            def tile_root(i, t, c=0):
                act.wait_ge(s(f"st_v{c}"), NT * i + t + 1)
                act.activation(sdv[:, NT * c + t:NT * c + t + 1], ve[:, NT * c + t:NT * c + t + 1], ACT.Sqrt).then_inc(s(f"st_s{c}"), 1)

            def layer_norm(i):
                for t in range(NT + 1):
                    if t < NT:
                        tile_root(i, t)
                    if t >= 1:
                        act.wait_ge(s("ln_half"), NT * i + t)
                        act.activation(XR[:, t - 1, :], XR[:, t - 1, :], ACT.Copy, scale=rs[:, t - 1:t]).then_inc(s("ln_scaled"), 1)

            def root(r, n=NT):
                act.wait_ge(s("ln_stat"), r)
                act.activation(sdv[:, 0:n], ve[:, 0:n], ACT.Sqrt).then_inc(s("ln_sd"), 1)

            def empty(n, out_ap, bias=0.0, scale=1.0, width=BW, rows=P, func=ACT.Identity):
                act.wait_ge(f_ready, n + 1)
                act.activation(out_ap, PS[0:rows, n % 4, 0:width], func, bias=bias, scale=scale).then_inc(f_free, 1)

            def empty_xt(name, scale=None, bias=None):
                for h in range(2):
                    for k in range(KC):
                        o = XT[:, k, BW * h:BW * h + BW]
                        if scale is None:
                            empty(FT[name] + 8 * h + k, o)
                        else:
                            empty(FT[name] + 8 * h + k, o, bias=bias(k), scale=scale(k))

            for g in range(2):
                empty(FT["vb"] + g, vb[0:NH, g, :], width=N_BIAS, rows=NH)
            act.wait_ge(f_free, FT["vb"] + 2)
            for g in range(2):
                act.dma_start(bias_d[g * NH:g * NH + NH], vb[0:NH, g, :].unsqueeze(1).to_broadcast([NH, P, N_BIAS])
                              ).then_inc(s("vb_out"), 16)
            layer_norm(0)
            act.wait_ge(cols_in, 16)
            act.activation(cx[:, :, :].rearrange("p k c -> p (k c)"), cols[:, COLS["c"][0]:COLS["c"][1]],
                           ACT.Silu).then_inc(s("cx_ready"), 1)
            empty_xt("xt0")
            act.wait_ge(s("ln_done"), NT)
            attn_in = s("attn_in")
            act.dma_start(mrow[:, 0:P], I["b_in"][0, 640:768].partition_broadcast(P)).then_inc(s("misc_in"), 16)
            act.dma_start(mrow[:, P:2 * P], I["b_in"][0, 1280:1408].partition_broadcast(P)).then_inc(s("misc_in"), 16)
            act.dma_start(mrow[:, 2 * P:MISC], I["b_in"][0, 1920:1992].partition_broadcast(P)).then_inc(s("misc_in"), 16)
            act.dma_start(kvg, I["dsa_kv_norm_g"][0].partition_broadcast(P)).then_inc(s("misc_in"), 16)
            act.dma_start(ikg[:, 0, :], I["idx_k_ln_g"][0].partition_broadcast(P)).then_inc(s("misc_in"), 16)
            act.dma_start(ikg[:, 1, :], I["idx_k_ln_b"][0].partition_broadcast(P)).then_inc(s("misc_in"), 16)
            act.dma_start(wuk, I["dsa_w_uk"][0].rearrange("h c d -> c h d")).then_inc(s("wuk_in"), 16)
            act.dma_start(wuv, I["dsa_w_uv"][0].rearrange("h c d -> c h d")).then_inc(attn_in, 16)
            act.dma_start(sink, I["swa_sinks"][0].partition_broadcast(P)).then_inc(attn_in, 16)
            for name, dst in (("qa", Q[:, 0:4, :]), ("qb", Q[:, 4:8, :]), ("iq", iqT)):
                for f in range(4):
                    for h in range(2):
                        empty(FT[name] + 2 * f + h, dst[:, f, BW * h:BW * h + BW],
                              bias=cols[:, COLS[name][0] + f:COLS[name][0] + f + 1])
            for h in range(2):
                a, z = BW * h, BW * h + BW
                empty(FT["ka"] + h, kaS[:, h, :], bias=cols[:, COLS["ka"][0]:COLS["ka"][1]])
                act.wait_ge(f_free, FT["ka"] + h + 1)
                for kv in range(2):
                    for r in range(2):
                        mark(act.activation(kaT[DH * r:DH * r + DH, kv, a:z], kaS[DH * kv:DH * kv + DH, h, :], ACT.Copy))
            empty(FT["ukT"], wukT.rearrange("p a b -> p (a b)"))
            root(1, 16)
            for i, dst in ((0, cT), (2, ikT)):
                for h in range(2):
                    empty(FT["ckT"] + i + h, dst[:, BW * h:BW * h + BW])
            act.wait_ge(s("vb_out"), 32)
            bt = bias_d.tensor
            act.wait_ge(f_ready, FT["ka"] + 1)
            act.wait_ge(t_ready, TT["misc"] + 8)
            for g in range(2):
                for h4 in range(2):
                    act.dma_start(bias[:, g * NH + 4 * h4:g * NH + 4 * h4 + 4, :],
                                  bass.AP(bt, (g * NH + 4 * h4) * P * N_BIAS + P - 1,
                                          [[N_BIAS - 1, P], [P * N_BIAS, 4], [1, 2 * P]])).then_inc(attn_in, 16)
            act.dma_start(far, bass.AP(bt, NH * P * N_BIAS, [[0, P], [P * N_BIAS, NH]]), allow_slow_non_contiguous=True).then_inc(attn_in, 16)
            for n in range(NT):
                w0 = P if n == 0 else 0
                act.wait_ge(s("a_m"), n + 1)
                for h in range(NH):
                    mark(act.activation(SB[:, h, w0:], SB[:, h, w0:], ACT.Exp, bias=nm[:, h:h + 1],
                                        accum_out=den[:, h:h + 1]))
                act.activation(es, sd, ACT.Exp).then_inc(s("a_p"), 1)
                act.wait_ge(s("ada_mm"), ADA_N // ADA_W * (n + 1))
                if n >= 2:
                    act.wait_ge(s(f"mods_out{n % 2}"), 16 * (n // 2))
                act.activation(modr[0:2, n % 2, :], PSf[0:2, 5 * BW:5 * BW + ADA_N], ACT.Copy).then_inc(s("ada_e"), 1)
                for b in range(4):
                    act.wait_ge(s("a_t"), 4 * n + b + 1)
                    if n == 0:
                        v = PS[:, b, :].rearrange("p (a b c) -> p a b c", a=2, b=2)
                        act.activation(PT[:, 4 * b + 1:4 * b + 4:2, :], v[:, :, 1, :], ACT.Copy).then_inc(s("a_te"), 1)
                    else:
                        act.activation(PT[:, 4 * b:4 * b + 4, :].rearrange("p a b -> p (a b)"), PS[:, b, :],
                                       ACT.Copy).then_inc(s("a_te"), 1)
                L = (n + 1) * P
                if 1 <= n < NT - 1:
                    act.wait_ge(s("a_o"), n + 1)
                    L1 = (n + 2) * P
                    for h in range(NH):
                        i = NH * (n - 1) + h
                        act.wait_ge(s("ix_d"), i + 1)
                        if h >= 2:
                            act.wait_ge(s("ix_s"), i - 1)
                        act.activation(RL[:, h % 2, 0:L1], PSf[:, 1024 * (h % 4):1024 * (h % 4) + L1], ACT.Relu,
                                       scale=DH ** -0.5).then_inc(s("ix_r"), 1)
                for b in range(2):
                    act.wait_ge(s("d_q"), 2 * n + b + 1)
                    act.activation(QL[:, b:NH:2, :], PS[:, b, :].rearrange("p (a b) -> p a b", a=4), ACT.Copy,
                                   scale=DH ** -0.5).then_inc(s("d_qe"), 1)
                for i in range(NH + 3):
                    if i < NH:
                        act.wait_ge(s("d_m"), NH * n + i + 1)
                        act.activation(LG[:, i % 2, 0:L], LG[:, i % 2, 0:L], ACT.Exp, bias=nm[:, i:i + 1],
                                       accum_out=den[:, i:i + 1]).then_inc(s("d_e"), 1)
                    if 1 <= i <= NH:
                        h = i - 1
                        act.wait_ge(s("d_r"), NH * n + h + 1)
                        act.activation(LG[:, h % 2, 0:L], LG[:, h % 2, 0:L], ACT.Copy, scale=den[:, h:h + 1]).then_inc(s("d_n"), 1)
                    if 2 <= i <= NH + 1:
                        h = i - 2
                        act.wait_ge(s("d_t"), NH * n + h + 1)
                        if 1 <= n < NT - 1 and h < 2:
                            act.wait_ge(s("ix_s"), NH * n)
                        act.activation(PT[:, 8 * (h % 2):8 * (h % 2) + n + 1, :].rearrange("p a b -> p (a b)"),
                                       PSf[:, 1024 * (h % 2):1024 * (h % 2) + L], ACT.Copy).then_inc(s("d_te"), 1)
                    if i >= 3:
                        h = i - 3
                        act.wait_ge(s("d_o"), NH * n + h + 1)
                        act.activation(OL[:, h, :], PS[:, 2 * (h % 2), 0:P], ACT.Copy).then_inc(s("d_oe"), 1)
            split_block(WO0)
            act.wait_ge(s("d_fe"), NT)
            for t in range(NT):
                act.activation(Q_HI[:, :, t * P:t * P + P], Q[:, :, t * P:t * P + P], ACT.Copy).then_inc(s("q_hi"), 1)
                if t == 1:
                    split_block(WO0 + 1)
            for j in range(2):
                act.wait_ge(s(f"mods_out{j}"), 64)
            act.wait_ge(s("d_oe"), NH * NT)
            load_rows((0, I["ln1_g"][0]), (1, I["ln1_b"][0]), (2, I["b_o"][0]))
            split_block(WO0 + 2)
            split_block(WO0 + 3)
            layer_norm(1)
            for k in range(0, KC, 2):
                empty(FT["memT"] + k // 2, memT[:, k:k + 2, :].rearrange("p a b -> p (a b)"))
            for f in range(KC):
                empty(FT["xk"] + f, xkT[:, f, :], bias=cols[:, COLS["xk"][0] + f:COLS["xk"][0] + f + 1], width=MEM)
            split_block(XQ0)
            empty_high("xt1", "x1_hi")
            split_block(XQ0 + 1)
            load_rows((0, I["ln2_g"][0]), (1, I["ln2_b"][0]), (2, I["xa_bo"][0]))
            for f in range(KC):
                for h in range(2):
                    empty(FT["xq"] + 2 * f + h, Q[:, f, BW * h:BW * h + BW], bias=cols[:, COLS["xq"][0] + f:COLS["xq"][0] + f + 1])
                    if 2 * f + h in (5, 9, 13):
                        split_block(XQ0 + 2 + (2 * f + h - 5) // 4)
            for i in range(NT + 1):
                if i < NT:
                    act.wait_ge(s("x_m"), i + 1)
                    if i >= 2:
                        act.wait_ge(s("x_t"), i - 1)
                    for h in range(XH):
                        ins = act.activation(XP[:, i % 2, h * MEM:h * MEM + MEM],
                                             PSf[:, 1024 * (i % 2) + h * MEM:1024 * (i % 2) + h * MEM + MEM], ACT.Exp,
                                             bias=xn[:, i % 2, h:h + 1], scale=XD ** -0.5, accum_out=xd[:, i % 2, h:h + 1])
                    ins.then_inc(s("x_p"), 1)
                if i >= 1:
                    t = i - 1
                    act.wait_ge(s("x_t"), t + 1)
                    act.activation(XPT[:, t % 2, :], PSf[:, 2048 + 1024 * (t % 2):3072 + 1024 * (t % 2)], ACT.Copy).then_inc(s("x_te"), 1)
            split_block(XO0 + 1)
            root(2, 2)
            split_block(XO0 + 2)
            split_block(XO0 + 3)
            layer_norm(2)
            empty_high("xt2", "x_hi")
            load_rows((0, I["ln3_g"][0]), (1, I["ln3_b"][0]), (2, I["b_down"][0]))


            with act.Fori(0, N_UP) as g:
                def rectify(m):
                    act.wait_ge(s("hidden1"), g * 8 + (m + 1))
                    act.wait_ge(f_ready, g * 8 + (FT["up"] + m + 1))
                    act.activation(RU[:, m % 4, :], PS[:, (FT["up"] + m) % 4, :], ACT.Relu,
                                   bias=upb[:, m // 4, (m % 4) // 2:(m % 4) // 2 + 1]).then_inc(f_free, 1)

                split(0, g * 48 + loaded(UP0))
                for m in (0, 1):
                    rectify(m)
                split(1, g * 48 + loaded(UP0 + 1))
                for m in (2, 3, 4, 5):
                    rectify(m)
                split(0, g * 48 + loaded(UP0 + 2))
                for m in (6, 7):
                    rectify(m)
                split(1, g * 48 + loaded(UP0 + 3))
            layer_norm(3)
            rows2_in = s("rows2_in")

            def load_rows2(*rows):
                for dst, v in rows:
                    act.dma_start(dst, v.partition_broadcast(P)).then_inc(rows2_in, 16)

            act.wait_ge(s("mod_ready"), 1)
            for k in range(KC):
                act.wait_ge(f_ready, FT["ctxT"] + k // 2 + 1)
                n = FT["ctxT"] + k // 2
                ins = act.activation(hcT[:, k, :], PS[:, n % 4, MEM * (k % 2):MEM * (k % 2) + MEM], ACT.Identity,
                                     bias=modc[:, 4, k:k + 1], scale=modc[:, 5, k:k + 1])
                if k % 2 == 1:
                    ins.then_inc(f_free, 1)

            mb = I["m_in_b_2"][0]
            act.wait_ge(s("ln_done"), 4 * NT)
            load_rows2((krow, mb[512:1024]), (ROW[:, 2, :], mb[1024:2048]))
            def gates(name, i, halves, width):
                n = FT[name]
                act.wait_ge(s("gw_in"), 128)
                for h in range(halves):
                    for row in (li, lf):
                        empty(n, row[0:GR, h * width:h * width + width], bias=gb[0:GR, (n - FT[name]) % 2:(n - FT[name]) % 2 + 1],
                              width=width, rows=GR)
                        n += 1
                w = halves * width
                act.wait_ge(s("g_a"), i + 1)
                mark(act.activation(enm[0:GR, 0:w], bb[0:GR, 0:w], ACT.Exp))
                settled()
                act.activation(enm[0:GR, 0:w], enm[0:GR, 0:w], ACT.Ln, bias=1.0).then_inc(s("g_l"), 1)

            def gates_exp(i, w):
                act.wait_ge(s("g_b"), i + 1)
                mark(act.activation(enm[0:GR, 0:w], tmp[0:GR, 0:w], ACT.Exp, scale=-1.0))
                act.activation(wsr[0:GR, 0:w], lf[0:GR, 0:w], ACT.Exp).then_inc(s("g_e"), 1)

            def scan(steps, i0, outs):
                for idx, (c, d) in enumerate(steps):
                    i, j = i0 + idx, idx
                    act.wait_ge(s("m_b"), i + 1)
                    if i >= 2:
                        act.wait_ge(s("m_cu"), 2 * i - 2)
                    if outs and j >= 2:
                        act.wait_ge(s("m_qs"), j - 1)
                    for h in range(MH):
                        ins = act.activation(WI[:, i % 2, h * P:h * P + P], PS[:, 0, h * P:h * P + P], ACT.Exp,
                                             bias=MPB[:, d * MH + h, c:c + 1], scale=-1.0)
                    ins.then_inc(s("m_w"), 1)
                    if outs:
                        act.wait_ge(s("m_arg"), j + 1)
                        for h in range(MH):
                            ins = act.activation(DD[:, j % 2, h * P:h * P + P], DD[:, j % 2, h * P:h * P + P], ACT.Exp,
                                                 bias=COL[:, c, 0, 32 * d + h:32 * d + h + 1])
                        ins.then_inc(s("m_e"), 1)

            gates("cg", 0, 1, MEM)
            gates_exp(0, MEM)
            act.wait_ge(s("g_c"), 1)
            scan(CTX_STEPS, 0, False)
            act.wait_ge(s("m_d"), 8)
            load_rows2((ROW[:, 2, :], mb[1024:2048]))
            root(3)
            empty_xt("xtm", scale=lambda k: modc[:, 1, k:k + 1], bias=lambda k: modc[:, 0, k:k + 1])
            n = FT["mg"]
            gates("mg", 1, 2, BW)
            for f in range(MH):
                for h in range(2):
                    empty(FT["mq"] + 2 * f + h, qT[:, f, BW * h:BW * h + BW], bias=cols[:, COLS["mq"][0] + f:COLS["mq"][0] + f + 1])
            gates_exp(1, T)
            for h in range(MH):
                for half in range(2):
                    empty(FT["kT"] + 2 * h + half, kT[:, h, BW * half:BW * half + BW])
            act.wait_ge(s("g_c"), 2)
            scan(X_STEPS, 4, True)
            act.wait_ge(s("m_h"), 16)
            act.wait_ge(s("m_d"), 40)
            load_rows2((ROW[:, 0, :], mb[2048:3072]), (ROW[:, 2, :], I["m_norm_g_2"][0]))
            root(4, 32)
            for m in range(16):
                act.wait_ge(t_free, TT["mo"] + m + 1)
                act.activation(OG[:, m % 2, :], OG[:, m % 2, :], ACT.Sigmoid).then_inc(s("o_s"), 1)
            act.wait_ge(s("o_y"), 16)
            load_rows2((ROW[:, 0, :], mods_d[0, 2 * D:3 * D]), (ROW[:, 1, :], I["ada_b_2"][0, 2 * D:3 * D]),
                       (ROW[:, 2, :], I["post_mix_g_2"][0]))
            split_block(MO0)
            empty_high("yT", "y_hi")
            for b in range(MO0 + 1, MO0 + 4):
                split_block(b)
            for t in range(NT + 3):
                if t < NT:
                    tile_root(4, t)
                if t >= 3:
                    tile_root(0, t - 3, 1)
            act.wait_ge(s("x_new"), NT)
            load_rows2((ROW[:, 0, :], mods_d[0, 5 * D:6 * D]), (ROW[:, 1, :], I["ada_b_2"][0, 5 * D:6 * D]),
                       (ROW[:, 2, :], I["post_ffn_g_2"][0]))
            for i in range(16):
                n, k = FT["xtf"] + i, i % KC
                act.wait_ge(f_ready, n + 1)
                if i >= 4:
                    act.wait_ge(s("xf_lo"), i - 3)
                act.activation(XS[:, i % 4, :], PS[:, n % 4, :], ACT.Identity, bias=modc[:, 2, k:k + 1],
                               scale=modc[:, 3, k:k + 1]).then_inc(f_free, 1)

            def chunks2(g, n_chunks, later):
                split(1, g * 112 + loaded(G0))
                for c in range(n_chunks):
                    act.wait_ge(s("hidden"), g * 4 + (c + 1))
                    for m in range(4):
                        n = FT["up2"] + 4 * c + m
                        dst = (UU, GG)[m // 2]
                        act.wait_ge(f_ready, g * 16 + (n + 1))
                        act.activation(dst[:, c % 2, BW * (m % 2):BW * (m % 2) + BW], PS[:, n % 4, :], ACT.Copy).then_inc(f_free, 1)
                        if m == 1:
                            later[c](g)
                    act.wait_ge(s("conv"), g * 4 + (c + 1))
                    act.activation(TC[:, c % 2, :], TC[:, c % 2, :], ACT.Silu).then_inc(s("silu"), 1)
                later[n_chunks](g)

            with act.Fori(0, N_G) as g:
                chunks2(g, 4, [lambda g, i=i: split(1 - i % 2, g * 112 + loaded(G0 + i)) for i in range(1, 6)])
            E0 = G0 + 6 * N_G
            split_rest = {1: lambda g: split(0, loaded(E0 + 1)), 2: lambda g: split(1, loaded(E0 + 2), 2 * BW),
                          3: lambda g: split(0, loaded(E0 + 3), 2 * BW)}
            chunks2(N_G, 2, [split_rest[1], split_rest[2], split_rest[3]])
            for t in range(NT):
                tile_root(5, t)

        @block.vector
        def _(dve):
            own = [0]

            def mark(ins):
                ins.then_inc(own_dve, 1)
                own[0] += 1

            def settled():
                dve.wait_ge(own_dve, own[0])

            def stats(t0, rows, parts):
                w = rows.shape[1] // parts
                for j in range(parts):
                    mark(dve.bn_stats(st[:, 2 * t0 + j if parts == 2 else t0, :], rows[:, j * w:j * w + w]))
                settled()
                if parts == 2:
                    mark(dve.bn_aggr(mv[:, t0, :], stf[:, 12 * t0:12 * t0 + 12]))
                else:
                    mark(dve.bn_aggr(mv[:, t0, :], stf[:, 6 * t0:6 * t0 + 6]))

            def rstd(n, r):
                dve.wait_ge(s("ln_sd"), r)
                mark(dve.reciprocal(rs[:, 0:n], sdv[:, 0:n]))
                settled()

            def tile_stats(t, rows, eps, rms, c=0):
                u = NT * c + t
                for j in range(2):
                    mark(dve.bn_stats(st[:, 2 * u + j, :], rows[:, j * BW:j * BW + BW]))
                settled()
                mark(dve.bn_aggr(mv[:, u, :], stf[:, 12 * u:12 * u + 12]))
                settled()
                if rms:
                    mark(dve.tensor_tensor(ve[:, u:u + 1], mv[:, u, 0:1], mv[:, u, 0:1], ALU.mult))
                    settled()
                    dve.scalar_tensor_tensor(ve[:, u:u + 1], ve[:, u:u + 1], eps, mv[:, u, 1:2], ALU.add, ALU.add).then_inc(s(f"st_v{c}"), 1)
                else:
                    dve.tensor_scalar(ve[:, u:u + 1], mv[:, u, 1:2], eps, None, ALU.add).then_inc(s(f"st_v{c}"), 1)

            def tile_rstd(i, t, c=0):
                u = NT * c + t
                dve.wait_ge(s(f"st_s{c}"), NT * i + t + 1)
                mark(dve.reciprocal(rs[:, u:u + 1], sdv[:, u:u + 1]))
                settled()

            def layer_norm(i, finish):
                for t in range(NT + 1):
                    if t < NT:
                        finish(t)
                        tile_stats(t, XR[:, t, :], LN_EPS, False)
                    if t >= 1:
                        tile_rstd(i, t - 1)
                        dve.scalar_tensor_tensor(XR[:, t - 1, :], XR[:, t - 1, :], mv[:, t - 1, 0:1], ROW[:, 0, :],
                                                 ALU.subtract, ALU.mult).then_inc(s("ln_half"), 1)

            rows2_v = s("rows2_in")
            dve.wait_ge(rows_in, 32)
            layer_norm(0, lambda t: dve.wait_ge(s(f"x_in{t}"), 16))

            dve.wait_ge(s("misc_in"), 96)
            for t in range(NT):
                n = TT["misc"] + t
                dve.wait_ge(t_ready, n + 1)
                dve.tensor_tensor(misc[:, t, :], PS[:, 4 + n % 4, 0:MISC], mrow, ALU.add).then_inc(t_free, 1)
            for t in range(NT):
                dve.wait_ge(t_free, TT["misc"] + t + 1)
                stats(t, misc[:, t, P:2 * P], 1)
                stats(NT + t, misc[:, t, 2 * P:2 * P + DH], 1)
            settled()
            mark(dve.tensor_tensor(ve[:, 0:NT], mv[:, 0:NT, 0], mv[:, 0:NT, 0], ALU.mult))
            settled()
            mark(dve.scalar_tensor_tensor(ve[:, 0:NT], ve[:, 0:NT], LN_EPS, mv[:, 0:NT, 1], ALU.add, ALU.add))
            dve.tensor_scalar(ve[:, NT:2 * NT], mv[:, NT:2 * NT, 1], LN_EPS, None, ALU.add).then_inc(s("ln_stat"), 1)
            rstd(2 * NT, 1)
            for t in range(NT):
                mark(dve.tensor_scalar(cR[:, t, :], misc[:, t, P:2 * P], rs[:, t:t + 1], None, ALU.mult))
                mark(dve.tensor_scalar(ikn[:, t, 0:DH], misc[:, t, 2 * P:2 * P + DH], mv[:, NT + t, 0:1],
                                       rs[:, NT + t:NT + t + 1], ALU.subtract, ALU.mult))
            mark(dve.tensor_scalar(iwt, misc[:, :, 2 * P + DH:MISC], NH ** -0.5, None, ALU.mult))
            settled()
            mark(dve.tensor_tensor(ikn[:, :, 0:DH], ikn[:, :, 0:DH], over_mid(ikg[:, 0, :], NT), ALU.mult))
            dve.tensor_tensor(cR, cR, over_mid(kvg, NT), ALU.mult).then_inc(s("ck_ready"), 1)
            settled()
            mark(dve.tensor_tensor(ikn[:, :, 0:DH], ikn[:, :, 0:DH], over_mid(ikg[:, 1, :], NT), ALU.add))
            settled()
            dve.tensor_copy(ikn[:, :, DH:2 * DH], ikn[:, :, 0:DH]).then_inc(s("ck_ready"), 1)

            dve.wait_ge(s("attn_in"), 16 * 7)
            dve.wait_ge(s("ck_ready"), 2)
            R8 = TOPK // 8

            def pick(m, first, last):
                w = (m + 1) * P
                for i in range(first, last):
                    if i == 0:
                        dve.wait_ge(s("ix_c"), m - 1)
                    src = score if i == 0 else work
                    settled()
                    mark(dve.max(top, src[:, 0:w]))
                    settled()
                    mark(dve.match_replace(work[:, 0:w], top, src[:, 0:w], TAKEN))
                    if i == R8 - 1:
                        settled()
                        mark(dve.tensor_scalar(msk[:, m % 2, 0:w], work[:, 0:w], TAKEN / 2, NEG, ALU.is_ge, ALU.mult))
                        settled()

            BEFORE, WINDOW = 16, 26
            for n in range(NT):
                w0 = P if n == 0 else 0
                L = (n + 1) * P
                for e in range(4):
                    dve.wait_ge(s("a_s"), 4 * n + e + 1)
                    if n > 0 and e == 0:
                        dve.wait_ge(s("d_t"), NH * n)
                    r, h0 = e % 2, 4 * (e // 2) + e % 2
                    v = PS[:, 2 * r + e // 2, :].rearrange("p (a b) -> p a b", a=2)
                    dve.scalar_tensor_tensor(SB[:, h0:h0 + 3:2, w0:], v[:, :, w0:], DH ** -0.5,
                                             bias[:, h0:h0 + 3:2, w0:], ALU.mult, ALU.add).then_inc(s("a_sb"), 1)
                dve.wait_ge(s("a_sb"), 4 * n + 4)
                mark(dve.tensor_reduce(mx, SB[:, :, w0:], AX.X, ALU.max))
                settled()
                mark(dve.tensor_tensor(mx, mx, sink, ALU.max))
                settled()
                mark(dve.tensor_scalar(nm, mx, -1.0, None, ALU.mult))
                dve.tensor_tensor(sd, sink, mx, ALU.subtract).then_inc(s("a_m"), 1)
                if n >= 2:
                    pick(n, BEFORE, (BEFORE + WINDOW) // 2)
                dve.wait_ge(s("a_p"), n + 1)
                mark(dve.tensor_tensor(den, den, es, ALU.add))
                settled()
                mark(dve.reciprocal(den, den))
                settled()
                dve.tensor_tensor(SB[:, :, w0:], SB[:, :, w0:], over_last(den, 2 * P - w0), ALU.mult).then_inc(s("a_r"), 1)
                if n >= 2:
                    pick(n, (BEFORE + WINDOW) // 2, WINDOW if n < NT - 1 else R8)
                dve.wait_ge(s("a_o"), n + 1)
                dve.tensor_copy(Q[:, 0:4, n * P:n * P + P], PS[:, 4, :].rearrange("p (a b) -> p a b", a=4)).then_inc(s("a_oe"), 1)
                ahead = 1 <= n < NT - 1
                L1 = (n + 2) * P
                if ahead:
                    for h in range(NH):
                        i = NH * (n - 1) + h
                        dve.wait_ge(s("ix_r"), i + 1)
                        if h == 0:
                            dve.tensor_scalar(score[:, 0:L1], RL[:, 0, 0:L1], iwt[:, n + 1, 0:1], None, ALU.mult).then_inc(s("ix_s"), 1)
                        else:
                            if n >= 2:
                                pick(n, WINDOW + (R8 - WINDOW) * (h - 1) // (NH - 1), WINDOW + (R8 - WINDOW) * h // (NH - 1))
                            dve.wait_ge(s("ix_s"), i)
                            dve.scalar_tensor_tensor(score[:, 0:L1], RL[:, h % 2, 0:L1], iwt[:, n + 1, h:h + 1], score[:, 0:L1],
                                                     ALU.mult, ALU.add).then_inc(s("ix_s"), 1)

                near = slice((n - 1) * P if n else 0, L)
                far_w = (n - 1) * P
                for i in range(NH + 1):
                    if i >= 1:
                        h = i - 1
                        dve.wait_ge(s("d_e"), NH * n + h + 1)
                        dve.reciprocal(den[:, h:h + 1], den[:, h:h + 1]).then_inc(s("d_r"), 1)
                    if i < NH:
                        dve.wait_ge(s("d_l"), NH * n + i + 1)
                        if i >= 2:
                            dve.wait_ge(s("d_t"), NH * n + i - 1)
                        if i == 0:
                            dve.wait_ge(s("a_t"), 4 * n + 4)
                        pair = PSf[:, 1024 * (2 + i % 2):1024 * (2 + i % 2) + L]
                        lg = LG[:, i % 2, :]
                        if n >= 2:
                            mark(dve.scalar_tensor_tensor(lg[:, 0:far_w], pair[:, 0:far_w], far[:, i:i + 1],
                                                          msk[:, n % 2, 0:far_w], ALU.add, ALU.add))
                        dve.tensor_tensor(lg[:, near], pair[:, near], bias[:, NH + i, w0:], ALU.add).then_inc(s("d_lb"), 1)
                        dve.wait_ge(s("d_lb"), NH * n + i + 1)
                        if n >= 2:
                            mark(dve.tensor_tensor(lg[:, near], lg[:, near], msk[:, n % 2, near], ALU.add))
                            settled()
                        dve.tensor_reduce(nm[:, i:i + 1], lg[:, 0:L], AX.X, ALU.max, negate=True).then_inc(s("d_m"), 1)
                    if ahead and i < NH:
                        pick(n + 1, BEFORE * i // NH, BEFORE * (i + 1) // NH)
                dve.wait_ge(s("d_f"), n + 1)
                dve.tensor_copy(Q[:, 4:8, n * P:n * P + P], PS[:, 0, :].rearrange("p (a b) -> p a b", a=4)).then_inc(s("d_fe"), 1)

            def x_low(name, sem_, dst):
                for h in range(2):
                    v = slice(BW * h, BW * h + BW)
                    for k in range(KC):
                        n = FT[name] + KC * h + k
                        dve.wait_ge(s(sem_), KC * h + k + 1)
                        dve.tensor_tensor(dst[k][:, v], PS[:, n % 4, :], X_HI[:, k, v], ALU.subtract).then_inc(f_free, 1)

            def residual(i, name=None):
                dve.wait_ge(rows_in, 32 + 48 * (i + 1))
                for t in range(NT):
                    if name and t % 4 == 0:
                        dve.wait_ge(f_ready, FT[name] + 2 * t + 8)
                    dve.scalar_tensor_tensor(XR[:, t, :], XR[:, t, :], ALPHA, ROW[:, 2, :], ALU.mult,
                                             ALU.add).then_inc(s("resid"), 1)

            def add_tile(name, i, j, t):
                n = TT[name] + 8 * j + t
                dve.wait_ge(s("resid"), NT * i + t + 1)
                dve.wait_ge(t_ready, n + 1)
                v = XR[:, t, HALF * j:HALF * j + HALF]
                ins = dve.tensor_tensor(v, v, PS[:, 4 + n % 4, 0:HALF], ALU.add)
                ins.then_inc(t_free, 1)
                if j == 3:
                    dve.wait_ge(t_free, n + 1)

            residual(0)
            for j in range(3):
                for t in range(NT):
                    add_tile("wo", 0, j, t)
            layer_norm(1, lambda t: add_tile("wo", 0, 3, t))
            dve.wait_ge(s("mem_in"), 32)
            for j in range(2):
                for t in range(2):
                    n = TT["xv"] + 2 * j + t
                    dve.wait_ge(t_ready, n + 1)
                    dve.tensor_tensor(xv[:, t, BW * j:BW * j + BW], PS[:, 4 + n % 4, :], vrow[:, BW * j:BW * j + BW],
                                      ALU.add).then_inc(t_free, 1)
            x_low("xt1", "x1_hi", X_LO0)
            residual(1, "xt1")
            for i in range(NT + 2):
                if i < NT:
                    dve.wait_ge(s("x_s"), i + 1)
                    mark(dve.tensor_reduce(xm[:, i % 2, :], PSf[:, 1024 * (i % 2):1024 * (i % 2) + 1024]
                                           .rearrange("p (a b) -> p a b", a=XH), AX.X, ALU.max))
                    settled()
                    dve.tensor_scalar(xn[:, i % 2, :], xm[:, i % 2, :], -XD ** -0.5, None, ALU.mult).then_inc(s("x_m"), 1)
                if 1 <= i <= NT:
                    t = i - 1
                    dve.wait_ge(s("x_p"), t + 1)
                    mark(dve.reciprocal(xd[:, t % 2, :], xd[:, t % 2, :]))
                    settled()
                    v = XP[:, t % 2, :].rearrange("p (a b) -> p a b", a=XH)
                    dve.tensor_tensor(v, v, over_last(xd[:, t % 2, :], MEM), ALU.mult).then_inc(s("x_n"), 1)
                if i >= 2:
                    t = i - 2
                    dve.wait_ge(s("x_o"), t + 1)
                    v = PSf[:, 2048 + 1024 * (t % 2):3072 + 1024 * (t % 2)].rearrange("p (a b) -> p a b", a=8)
                    q = (slice(None), slice(None), slice(t * P, t * P + P))
                    mark(dve.tensor_copy(Q_HI[q], v))
                    settled()
                    dve.tensor_tensor(Q_LO[q], v, Q_HI[q], ALU.subtract).then_inc(s("x_oe"), 1)
            def mean_square(n, eps):
                settled()
                mark(dve.tensor_tensor(ve[:, 0:n], mv[:, 0:n, 0], mv[:, 0:n, 0], ALU.mult))
                settled()
                dve.scalar_tensor_tensor(ve[:, 0:n], ve[:, 0:n], eps, mv[:, 0:n, 1], ALU.add, ALU.add).then_inc(s("ln_stat"), 1)

            dve.wait_ge(s("modc_in"), 96)
            sh = COLS["sh1"][0]
            mark(dve.tensor_tensor(modc[:, 0:4, :], modc[:, 0:4, :], cols[:, sh:sh + 32].rearrange("p (a b) -> p a b", a=4), ALU.add))
            mark(dve.tensor_tensor(modc[:, 4:6, :], modc[:, 4:6, :], cols[:, sh:sh + 16].rearrange("p (a b) -> p a b", a=2), ALU.add))
            settled()
            for i, name in ((1, "pre_mix"), (3, "pre_ffn"), (5, "pre_mix")):
                ins = dve.scalar_tensor_tensor(modc[:, i, :], modc[:, i, :], 1.0, cols[:, COLS[name][0]:COLS[name][1]],
                                               ALU.add, ALU.mult)
                if i < 5:
                    mark(ins)
                else:
                    ins.then_inc(s("mod_ready"), 1)
            dve.wait_ge(s("ctx_in"), 16)
            for t in range(2):
                stats(t, ctxR[:, t, :], 2)
            mean_square(2, RMS_EPS)
            rstd(2, 2)
            for t in range(2):
                ins = dve.tensor_scalar(ctxR[:, t, :], ctxR[:, t, :], rs[:, t:t + 1], None, ALU.mult)
                if t == 0:
                    mark(ins)
                else:
                    ins.then_inc(s("ctx_rows"), 1)
            for j in range(3):
                for t in range(NT):
                    add_tile("xo", 1, j, t)
            layer_norm(2, lambda t: add_tile("xo", 1, 3, t))
            x_low("xt2", "x_hi", [X_LO1[:, k, :] for k in range(KC)])
            residual(2, "xt2")
            dve.wait_ge(s("resid"), 3 * NT)

            def split_hidden(g):
                for m in range(8):
                    dve.wait_ge(s("squared"), g * 8 + (m + 1))
                    at = (slice(None), m // 2, slice(BW * (m % 2), BW * (m % 2) + BW))
                    dve.tensor_copy(H_HI[at], RU[:, m % 4, :]).then_inc(s("h_hi"), 1)
                    dve.wait_ge(s("h_hi"), g * 8 + (m + 1))
                    dve.tensor_tensor(H_LO[at], RU[:, m % 4, :], H_HI[at], ALU.subtract).then_inc(s("hidden1"), 1)

            def add_down(g, m):
                dve.wait_ge(t_ready, g * 16 + (TT["down"] + m + 1))
                v = XR[:, m % 8, BW * (m // 8):BW * (m // 8) + BW]
                dve.tensor_tensor(v, v, PS[:, 4 + (TT["down"] + m) % 4, :], ALU.add).then_inc(t_free, 1)

            with dve.Fori(0, N_UP - 1) as g:
                split_hidden(g)
                for m in range(16):
                    add_down(g, m)
            G = N_UP - 1
            split_hidden(G)
            for m in range(8):
                add_down(G, m)

            def finish_down(t):
                add_down(G, 8 + t)
                dve.wait_ge(t_free, TT["down"] + 16 * G + 8 + t + 1)

            layer_norm(3, finish_down)

            mark(dve.memset(ones[0:GR, :], 1.0))
            mark(dve.memset(ms[0:GR, :], 0.0))
            mark(dve.memset(mpc[0:GR, :], 0.0))
            dve.wait_ge(s("ln_half"), 4 * NT)
            mark(dve.memset(MM[0:GR, :], 0.0))
            settled()

            def gates(i, w, steps, ready):
                dve.wait_ge(f_free, ready)
                n = w // P
                g = slice(0, GR)
                mark(dve.tensor_scalar(tmp[g, 0:w], lf[g, 0:w], 0.0, None, ALU.min))
                settled()
                dve.scalar_tensor_tensor(bb[g, 0:w], tmp[g, 0:w], 2.0, lf[g, 0:w], ALU.mult, ALU.subtract).then_inc(s("g_a"), 1)
                dve.wait_ge(s("g_l"), i + 1)
                mark(dve.tensor_tensor(lf[g, 0:w], tmp[g, 0:w], enm[g, 0:w], ALU.subtract))
                mark(dve.memset(bb[g, 0:w], 0.0))
                settled()

                def piece(v, c, d):
                    x = v[32 * d:32 * d + 4, c * P:c * P + P]
                    return x[:, ::-1] if d else x

                for c, d in steps:
                    mark(dve.tensor_tensor_scan(piece(bb, c, d), piece(ones, 0, d), piece(lf, c, d), 0.0, ALU.mult, ALU.add))
                settled()
                mark(dve.tensor_tensor(uu[g, 0:w], li[g, 0:w], bb[g, 0:w], ALU.subtract))
                settled()
                for d in range(2):
                    c = [c for c, d2 in steps if d2 == d][0]
                    mark(dve.tensor_copy(mpc[32 * d:32 * d + 4, c:c + 1], ms[32 * d:32 * d + 4, :]))
                settled()
                for k in range(0, len(steps), 2):
                    for c, d in steps[k:k + 2]:
                        mark(dve.tensor_tensor_scan(piece(MM, c, d), piece(uu, c, d), piece(uu, c, d),
                                                    mpc[32 * d:32 * d + 4, c:c + 1], ALU.max, ALU.max))
                    settled()
                    for e, (c, d) in enumerate(steps[k:k + 2]):
                        last = c * P + (0 if d else P - 1)
                        if k + 2 < len(steps):
                            c2 = steps[k + 2 + e][0]
                            to = mpc[32 * d:32 * d + 4, c2:c2 + 1]
                        else:
                            to = ms[32 * d:32 * d + 4, :]
                        r = slice(32 * d, 32 * d + 4)
                        mark(dve.tensor_tensor(to, bb[r, last:last + 1], MM[r, last:last + 1], ALU.add))
                    settled()
                mark(dve.tensor_tensor(tmp[g, 0:w], bb[g, 0:w], MM[g, 0:w], ALU.add))
                for d in range(2):
                    r = slice(32 * d, 32 * d + 4)
                    end = MM[r, 0:w].rearrange("p (a b) -> p a b", b=P)[:, :, (0 if d else P - 1)]
                    ins = dve.tensor_tensor(lf[r, 0:w].rearrange("p (a b) -> p a b", b=P), uu[r, 0:w].rearrange("p (a b) -> p a b", b=P),
                                            over_last(end, P), ALU.subtract)
                    if d == 0:
                        mark(ins)
                    else:
                        ins.then_inc(s("g_b"), 1)

            def gate_columns(n, i):
                dve.wait_ge(s("g_t"), i + 1)
                for c in range(0, n, 4):
                    m = min(4, n - c)
                    mark(dve.tensor_copy(COL[:, c:c + m, :, :].rearrange("p a b c -> p (a b c)"), PS[:, c // 4, 0:m * 3 * GR]))
                dve.tensor_copy(MPB[:, :, 0:n], PS[:, 2, 0:2 * MH * NC].rearrange("p (a b) -> p a b", b=NC)[:, :, 0:n]).then_inc(s("g_c"), 1)

            def scan(steps, i0, outs):
                def exponents(j):
                    dve.wait_ge(s("m_w"), i0 + j + 1)
                    if j >= 2:
                        dve.wait_ge(s("m_pt"), j - 1)
                    dve.scalar_tensor_tensor(DD[:, j % 2, :].rearrange("p (a b) -> p a b", a=MH),
                                             PS[:, 0, :].rearrange("p (a b) -> p a b", a=MH), -1.0,
                                             over_mid(MASK[:, steps[j][1], :], MH), ALU.mult, ALU.add).then_inc(s("m_arg"), 1)

                for idx, (c, d) in enumerate(steps):
                    i, j = i0 + idx, idx
                    if outs:
                        if j == 0:
                            exponents(0)
                        dve.wait_ge(s("m_e"), j + 1)
                        dve.wait_ge(s("m_st"), j + 1)
                        if j >= 2:
                            dve.wait_ge(s("m_n"), j - 1)
                        dve.tensor_tensor(PP[:, j % 2, :], PS[:, 1, :], DD[:, j % 2, :], ALU.mult).then_inc(s("m_pt"), 1)
                        if j + 1 < len(steps):
                            exponents(j + 1)
                        dve.wait_ge(s("m_n"), j + 1)
                        dn0, dn1 = dn[:, 0, :], dn[:, 1, :]
                        if j >= 1:
                            dve.wait_ge(s("m_h"), j)
                        mark(dve.tensor_copy(dn0, PS[:, 2:6, DV]))
                        settled()
                        mark(dve.scalar_tensor_tensor(dn1, dn0, -1.0, dn0, ALU.mult, ALU.max))
                        settled()
                        mark(dve.tensor_tensor(dn1, dn1, COL[:, c, 1, 32 * d:32 * d + 4], ALU.max))
                        settled()
                        mark(dve.reciprocal(dn0, dn1))
                        settled()
                        first = (d == 0) == (c < NC // 2)
                        for h in range(MH):
                            o = Q[:, c, DV * h:DV * h + DV]
                            if first:
                                ins = dve.tensor_scalar(o, PS[:, 2 + h, 0:DV], dn0[:, h:h + 1], None, ALU.mult)
                            else:
                                ins = dve.scalar_tensor_tensor(o, PS[:, 2 + h, 0:DV], dn0[:, h:h + 1], o, ALU.mult, ALU.add)
                            if h < MH - 1:
                                mark(ins)
                            else:
                                ins.then_inc(s("m_h"), 1)
                    dve.wait_ge(s("m_w"), i + 1)
                    if i == 0:
                        dve.wait_ge(s("c_zero"), 1)
                    else:
                        dve.wait_ge(s("m_cu"), 2 * i)
                    for pair in range(2):
                        dve.wait_ge(s("m_d"), 2 * i + pair + 1)
                        for h in (2 * pair, 2 * pair + 1):
                            cc = CC[:, d * MH + h, :]
                            last = h * P + (0 if d else P - 1)
                            ins = dve.scalar_tensor_tensor(cc, cc, WI[:, i % 2, last:last + 1], PS[:, 6 + h % 2, 0:V1],
                                                           ALU.mult, ALU.add)
                            if h % 2 == 0:
                                mark(ins)
                            else:
                                ins.then_inc(s("m_cu"), 1)

            gates(0, MEM, CTX_STEPS, FT["cg"] + 2)
            dve.wait_ge(s("rows2_in"), 32)
            mark(dve.tensor_scalar(krow, krow, DK ** -0.5, None, ALU.mult))
            settled()

            def keys(name, dst, tiles):
                for t in range(tiles):
                    n = TT[name] + t
                    dve.wait_ge(t_ready, n + 1)
                    dve.scalar_tensor_tensor(dst[:, t, :], PS[:, 4 + n % 4, :], DK ** -0.5, krow, ALU.mult, ALU.add).then_inc(t_free, 1)

            def values(name, dst, tiles):
                for j in range(2):
                    for t in range(tiles):
                        n = TT[name] + tiles * j + t
                        dve.wait_ge(t_ready, n + 1)
                        dve.tensor_tensor(dst[:, t, 2 * j:2 * j + 2, 0:DV], PS[:, 4 + n % 4, :].rearrange("p (a b) -> p a b", a=2),
                                          ROW[:, 2, BW * j:BW * j + BW].rearrange("p (a b) -> p a b", a=2), ALU.add).then_inc(t_free, 1)

            keys("ck", KX, 2)
            values("cv", VX, 2)
            gate_columns(2, 0)
            scan(CTX_STEPS, 0, False)
            dve.wait_ge(s("x_out"), 32)
            for t in range(NT):
                stats(t, XR[:, t, :], 2)
            mean_square(NT, RMS_EPS)
            rstd(NT, 3)
            for t in range(NT):
                dve.tensor_scalar(XR[:, t, :], XR[:, t, :], rs[:, t:t + 1], None, ALU.mult).then_inc(s("xr_norm"), 1)
            gates(1, T, X_STEPS, FT["mg"] + 4)
            keys("mk", KK, NT)
            dve.wait_ge(s("rows2_in"), 48)
            values("mv", VV, NT)
            gate_columns(NC, 1)
            scan(X_STEPS, 4, True)
            dve.wait_ge(s("m_h"), 16)
            for t in range(NT):
                for h in range(MH):
                    mark(dve.bn_stats(st[:, MH * t + h, :], Q[:, t, DV * h:DV * h + DV]))
            settled()
            for i in range(32):
                mark(dve.bn_aggr(mv[:, i, :], st[:, i, :]))
            mean_square(32, RMS_EPS)
            rstd(32, 4)
            for t in range(NT):
                for h in range(MH):
                    v = Q[:, t, DV * h:DV * h + DV]
                    mark(dve.tensor_scalar(v, v, rs[:, MH * t + h:MH * t + h + 1], None, ALU.mult))
            dve.wait_ge(rows2_v, 80)
            settled()
            for t in range(NT):
                mark(dve.tensor_tensor(Q[:, t, :], Q[:, t, :], ROW[:, 2, :], ALU.mult))
            for m in range(17):
                if m < 16:
                    n = TT["mo"] + m
                    dve.wait_ge(t_ready, n + 1)
                    if m >= 2:
                        dve.wait_ge(s("o_y"), m - 1)
                    dve.tensor_tensor(OG[:, m % 2, :], PS[:, 4 + n % 4, :], ROW[:, 0, BW * (m // 8):BW * (m // 8) + BW],
                                      ALU.add).then_inc(t_free, 1)
                if m >= 1:
                    j, t = (m - 1) // 8, (m - 1) % 8
                    dve.wait_ge(s("o_s"), m)
                    if m == 1:
                        settled()
                    v = Q[:, t, BW * j:BW * j + BW]
                    dve.tensor_tensor(v, v, OG[:, (m - 1) % 2, :], ALU.mult).then_inc(s("o_y"), 1)

            def gate_row(rows_at):
                dve.wait_ge(rows2_v, rows_at)
                mark(dve.tensor_tensor(ROW[:, 0, :], ROW[:, 0, :], ROW[:, 1, :], ALU.add))
                settled()
                mark(dve.tensor_tensor(ROW[:, 0, :], ROW[:, 0, :], ROW[:, 2, :], ALU.mult))
                settled()

            def branch_scale(i, t):
                tile_rstd(i, t)
                dve.scalar_tensor_tensor(Q[:, t, :], Q[:, t, :], rs[:, t:t + 1], ROW[:, 0, :], ALU.mult, ALU.mult).then_inc(s("b_norm"), 1)

            def copy_out(j, t):
                n = TT["mout"] + 8 * j + t
                dve.wait_ge(t_ready, n + 1)
                dve.tensor_copy(Q[:, t, HALF * j:HALF * j + HALF], PS[:, 4 + n % 4, 0:HALF]).then_inc(t_free, 1)
                if j == 3:
                    dve.wait_ge(t_free, n + 1)

            x_low("yT", "y_hi", [X_LO3[:, k, :] for k in range(KC)])
            for j in range(3):
                for t in range(NT):
                    copy_out(j, t)
            gate_row(128)
            for t in range(NT + 3):
                if t < NT:
                    copy_out(3, t)
                    tile_stats(t, Q[:, t, :], RMS_EPS, True)
                if 1 <= t <= NT:
                    branch_scale(4, t - 1)
                if 3 <= t < NT + 3:
                    dve.wait_ge(s("x_new"), t - 2)
                    tile_stats(t - 3, XR[:, t - 3, :], RMS_EPS, True, 1)
            for t in range(NT):
                tile_rstd(0, t, 1)
                dve.tensor_scalar(XN[:, t, :], XR[:, t, :], rs[:, NT + t:NT + t + 1], None, ALU.mult).then_inc(s("xn_norm"), 1)
            for i in range(16):
                dve.wait_ge(f_free, FT["xtf"] + i + 1)
                dve.tensor_copy(X_HI[:, i % KC, BW * (i // KC):BW * (i // KC) + BW], XS[:, i % 4, :]).then_inc(s("xf_hi"), 1)

            def rows_of(v):
                return v.rearrange("p (a b) -> p a b", b=GRID)

            def add_down2(g, m):
                n = TT["down2"] + m
                dve.wait_ge(t_ready, g * 16 + (n + 1))
                v = Q[:, m % 8, BW * (m // 8):BW * (m // 8) + BW]
                dve.tensor_tensor(v, v, PS[:, 4 + n % 4, :], ALU.add).then_inc(t_free, 1)

            def group2(g, n_chunks):
                for c in range(n_chunks):
                    dve.wait_ge(f_free, g * 16 + (FT["up2"] + 4 * c + 4))
                    k = cw[:, c, :]
                    src, dst = rows_of(GG[:, c % 2, :]), rows_of(TC[:, c % 2, :])
                    dve.tensor_scalar(dst, src, k[:, 1:2], k[:, 3:4], ALU.mult, ALU.add).then_inc(s("taps"), 1)
                    dve.wait_ge(s("taps"), g * 8 + (2 * c + 1))
                    dve.scalar_tensor_tensor(dst[:, :, 1:], src[:, :, :-1], k[:, 0:1], dst[:, :, 1:], ALU.mult, ALU.add).then_inc(s("taps"), 1)
                    dve.wait_ge(s("taps"), g * 8 + (2 * c + 2))
                    dve.scalar_tensor_tensor(dst[:, :, :-1], src[:, :, 1:], k[:, 2:3], dst[:, :, :-1], ALU.mult, ALU.add).then_inc(s("conv"), 1)
                    dve.wait_ge(s("gated"), g * 4 + (c + 1))
                    dve.tensor_copy(H_HI[:, c, :], TC[:, c % 2, :]).then_inc(s("h2_hi"), 1)
                    dve.wait_ge(s("h2_hi"), g * 4 + (c + 1))
                    dve.tensor_tensor(H_LO[:, c, :], TC[:, c % 2, :], H_HI[:, c, :], ALU.subtract).then_inc(s("hidden"), 1)

            dve.wait_ge(s("y_zero"), 1)
            with dve.Fori(0, N_G) as g:
                group2(g, 4)
                for m in range(16):
                    add_down2(g, m)
            group2(N_G, 2)
            for m in range(8):
                add_down2(N_G, m)
            gate_row(176)
            for t in range(NT + 1):
                if t < NT:
                    add_down2(N_G, 8 + t)
                    dve.wait_ge(t_free, TT["down2"] + 16 * N_G + 8 + t + 1)
                    tile_stats(t, Q[:, t, :], RMS_EPS, True)
                if t >= 1:
                    branch_scale(5, t - 1)

        @block.gpsimd
        def _(pool):
            pool.memset(relb[0:NB + 1, :], 1.0).then_inc(s("relb_one"), 1)
            pool.memset(ident[:, :], 0.0).then_inc(s("pool_c"), 1)
            pool.wait_ge(s("pool_c"), 1)
            pool.affine_select(out=ident[:, :], in_=ident[:, :], compare_op=ALU.not_equal, fill=1.0, base=0,
                               pattern=[[-1, P]], channel_multiplier=1).then_inc(s("ident_ok"), 1)

            def low(buf, at, width=4 * BW):
                pool.wait_ge(s("w_hi"), at)
                pool.tensor_tensor(WLO[buf][:, 0:width], WRAW[buf][:, 0:width], WHI[buf][:, 0:width], ALU.subtract).then_inc(s("w_lo"), 1)

            def low_block(b):
                low(b % 2, split_count(b))

            def offset(i):
                pool.wait_ge(rows_in, 32 + 48 * i)
                for t in range(NT):
                    pool.wait_ge(s("ln_scaled"), NT * i + t + 1)
                    pool.tensor_tensor(XR[:, t, :], XR[:, t, :], ROW[:, 1, :], ALU.add).then_inc(s("ln_done"), 1)
            offset(0)
            for n in range(2, NT):
                pool.wait_ge(s("ix_s"), NH * (n - 1))
                v = score[:, n * P:n * P + P]
                pool.affine_select(out=v, in_=v, compare_op=ALU.is_ge, fill=NEG, base=0,
                                   pattern=[[-1, P]], channel_multiplier=1).then_inc(s("ix_c"), 1)
            low_block(WO0)
            for t in range(NT):
                pool.wait_ge(s("q_hi"), t + 1)
                v = (slice(None), slice(None), slice(t * P, t * P + P))
                pool.tensor_tensor(Q_LO[v], Q[v], Q_HI[v], ALU.subtract).then_inc(s("q_lo"), 1)
                if t == 1:
                    low_block(WO0 + 1)
            low_block(WO0 + 2)
            low_block(WO0 + 3)
            offset(1)
            for b in range(XQ0, XO0 + 2):
                low_block(b)
            pool.wait_ge(s("x_oe"), NT)
            pool.memset(GW, 0.0).then_inc(s("gw_zero"), 1)
            pool.memset(gb[0:GR, :], 0.0).then_inc(s("gw_zero"), 1)
            low_block(XO0 + 2)
            low_block(XO0 + 3)
            offset(2)
            pool.wait_ge(s("x_oe"), NT)
            for i in range(4):
                pool.memset(RU[:, i, :], 0.0).then_inc(s("hidden1"), 1)

            with pool.Fori(0, N_UP) as g:
                def square(m):
                    pool.wait_ge(f_free, g * 8 + (FT["up"] + m + 1))
                    v = RU[:, m % 4, :]
                    pool.tensor_tensor(v, v, v, ALU.mult).then_inc(s("squared"), 1)

                low(0, g * 4 + (F1 + 1))
                for m in (0, 1):
                    square(m)
                low(1, g * 4 + (F1 + 2))
                for m in (2, 3, 4, 5):
                    square(m)
                low(0, g * 4 + (F1 + 3))
                for m in (6, 7):
                    square(m)
                low(1, g * 4 + (F1 + 4))
            offset(3)
            pool.wait_ge(s("ln_done"), 4 * NT)
            pool.memset(SEL[0:GR, :, :], 0.0).then_inc(s("pool_c"), 1)
            pool.memset(MASK, 0.0).then_inc(s("pool_c"), 1)
            pool.wait_ge(s("pool_c"), 3)
            pool.affine_select(out=SEL[0:GR, :, :], in_=SEL[0:GR, :, :], compare_op=ALU.not_equal, fill=1.0, base=0,
                               pattern=[[-32, 2], [-1, MH], [0, P]], channel_multiplier=1).then_inc(s("pool_c"), 1)
            pool.affine_select(out=MASK[:, 0, :], in_=MASK[:, 0, :], compare_op=ALU.is_ge, fill=NEG, base=0,
                               pattern=[[1, P]], channel_multiplier=-1).then_inc(s("pool_c"), 1)
            pool.affine_select(out=MASK[:, 1, :], in_=MASK[:, 1, :], compare_op=ALU.is_ge, fill=NEG, base=0,
                               pattern=[[-1, P]], channel_multiplier=1).then_inc(s("pool_c"), 1)
            pool.wait_ge(f_ready, FT["ctxT"] + 4)
            pool.memset(CC, 0.0).then_inc(s("c_zero"), 1)
            pool.memset(VX[:, :, :, DV:V1], 1.0).then_inc(s("v_one"), 1)

            def scan(steps, i0, outs, K):
                for idx, (c, d) in enumerate(steps):
                    i, j = i0 + idx, idx
                    if i >= 2:
                        pool.wait_ge(s("m_d"), 2 * i - 2)
                    pool.tensor_tensor(KS[:, i % 2, :].rearrange("p (a b) -> p a b", a=MH), K[:, c, :].rearrange("p (a b) -> p a b", a=MH),
                                       over_last(COL[:, c, 2, 32 * d:32 * d + 4], DK), ALU.mult).then_inc(s("m_ks"), 1)
                    if outs:
                        pool.wait_ge(s("m_w"), i + 1)
                        if j >= 2:
                            pool.wait_ge(s("m_n"), j - 1)
                        pool.tensor_tensor(QS[:, j % 2, :].rearrange("p (a b) -> p a b", a=MH), qT[:, :, c * P:c * P + P],
                                           WI[:, i % 2, :].rearrange("p (a b) -> p a b", a=MH), ALU.mult).then_inc(s("m_qs"), 1)

            pool.wait_ge(s("g_c"), 1)
            pool.wait_ge(t_free, TT["mk"])
            scan(CTX_STEPS, 0, False, KX)
            pool.wait_ge(s("m_d"), 8)
            pool.wait_ge(f_ready, FT["mg"] + 4)
            pool.memset(VV[:, :, :, DV:V1], 1.0).then_inc(s("v_one"), 1)
            pool.wait_ge(s("g_c"), 2)
            pool.wait_ge(t_free, TT["mo"])
            scan(X_STEPS, 4, True, KK)

            def add_branch(i):
                for t in range(NT):
                    pool.wait_ge(s("b_norm"), NT * i + t + 1)
                    pool.tensor_tensor(XR[:, t, :], XR[:, t, :], Q[:, t, :], ALU.add).then_inc(s("x_new"), 1)

            for b in range(MO0, MO0 + 4):
                low_block(b)
            pool.wait_ge(s("x_back"), 32)
            add_branch(0)
            for i in range(2):
                pool.memset(R[:, 14400 + i:14401 + i], 0.0).then_inc(s("hidden"), 1)
            pool.wait_ge(s("x_new"), NT)
            pool.memset(Q[:, :, :], 0.0).then_inc(s("y_zero"), 1)

            pool.wait_ge(s("x_out2"), 16 * NT)
            pool.wait_ge(s("xn_norm"), NT)
            for i in range(16):
                pool.wait_ge(s("xf_hi"), i + 1)
                v = (slice(None), i % KC, slice(BW * (i // KC), BW * (i // KC) + BW))
                pool.tensor_tensor(X_LO2[v], XS[:, i % 4, :], X_HI[v], ALU.subtract).then_inc(s("xf_lo"), 1)

            def gate2(g, c):
                pool.wait_ge(s("silu"), g * 4 + (c + 1))
                pool.tensor_tensor(TC[:, c % 2, :], TC[:, c % 2, :], UU[:, c % 2, :], ALU.mult).then_inc(s("gated"), 1)

            W0 = F2
            with pool.Fori(0, N_G) as g:
                low(1, g * 6 + (W0 + 1))
                low(0, g * 6 + (W0 + 2))
                for c in range(4):
                    gate2(g, c)
                    if c < 3:
                        low(1 - c % 2, g * 6 + (W0 + 3 + c))
                low(0, g * 6 + (W0 + 6))
            W0 += 6 * N_G
            low(1, W0 + 1)
            low(0, W0 + 2)
            gate2(N_G, 0)
            low(1, W0 + 3, 2 * BW)
            gate2(N_G, 1)
            low(0, W0 + 4, 2 * BW)
            pool.wait_ge(s("x_back2"), 32)
            add_branch(1)


def host_layout(inputs):
    a = {k: np.ascontiguousarray(v) for k, v in inputs.items() if np.asarray(v).size}

    def col(v):
        return v.reshape(-1, P).T

    b_in, ada_b = a["b_in"][0], a["ada_b_2"][0]
    parts = {"qa": col(b_in[0:512]), "qb": col(b_in[768:1280]), "iq": col(b_in[1408:1920]), "ka": col(b_in[512:640]),
             "xq": col(a["xa_bq"][0]), "xk": col(a["xa_bkv"][0, :D]), "mq": col(a["m_in_b_2"][0, :512]),
             "pre_mix": col(a["pre_mix_g_2"][0]), "pre_ffn": col(a["pre_ffn_g_2"][0]),
             "sh1": col(ada_b[0:D]), "sc1": col(ada_b[D:2 * D]), "sh2": col(ada_b[3 * D:4 * D]), "sc2": col(ada_b[4 * D:5 * D]),
             "c": np.stack([col(a["c_2"][0]), col(a["c_ctx_2"])], -1).reshape(P, 16)}
    a["cols_h"] = np.ascontiguousarray(np.concatenate([parts[k] for k in COLS], 1))
    dist = 2 * P - 1 - np.arange(N_BIAS)
    near = np.maximum(dist, 0)
    exact = NB // 2
    far = exact + (np.log(np.maximum(near, 1) / exact) / np.log(MAXD / exact) * (NB - exact) + 1e-6).astype(np.int64)
    bucket = np.where(near < exact, near, np.minimum(far, NB - 1))
    hot = np.zeros((NB + 1, 2, N_BIAS), np.float32)
    hot[bucket, :, np.arange(N_BIAS)] = 1.0
    hot[NB, 0] = np.where((dist < 0) | (dist >= P), NEG, 0.0)
    hot[NB, 1] = np.where(dist < 0, NEG, 0.0)
    a["hot_h"] = hot
    a["bup_h"] = np.ascontiguousarray(a["b_up"][0].reshape(16, 2, P).transpose(0, 2, 1))
    conv = np.concatenate([a["ffn_conv_w_2"][0], a["ffn_conv_b_2"]], 0)
    a["conv_h"] = np.ascontiguousarray(conv.reshape(4, -1, P).transpose(1, 2, 0))
    return a


def kernel(**inputs):
    import concourse.bacc as bacc
    from concourse.bass_utils import run_bass_kernel_spmd

    arrays = host_layout(inputs)
    nc = bacc.Bacc("TRN2", target_bir_lowering=False, num_devices=1)
    aps = {n: nc.dram_tensor(f"in_{n}_dram", v.shape, mybir.dt.from_np(v.dtype), kind="ExternalInput").ap()
           for n, v in arrays.items()}
    out = nc.dram_tensor("out_dram", (1, T, D), F32, kind="ExternalOutput").ap()
    build_program(nc, aps, out)
    r = run_bass_kernel_spmd(nc, [{f"in_{n}_dram": v for n, v in arrays.items()}], core_ids=[0])
    return r.results[0]["out_dram"]
```
